# Optimizing a Trainium2 kernel written in Bass

```python
import jax, jax.numpy as jnp
from jax import lax
import numpy as np

D_MODEL = 1024
BATCH = 1
SEQ = 1024
DEPTH = 2
DEC_BATCH = 8
DEC_SEQ = 8
PAST_LEN = 1024
PAGE_SIZE = 128

N_HEADS = 16
QK_NOPE = 64
QK_ROPE = 32
V_HEAD = 64
Q_LORA = 512
KV_LORA = 256
ROPE_THETA = 10000.0
ATTN_SCALE = (QK_NOPE + QK_ROPE) ** -0.5
Q_BLOCK = 128
POOL_WINDOWS = (2, 4, 8, 16)
N_GROUPS = 4
GROUP_W = D_MODEL // N_GROUPS
POOL_BUF = 16 - 1
D_FF = 2816
CONV_W = 3
CONV_BUF = CONV_W - 1
N_MIXERS = 2
N_MLA_LAYERS = (DEPTH + 1) // 2
N_POOL_LAYERS = DEPTH // 2
EPS = 1e-6

kernel_name = 'hybrid_mla_pool_convffn_step'

def rms_norm(x, g):
    xf = x.astype(jnp.float32)
    y = xf * lax.rsqrt(jnp.mean(xf * xf, axis=-1, keepdims=True) + EPS)
    return (y * g.astype(jnp.float32)).astype(x.dtype)

def modulate(x, g, shift, scale):
    return rms_norm(x, g) * (1 + scale[:, None, :]) + shift[:, None, :]

def adaln(c, w, b):
    m = jax.nn.silu(c) @ w + b
    return jnp.split(m, 6, axis=-1)

def rope(x, pos):
    half = QK_ROPE // 2
    inv = ROPE_THETA ** (-jnp.arange(half, dtype=jnp.float32) / half)
    ang = pos.astype(jnp.float32)[:, None] * inv[None, :]
    shape = (1, ang.shape[0]) + (1,) * (x.ndim - 3) + (half,)
    cos = jnp.cos(ang).reshape(shape)
    sin = jnp.sin(ang).reshape(shape)
    x1 = x[..., :half].astype(jnp.float32)
    x2 = x[..., half:].astype(jnp.float32)
    out = jnp.concatenate([x1 * cos - x2 * sin, x2 * cos + x1 * sin], axis=-1)
    return out.astype(x.dtype)

def mla_project(h, pos, w_dq, q_norm, w_uq, w_dkv, kv_norm, w_uk):
    B, T, _ = h.shape
    cq = rms_norm(h @ w_dq, q_norm)
    q = (cq @ w_uq).reshape(B, T, N_HEADS, QK_NOPE + QK_ROPE)
    q_rope = rope(q[..., QK_NOPE:], pos)
    q_lat = jnp.einsum('bthn,khn->bthk', q[..., :QK_NOPE], w_uk)
    kv = h @ w_dkv
    ckv = rms_norm(kv[..., :KV_LORA], kv_norm)
    kr = rope(kv[..., KV_LORA:], pos)
    return q_lat, q_rope, ckv, kr

def mla_prompt_attend(q_lat, q_rope, ckv, kr):
    B, T = q_lat.shape[0], q_lat.shape[1]
    key_pos = jnp.arange(T)

    def block(i):
        s0 = i * Q_BLOCK
        qb = lax.dynamic_slice_in_dim(q_lat, s0, Q_BLOCK, axis=1)
        qrb = lax.dynamic_slice_in_dim(q_rope, s0, Q_BLOCK, axis=1)
        s = (jnp.einsum('bqhk,bsk->bhqs', qb, ckv)
             + jnp.einsum('bqhr,bsr->bhqs', qrb, kr)).astype(jnp.float32) * ATTN_SCALE
        qpos = s0 + jnp.arange(Q_BLOCK)
        s = jnp.where(key_pos[None, :] <= qpos[:, None], s, -jnp.inf)
        p = jax.nn.softmax(s, axis=-1).astype(ckv.dtype)
        return jnp.einsum('bhqs,bsk->bqhk', p, ckv)

    o = lax.map(block, jnp.arange(T // Q_BLOCK))
    return o.transpose(1, 0, 2, 3, 4).reshape(B, T, N_HEADS, KV_LORA)

def mla_sample_attend(q_lat, q_rope, ckv_new, kr_new, ckv_past, kr_past):
    S = q_lat.shape[1]
    P = ckv_past.shape[1]
    s_past = (jnp.einsum('bqhk,bsk->bhqs', q_lat, ckv_past)
              + jnp.einsum('bqhr,bsr->bhqs', q_rope, kr_past)).astype(jnp.float32) * ATTN_SCALE
    s_new = (jnp.einsum('bqhk,bsk->bhqs', q_lat, ckv_new)
             + jnp.einsum('bqhr,bsr->bhqs', q_rope, kr_new)).astype(jnp.float32) * ATTN_SCALE
    causal = jnp.tril(jnp.ones((S, S), dtype=bool))
    s_new = jnp.where(causal, s_new, -jnp.inf)
    p = jax.nn.softmax(jnp.concatenate([s_past, s_new], axis=-1), axis=-1).astype(ckv_new.dtype)
    return (jnp.einsum('bhqs,bsk->bqhk', p[..., :P], ckv_past)
            + jnp.einsum('bhqs,bsk->bqhk', p[..., P:], ckv_new))

def mla_out(o_lat, w_uv, w_o):
    B, T = o_lat.shape[0], o_lat.shape[1]
    o = jnp.einsum('bthk,khv->bthv', o_lat, w_uv).reshape(B, T, N_HEADS * V_HEAD)
    return o @ w_o

def pool_mix(h, prev, pos0, w_grp, ls):
    B, T, D = h.shape
    xp = jnp.concatenate([prev.astype(h.dtype), h], axis=1)
    xf = xp.astype(jnp.float32)
    cs = jnp.concatenate([jnp.zeros((B, 1, D), jnp.float32), jnp.cumsum(xf, axis=1)], axis=1)
    pos = pos0 + jnp.arange(T)
    outs = []
    for g, w in enumerate(POOL_WINDOWS):
        sl = slice(g * GROUP_W, (g + 1) * GROUP_W)
        win_sum = cs[:, POOL_BUF + 1:, sl] - cs[:, POOL_BUF + 1 - w:POOL_BUF + 1 - w + T, sl]
        cnt = jnp.minimum(pos + 1, w).astype(jnp.float32)[None, :, None]
        pooled = (win_sum / cnt - xf[:, POOL_BUF:, sl]).astype(h.dtype)
        outs.append(jnp.einsum('btc,cd->btd', pooled, w_grp[g]))
    return jnp.concatenate(outs, axis=-1) * ls, xp[:, -POOL_BUF:]

def conv_ffn(h, prev, w_up, conv_w, conv_b, w_down):
    T = h.shape[1]
    u = h @ w_up
    up = jnp.concatenate([prev.astype(u.dtype), u], axis=1)
    conv = conv_b + up[:, 0:T] * conv_w[0]
    for k in range(1, CONV_W):
        conv = conv + up[:, k:k + T] * conv_w[k]
    y = (jax.nn.silu(conv[..., :D_FF]) * conv[..., D_FF:]) @ w_down
    return y, up[:, -CONV_BUF:]

def setup_inputs(seed: int = 0) -> dict:
    key = jax.random.key(seed)
    ks = jax.random.split(key, 40)
    f32 = jnp.float32
    n_pages = PAST_LEN // PAGE_SIZE
    used_pages = DEC_BATCH * n_pages
    n_pool_pages = used_pages + used_pages // 4
    nrm = lambda k, shape, s: jax.random.normal(k, shape, f32) * s
    page_table = jax.random.permutation(ks[0], n_pool_pages)[:used_pages].reshape(DEC_BATCH, n_pages).astype(jnp.int32)
    return {
        'x_prompt': nrm(ks[1], (BATCH, SEQ, D_MODEL), 1.0),
        'x_sample': nrm(ks[2], (DEC_BATCH, DEC_SEQ, D_MODEL), 1.0),
        'cache_kv_latent': nrm(ks[3], (N_MLA_LAYERS, n_pool_pages, PAGE_SIZE, KV_LORA), 1.0),
        'cache_k_rope': nrm(ks[4], (N_MLA_LAYERS, n_pool_pages, PAGE_SIZE, QK_ROPE), 1.0),
        'state_pool': nrm(ks[5], (N_POOL_LAYERS, DEC_BATCH, POOL_BUF, D_MODEL), 1.0),
        'state_conv': nrm(ks[6], (DEPTH, DEC_BATCH, CONV_BUF, 2 * D_FF), 1.0),
        'page_table': page_table,
        'c_prompt': nrm(ks[7], (BATCH, D_MODEL), 1.0),
        'c_sample': nrm(ks[8], (DEC_BATCH, D_MODEL), 1.0),
        'ada_w': nrm(ks[9], (DEPTH, D_MODEL, 6 * D_MODEL), 0.5 * D_MODEL ** -0.5),
        'ada_b': nrm(ks[10], (DEPTH, 6 * D_MODEL), 0.02),
        'norm_mix_pre': 1.0 + nrm(ks[11], (DEPTH, D_MODEL), 0.1),
        'norm_mix_post': 1.0 + nrm(ks[12], (DEPTH, D_MODEL), 0.1),
        'norm_ffn_pre': 1.0 + nrm(ks[13], (DEPTH, D_MODEL), 0.1),
        'norm_ffn_post': 1.0 + nrm(ks[14], (DEPTH, D_MODEL), 0.1),
        'mla_w_dq': nrm(ks[15], (N_MLA_LAYERS, D_MODEL, Q_LORA), D_MODEL ** -0.5),
        'mla_q_norm': 1.0 + nrm(ks[16], (N_MLA_LAYERS, Q_LORA), 0.1),
        'mla_w_uq': nrm(ks[17], (N_MLA_LAYERS, Q_LORA, N_HEADS * (QK_NOPE + QK_ROPE)), Q_LORA ** -0.5),
        'mla_w_dkv': nrm(ks[18], (N_MLA_LAYERS, D_MODEL, KV_LORA + QK_ROPE), D_MODEL ** -0.5),
        'mla_kv_norm': 1.0 + nrm(ks[19], (N_MLA_LAYERS, KV_LORA), 0.1),
        'mla_w_uk': nrm(ks[20], (N_MLA_LAYERS, KV_LORA, N_HEADS, QK_NOPE), KV_LORA ** -0.5),
        'mla_w_uv': nrm(ks[21], (N_MLA_LAYERS, KV_LORA, N_HEADS, V_HEAD), KV_LORA ** -0.5),
        'mla_w_o': nrm(ks[22], (N_MLA_LAYERS, N_HEADS * V_HEAD, D_MODEL), (N_HEADS * V_HEAD) ** -0.5),
        'pool_w': nrm(ks[23], (N_POOL_LAYERS, N_GROUPS, GROUP_W, GROUP_W), GROUP_W ** -0.5),
        'pool_scale': 1.0 + nrm(ks[24], (N_POOL_LAYERS, D_MODEL), 0.1),
        'ffn_w_up': nrm(ks[25], (DEPTH, D_MODEL, 2 * D_FF), D_MODEL ** -0.5),
        'ffn_conv_w': nrm(ks[26], (DEPTH, CONV_W, 2 * D_FF), CONV_W ** -0.5),
        'ffn_conv_b': nrm(ks[27], (DEPTH, 2 * D_FF), 0.02),
        'ffn_w_down': nrm(ks[28], (DEPTH, D_FF, D_MODEL), D_FF ** -0.5),
    }

def reference(x_prompt, x_sample, cache_kv_latent, cache_k_rope, state_pool, state_conv, page_table,
              c_prompt, c_sample, ada_w, ada_b, norm_mix_pre, norm_mix_post, norm_ffn_pre, norm_ffn_post,
              mla_w_dq, mla_q_norm, mla_w_uq, mla_w_dkv, mla_kv_norm, mla_w_uk, mla_w_uv, mla_w_o,
              pool_w, pool_scale, ffn_w_up, ffn_conv_w, ffn_conv_b, ffn_w_down):
    B, T = x_prompt.shape[0], x_prompt.shape[1]
    Bd, S = x_sample.shape[0], x_sample.shape[1]
    n_pages = page_table.shape[1]
    past = n_pages * PAGE_SIZE
    pos_p = jnp.arange(T)
    pos_s = past + jnp.arange(S)
    pool_zero = jnp.zeros((B, POOL_BUF, D_MODEL), x_prompt.dtype)
    conv_zero = jnp.zeros((B, CONV_BUF, 2 * D_FF), x_prompt.dtype)

    xp, xs = x_prompt, x_sample
    kv_p, kr_p, kv_s, kr_s = [], [], [], []
    pool_p, pool_s, conv_p, conv_s = [], [], [], []
    for i in range(DEPTH):
        sh_mp, sc_mp, g_mp, sh_fp, sc_fp, g_fp = adaln(c_prompt, ada_w[i], ada_b[i])
        sh_ms, sc_ms, g_ms, sh_fs, sc_fs, g_fs = adaln(c_sample, ada_w[i], ada_b[i])
        hp = modulate(xp, norm_mix_pre[i], sh_mp, sc_mp)
        hs = modulate(xs, norm_mix_pre[i], sh_ms, sc_ms)
        j = i // N_MIXERS
        if i % N_MIXERS == 0:
            ql, qr, ckv, kr = mla_project(hp, pos_p, mla_w_dq[j], mla_q_norm[j], mla_w_uq[j],
                                          mla_w_dkv[j], mla_kv_norm[j], mla_w_uk[j])
            op = mla_out(mla_prompt_attend(ql, qr, ckv, kr), mla_w_uv[j], mla_w_o[j])
            qls, qrs, ckvs, krs = mla_project(hs, pos_s, mla_w_dq[j], mla_q_norm[j], mla_w_uq[j],
                                              mla_w_dkv[j], mla_kv_norm[j], mla_w_uk[j])
            ckv_past = cache_kv_latent[j, page_table].reshape(Bd, past, KV_LORA).astype(hs.dtype)
            kr_past = cache_k_rope[j, page_table].reshape(Bd, past, QK_ROPE).astype(hs.dtype)
            os_ = mla_out(mla_sample_attend(qls, qrs, ckvs, krs, ckv_past, kr_past), mla_w_uv[j], mla_w_o[j])
            kv_p.append(ckv); kr_p.append(kr); kv_s.append(ckvs); kr_s.append(krs)
        else:
            op, st_p = pool_mix(hp, pool_zero, 0, pool_w[j], pool_scale[j])
            os_, st_s = pool_mix(hs, state_pool[j], past, pool_w[j], pool_scale[j])
            pool_p.append(st_p); pool_s.append(st_s)
        xp = xp + g_mp[:, None, :] * rms_norm(op, norm_mix_post[i])
        xs = xs + g_ms[:, None, :] * rms_norm(os_, norm_mix_post[i])

        hp = modulate(xp, norm_ffn_pre[i], sh_fp, sc_fp)
        hs = modulate(xs, norm_ffn_pre[i], sh_fs, sc_fs)
        fp, cst_p = conv_ffn(hp, conv_zero, ffn_w_up[i], ffn_conv_w[i], ffn_conv_b[i], ffn_w_down[i])
        fs, cst_s = conv_ffn(hs, state_conv[i], ffn_w_up[i], ffn_conv_w[i], ffn_conv_b[i], ffn_w_down[i])
        xp = xp + g_fp[:, None, :] * rms_norm(fp, norm_ffn_post[i])
        xs = xs + g_fs[:, None, :] * rms_norm(fs, norm_ffn_post[i])
        conv_p.append(cst_p); conv_s.append(cst_s)

    new_kv_p = jnp.stack(kv_p)
    new_kr_p = jnp.stack(kr_p)
    new_kv_s = jnp.stack(kv_s)
    new_kr_s = jnp.stack(kr_s)
    new_pool_p = jnp.stack(pool_p)
    new_pool_s = jnp.stack(pool_s)
    new_conv_p = jnp.stack(conv_p)
    new_conv_s = jnp.stack(conv_s)
    return (xp, xs, new_kv_p, new_kr_p, new_kv_s, new_kr_s, new_pool_p, new_pool_s, new_conv_p, new_conv_s)


_drawn_inputs = setup_inputs


def setup_inputs(seed=0):
    import zlib

    import numpy as np

    out = dict(_drawn_inputs(seed))
    spreads = {}
    factors = {'ffn_conv_b': 5.737}
    for name, (base, spread) in spreads.items():
        noise = np.random.default_rng([zlib.crc32(name.encode()), seed]).standard_normal(out[name].shape)
        drawn = base * np.exp(spread * noise) if base else spread * noise
        out[name] = __import__('jax').numpy.asarray(drawn.astype(out[name].dtype))
    for name, factor in factors.items():
        out[name] = (out[name] * factor).astype(out[name].dtype)
    return out
```

```python
import numpy as np

import concourse.bass as bass
from concourse import mybir
from contextlib import ExitStack

F32 = mybir.dt.float32
F32R = mybir.dt.float32r
I32 = mybir.dt.int32
ALU = mybir.AluOpType
ACT = mybir.ActivationFunctionType
AX = mybir.AxisListType

P = 128
D_MODEL, SEQ, DEC_B, DEC_S = 1024, 1024, 8, 8
D_FF, CONV_W = 2816, 3
KT = D_MODEL // P
NS = DEC_B * DEC_S
NT = SEQ + NS
CHUNKS = [(0, 384), (384, 384), (768, NT - 768)]
NC = len(CHUNKS)
MAXC = 384
PAIRS = D_FF // P
N_SEQ = 1 + DEC_B
SIX = 6 * KT
SHIFT_MIX, SCALE_MIX, GATE_MIX, SHIFT_FFN, SCALE_FFN, GATE_FFN = range(0, SIX, KT)
EPS = 1e-6
ADA_GROUP = 4
ADA_SLOTS = 4


def col_tiles(c):
    n = CHUNKS[c][1]
    return [(o, min(P, n - o)) for o in range(0, n, P)]


class Norm:

    def __init__(self, k, name, src, tiles):
        self.src, self.tiles = src, tiles
        self.groups = [(g, min(4, tiles - g)) for g in range(0, tiles, 4)]
        self.inv_d = 1.0 / (tiles * P)
        s = lambda what: k.sem(f"{name}_{what}")
        self.squared = s("squared")
        self.reduced = s("reduced")
        self.summed = s("summed") if len(self.groups) > 1 else self.reduced
        self.stat = s("stat")
        self.var = s("var")
        self.std = s("std")
        self.rstd = s("rstd")
        self.spread = s("spread")

    def act_squares(self, k, act, c, ready=None):
        t0, n = CHUNKS[c]
        for i, (g, w) in enumerate(self.groups):
            done = c * len(self.groups) + i
            if ready:
                ready(act, c)
            if done:
                act.wait_ge(self.reduced, done)
            act.activation(k.sq[:, 0:w, 0:n], self.src[:, g:g + w, t0:t0 + n], ACT.Square)\
               .then_inc(self.squared, 1)

    def dve_sums(self, k, dve, c):
        n = CHUNKS[c][1]
        for i, (g, w) in enumerate(self.groups):
            done = c * len(self.groups) + i
            dve.wait_ge(self.squared, done + 1)
            if i == 0 and c:
                dve.wait_ge(self.stat, c)
            dst = k.ss if i == 0 else k.ss2
            last = dve.tensor_reduce(dst[:, 0:n], k.sq[:, 0:w, 0:n].rearrange("p k t -> p t k"),
                                     AX.X, ALU.add)
            last.then_inc(self.reduced, 1)
            if i:
                dve.wait_ge(self.reduced, done + 1)
                dve.tensor_tensor(k.ss[:, 0:n], k.ss[:, 0:n], k.ss2[:, 0:n], ALU.add)\
                   .then_inc(self.summed, 1)

    def pe_stats(self, k, pe, c, bank):
        pe.wait_ge(self.summed, c + 1)
        if c:
            pe.wait_ge(self.var, c)
        for j, (o, w) in enumerate(col_tiles(c)):
            last = pe.matmul(bank[0:w, j:j + 1], k.ss[:, o:o + w], k.ones[:, 0:1], start=True, stop=True)
        last.then_inc(self.stat, 1)

    def dve_var(self, k, dve, c, bank):
        dve.wait_ge(self.stat, c + 1)
        dve.tensor_scalar(k.small[:, 0, c, :], bank[:, 0:3], self.inv_d, EPS, ALU.mult, ALU.add)\
           .then_inc(self.var, 1)

    def act_sqrt(self, k, act, c):
        act.wait_ge(self.var, c + 1)
        act.activation(k.small[:, 1, c, :], k.small[:, 0, c, :], ACT.Sqrt).then_inc(self.std, 1)

    def dve_rstd(self, k, dve, c):
        dve.wait_ge(self.std, c + 1)
        dve.reciprocal(k.small[:, 2, c, :], k.small[:, 1, c, :]).then_inc(self.rstd, 1)

    def pe_spread(self, k, pe, c, bank):
        pe.wait_ge(self.rstd, c + 1)
        for j, (o, w) in enumerate(col_tiles(c)):
            last = pe.matmul(bank[:, o:o + w], k.small[0:w, 2, c, j:j + 1].to_broadcast([w, P]),
                             k.ident[0:w, 0:w], start=True, stop=True)
        last.then_inc(self.spread, 1)


class Kernel:

    def __init__(self, nc, ctx, io):
        self.nc, self.ctx, self.io, self.sems = nc, ctx, io, []
        self.x = self.sbuf(ctx, "x", [P, KT, NT])
        self.ada = self.sbuf(ctx, "ada", [P, 2, SIX, N_SEQ])
        self.ident = self.sbuf(ctx, "ident", [P, P])
        self.ones = self.sbuf(ctx, "ones", [P, 1])
        self.small = self.sbuf(ctx, "small", [P, 3, NC, 3])
        self.psum = ctx.enter_context(nc.psum_tensor("psum", [P, 8, 512], F32))
        self.banks = [self.psum[:, i, :] for i in range(8)]

    def sbuf(self, ctx, name, shape, dt=F32):
        return ctx.enter_context(self.nc.sbuf_tensor(name, shape, dt))

    def sem(self, name):
        self.sems.append(self.nc.alloc_semaphore(name=name))
        return self.sems[-1]

    def stage_done(self):
        self.nc.clear_and_free_semaphores(self.sems)
        self.nc.all_engine_barrier()
        self.sems = []


def adaln_stage(k):
    nc, io = k.nc, k.io
    turns = 2 * SIX // (ADA_GROUP * ADA_SLOTS)
    with ExitStack() as own:
        w = k.sbuf(own, "ada_w", [P, ADA_SLOTS, ADA_GROUP * D_MODEL])
        c = k.sbuf(own, "cond", [P, KT, N_SEQ])
        c_silu = k.sbuf(own, "cond_silu", [P, KT, N_SEQ])
        rows = k.sbuf(own, "ada_rows", [P, ADA_SLOTS, ADA_GROUP * P])
        bias = k.sbuf(own, "ada_bias", [P, 2, SIX])
        gains = k.sbuf(own, "gains", [P, 2, 4, KT])
        small_in, const_in, x_in = k.sem("ada_small_in"), k.sem("const_in"), k.sem("x_in")
        w_in = [k.sem(f"ada_w_in{s}") for s in range(ADA_SLOTS)]
        w_used = [k.sem(f"ada_w_used{s}") for s in range(ADA_SLOTS)]
        silu_done = k.sem("cond_silu_done")
        rows_done = [k.sem(f"ada_rows{s}") for s in range(ADA_SLOTS)]
        turned = [k.sem(f"ada_turned{s}") for s in range(ADA_SLOTS)]
        evac = [k.sem(f"ada_evac{s}") for s in range(ADA_SLOTS)]
        folded = k.sem("ada_folded")
        cleared = k.sem("ada_cleared")
        block = own.enter_context(nc.Block())

        @block.sync
        def _(sp):
            sp.dma_start(c[:], io["cond"]).then_inc(small_in, 16)
            def load(n, s, wait):
                if wait:
                    sp.wait_ge(w_used[s], n)
                sp.dma_start(w[:, s, :], io["ada_w"][bass.ds(n * ADA_SLOTS + s, 1)]
                             .rearrange("a p n -> p (a n)")).then_inc(w_in[s], 16)

            for s in range(ADA_SLOTS):
                load(0, s, False)
            sp.dma_start(k.x[:], io["x"]).then_inc(x_in, 16)
            with sp.Fori(1, turns) as n:
                for s in range(ADA_SLOTS):
                    load(n, s, True)
            sp.wait_ge(x_in, 16)

        @block.scalar
        def _(act):
            act.dma_start(bias[:], io["ada_b"]).then_inc(const_in, 16)
            act.dma_start(gains[:], io["gains"]).then_inc(const_in, 16)
            act.dma_start(k.ident[:], io["ident"]).then_inc(const_in, 16)
            act.wait_ge(small_in, 16)
            act.activation(c_silu[:], c[:], ACT.Silu).then_inc(silu_done, 1)

            def slot(n, s, wait):
                act.wait_ge(w_used[s], n + 1)
                if wait:
                    act.wait_ge(turned[s], n)
                act.activation(rows[0:N_SEQ, s, :], k.banks[s][0:N_SEQ, :], ACT.Copy).then_inc(rows_done[s], 1)

            act.wait_ge(cleared, 1)
            for s in range(ADA_SLOTS):
                slot(0, s, False)
            with act.Fori(1, turns) as n:
                for s in range(ADA_SLOTS):
                    slot(n, s, True)
            act.wait_ge(const_in, 48)

        @block.tensor
        def _(pe):
            pe.wait_ge(silu_done, 1)

            def slot(n, s, wait):
                pe.wait_ge(w_in[s], 16 * n + 16)
                if wait:
                    pe.wait_ge(rows_done[s], n)
                for kt in range(KT):
                    last = pe.matmul(k.banks[s][0:N_SEQ, :], c_silu[:, kt, :],
                                     w[:, s, kt * ADA_GROUP * P:(kt + 1) * ADA_GROUP * P],
                                     start=kt == 0, stop=kt == KT - 1)
                last.then_inc(w_used[s], 1)

            def turn(n, s, wait):
                pe.wait_ge(rows_done[s], n + 1)
                if wait:
                    pe.wait_ge(evac[s], n)
                for a in range(ADA_GROUP):
                    last = pe.transpose(k.banks[4 + s][:, a * P:(a + 1) * P], rows[:, s, a * P:(a + 1) * P],
                                        k.ident[:])
                last.then_inc(turned[s], 1)

            pe.wait_ge(const_in, 48)
            slot(0, 0, False)
            for s in range(1, ADA_SLOTS):
                slot(0, s, False)
                turn(0, s - 1, False)
            slot(1, 0, True)
            turn(0, ADA_SLOTS - 1, False)
            for s in range(1, ADA_SLOTS):
                slot(1, s, True)
                turn(1, s - 1, True)
            with pe.Fori(2, turns) as n:
                slot(n, 0, True)
                turn(n - 1, ADA_SLOTS - 1, True)
                for s in range(1, ADA_SLOTS):
                    slot(n, s, True)
                    turn(n, s - 1, True)
            turn(turns - 1, ADA_SLOTS - 1, True)

        @block.vector
        def _(dve):
            dve.memset(k.ones[:], 1.0)
            dve.memset(rows[:], 0.0).then_inc(cleared, 1)
            dve.wait_ge(const_in, 48)
            flat, flat_bias = k.ada[:].rearrange("p l m s -> p (l m) s"), bias[:].rearrange("p l m -> p (l m)")
            with dve.Fori(0, turns) as n:
                for s in range(ADA_SLOTS):
                    m = (n * ADA_SLOTS + s) * ADA_GROUP
                    dve.wait_ge(turned[s], n + 1)
                    dve.tensor_tensor(flat[:, bass.ds(m, ADA_GROUP), :],
                                      k.banks[4 + s].rearrange("p (m s) -> p m s", s=P)[:, :, 0:N_SEQ],
                                      flat_bias[:, bass.ds(m, ADA_GROUP)].unsqueeze(2)
                                      .to_broadcast([P, ADA_GROUP, N_SEQ]), ALU.add).then_inc(evac[s], 1)
            for s in range(ADA_SLOTS):
                dve.wait_ge(evac[s], turns)
            for l in range(2):
                for which, (first, one) in enumerate([(SCALE_MIX, 1.0), (GATE_MIX, 0.0),
                                                      (SCALE_FFN, 1.0), (GATE_FFN, 0.0)]):
                    part = k.ada[:, l, first:first + KT, :]
                    dve.scalar_tensor_tensor(part, part, one,
                                             gains[:, l, which, :].unsqueeze(2).to_broadcast([P, KT, N_SEQ]),
                                             ALU.add, ALU.mult).then_inc(folded, 1)
            dve.wait_ge(folded, 8)


def prompt_cols(c):
    t0, n = CHUNKS[c]
    return t0, min(n, SEQ - t0)


class Entry:

    def __init__(self, k, name, layer, scale, shift, scaled, scaled_s, split=True):
        self.split = split
        self.norm = Norm(k, name, k.x, KT)
        self.a = k.ada[:, layer, scale:scale + KT, :]
        self.s = k.ada[:, layer, shift:shift + KT, :]
        self.t, self.ts = scaled, scaled_s
        self.scaled = k.sem(f"{name}_scaled")
        self.scaled_s = k.sem(f"{name}_scaled_s")
        self.hi = k.sem(f"{name}_hi")
        self.lo = k.sem(f"{name}_lo")

    def dve(self, k, dve, c, bank, h_hi, h_lo):
        t0, n = prompt_cols(c)
        dve.wait_ge(self.norm.spread, c + 1)
        for kt in range(KT + 1):
            i = c * KT + kt
            if kt < KT:
                if i >= 2:
                    dve.wait_ge(self.hi, i - 1)
                    if self.split:
                        dve.wait_ge(self.lo, i - 1)
                dve.scalar_tensor_tensor(self.t[:, kt % 2, 0:n], k.x[:, kt, t0:t0 + n], self.a[:, kt, 0:1],
                                         bank[:, 0:n], ALU.mult, ALU.mult).then_inc(self.scaled, 1)
            if kt >= 1 and self.split:
                j = kt - 1
                dve.wait_ge(self.hi, i)
                dve.scalar_tensor_tensor(h_lo[:, j, t0:t0 + n], self.t[:, j % 2, 0:n], self.s[:, j, 0:1],
                                         h_hi[:, j, t0:t0 + n], ALU.add, ALU.subtract).then_inc(self.lo, 1)
        if c == NC - 1:
            o = SEQ - CHUNKS[c][0]
            seqs = lambda ap: ap.rearrange("p k (s t) -> p k s t", t=DEC_S)
            dve.tensor_tensor(self.ts[:], k.x[:, :, SEQ:NT],
                              bank[:, o:o + NS].unsqueeze(1).to_broadcast([P, KT, NS]), ALU.mult)\
               .then_inc(self.scaled_s, 1)
            dve.wait_ge(self.scaled_s, 1)
            dve.tensor_tensor(seqs(self.ts[:]), seqs(self.ts[:]),
                              self.a[:, :, 1:].unsqueeze(3).to_broadcast([P, KT, DEC_B, DEC_S]), ALU.mult)\
               .then_inc(self.scaled_s, 1)
            dve.wait_ge(self.scaled_s, 2)
            dve.tensor_tensor(seqs(self.ts[:]), seqs(self.ts[:]),
                              self.s[:, :, 1:].unsqueeze(3).to_broadcast([P, KT, DEC_B, DEC_S]), ALU.add)\
               .then_inc(self.scaled_s, 1)
            if self.split:
                dve.wait_ge(self.hi, NC * KT + 1)
                dve.tensor_tensor(h_lo[:, :, SEQ:NT], self.ts[:], h_hi[:, :, SEQ:NT], ALU.subtract)\
                   .then_inc(self.lo, 1)

    def act(self, k, act, c, put, put_s):
        t0, n = prompt_cols(c)
        for kt in range(KT):
            act.wait_ge(self.scaled, c * KT + kt + 1)
            act.activation(put(kt, t0, n), self.t[:, kt % 2, 0:n], ACT.Identity,
                           bias=self.s[:, kt, 0:1]).then_inc(self.hi, 1)
        if c == NC - 1:
            act.wait_ge(self.scaled_s, 3)
            act.activation(put_s, self.ts[:].rearrange("p k (s t) -> p k s t", t=DEC_S), ACT.Copy)\
               .then_inc(self.hi, 1)

    def ready(self, eng, c):
        eng.wait_ge(self.lo if self.split else self.hi, (c + 1) * KT + (c == NC - 1))


class Exit:

    def __init__(self, k, name, layer, gate, y):
        self.norm = Norm(k, name, y, KT)
        self.y = y
        self.b = k.ada[:, layer, gate:gate + KT, :]
        self.scaled = k.sem(f"{name}_scaled")
        self.scaled_s = k.sem(f"{name}_scaled_s")
        self.added = k.sem(f"{name}_added")

    def dve(self, k, dve, c, bank):
        t0, n = prompt_cols(c)
        dve.wait_ge(self.norm.spread, c + 1)
        for kt in range(KT):
            y = self.y[:, kt, t0:t0 + n]
            dve.scalar_tensor_tensor(y, y, self.b[:, kt, 0:1], bank[:, 0:n], ALU.mult, ALU.mult)\
               .then_inc(self.scaled, 1)
        if c == NC - 1:
            o = SEQ - CHUNKS[c][0]
            seqs = lambda ap: ap.rearrange("p k (s t) -> p k s t", t=DEC_S)
            y = self.y[:, :, SEQ:NT]
            dve.tensor_tensor(y, y, bank[:, o:o + NS].unsqueeze(1).to_broadcast([P, KT, NS]), ALU.mult)\
               .then_inc(self.scaled_s, 1)
            dve.wait_ge(self.scaled_s, 1)
            dve.tensor_tensor(seqs(y), seqs(y), self.b[:, :, 1:].unsqueeze(3).to_broadcast([P, KT, DEC_B, DEC_S]),
                              ALU.mult).then_inc(self.scaled_s, 1)

    def pool(self, k, pool, c):
        t0, n = prompt_cols(c)
        for kt in range(KT):
            pool.wait_ge(self.scaled, c * KT + kt + 1)
            x = k.x[:, kt, t0:t0 + n]
            pool.tensor_tensor(x, x, self.y[:, kt, t0:t0 + n], ALU.add).then_inc(self.added, 1)
        if c == NC - 1:
            pool.wait_ge(self.scaled_s, 2)
            x = k.x[:, :, SEQ:NT]
            pool.tensor_tensor(x, x, self.y[:, :, SEQ:NT], ALU.add).then_inc(self.added, 1)


def put_in(h):
    return (lambda kt, t0, n: h[:, kt, t0:t0 + n],
            h[:, :, SEQ:NT].rearrange("p k (s t) -> p k s t", t=DEC_S))


def run_norm_dve(k, dve, norm, stat_bank, apply):
    def stats(c):
        norm.dve_sums(k, dve, c)
        norm.dve_var(k, dve, c, stat_bank)
        norm.dve_rstd(k, dve, c)
    stats(0)
    for c in range(NC):
        if c + 1 < NC:
            stats(c + 1)
        apply(c)


def run_norm_act(k, act, norm, apply, ready=None):
    def stats(c):
        norm.act_squares(k, act, c, ready)
        norm.act_sqrt(k, act, c)
    stats(0)
    for c in range(NC):
        if c + 1 < NC:
            stats(c + 1)
        apply(c)


def run_norm_pe(k, pe, norm, stat_bank, spread_bank):
    for c in range(NC):
        norm.pe_stats(k, pe, c, stat_bank)
        norm.pe_spread(k, pe, c, spread_bank[c])


HEADS, NOPE, ROPE, V_DIM = 16, 64, 32, 64
Q_LORA, KV_LORA = 512, 256
QT, LT = Q_LORA // P, KV_LORA // P
HP = HEADS // 2
QB = SEQ // P
PAGE, PAGES = 128, 8
PAST = PAGE * PAGES
N_POOL = 80
SCALE = float((NOPE + ROPE) ** -0.5)
NEG = -1e30
PAIR_W = 2 * QT * P + 2 * LT * P
CACHE_W = KV_LORA + LT * PAGE + PAGE



def mla_project_stage(k, m):
    nc, io = k.nc, k.io
    UNITS = LT + 1 + QT
    with ExitStack() as own:
        h_hi = k.sbuf(own, "mla_h_hi", [P, KT, NT], F32R)
        h_lo = k.sbuf(own, "mla_h_lo", [P, KT, NT], F32R)
        ktab = k.sbuf(own, "ktab", [P, NT])
        raw = [k.sbuf(own, f"proj_raw{s}", [P, D_MODEL]) for s in range(2)]
        w_hi = [k.sbuf(own, f"proj_w_hi{s}", [P, D_MODEL], F32R) for s in range(2)]
        w_lo = [k.sbuf(own, f"proj_w_lo{s}", [P, D_MODEL], F32R) for s in range(2)]
        work = k.sbuf(own, "proj_work", [P, 2304])
        scaled = k.sbuf(own, "proj_scaled", [P, 2, MAXC])
        scaled_s = k.sbuf(own, "proj_scaled_s", [P, KT, NS])
        gain = k.sbuf(own, "latent_gain", [P, LT + QT])
        k.sq = work[:, 0:4 * MAXC].rearrange("p (k t) -> p k t", k=4)
        k.ss, k.ss2 = work[:, 1536:1536 + MAXC], work[:, 1920:1920 + MAXC]
        rot_tmp = work[:, 0:MAXC]
        cq = k.x[:, 0:QT, :]
        entry = Entry(k, "mla_in", 0, SCALE_MIX, SHIFT_MIX, scaled, scaled_s)
        kv_norm = Norm(k, "kv_norm", m.ckv, LT)
        q_norm = Norm(k, "q_norm", cq, QT)
        raw_in = [k.sem(f"proj_raw_in{s}") for s in range(2)]
        const_in = k.sem("proj_const_in")
        hi_ready, lo_ready = k.sem("proj_hi"), k.sem("proj_lo")
        done = k.sem("proj_done")
        evac_a, evac_d = k.sem("proj_evac_a"), k.sem("proj_evac_d")
        rot = k.sem("proj_rot")
        kv_scaled, q_scaled = k.sem("kv_scaled"), k.sem("q_scaled")
        cq_hi, cq_lo = k.sem("cq_hi_ready"), k.sem("cq_lo_ready")
        out = k.sem("latent_out")
        ROPE_UNIT = LT
        banks = [k.banks[0:3], k.banks[3:6]]
        stat, = k.banks[6:7]
        block = own.enter_context(nc.Block())

        @block.sync
        def _(sp):
            for j in range(UNITS):
                if j >= 2:
                    sp.wait_ge(lo_ready, j - 1)
                sp.dma_start(raw[j % 2][:], io["proj_w"][j]).then_inc(raw_in[j % 2], 16)
            sp.wait_ge(rot, 3 * NC + 1)
            sp.dma_start(io["kr_out"], m.kr[0:ROPE, :]).then_inc(out, 16)
            sp.wait_ge(kv_scaled, LT * NC)
            sp.dma_start(io["ckv_out"], m.ckv[:]).then_inc(out, 16)
            sp.wait_ge(out, 32)

        @block.scalar
        def _(act):
            act.dma_start(ktab[:], io["ktab"]).then_inc(const_in, 16)
            act.dma_start(gain[:], io["latent_gain"]).then_inc(const_in, 16)
            run_norm_act(k, act, entry.norm, lambda c: entry.act(k, act, c, *put_in(h_hi)))

            def split(j):
                act.wait_ge(raw_in[j % 2], 16 * (j // 2 + 1))
                if j >= 2:
                    act.wait_ge(done, NC * (j - 1))
                act.activation(w_hi[j % 2][:], raw[j % 2][:], ACT.Copy).then_inc(hi_ready, 1)
            split(0)
            entry.ready(act, NC - 1)
            n = 0
            for j in range(UNITS):
                if j + 1 < UNITS:
                    split(j + 1)
                if j == ROPE_UNIT:
                    continue
                dst = m.ckv[:, j] if j < LT else cq[:, j - LT - 1]
                for c, (t0, w) in enumerate(CHUNKS):
                    act.wait_ge(done, NC * j + c + 1)
                    act.activation(dst[:, t0:t0 + w], banks[j % 2][c][:, 0:w], ACT.Copy).then_inc(evac_a, 1)
            act.wait_ge(rot, 3 * NC)
            act.wait_ge(evac_a, NC * (UNITS - 1))
            run_norm_act(k, act, kv_norm, lambda c: None)
            act.wait_ge(kv_norm.reduced, NC)

            def cq_hi_chunk(c):
                t0, w = CHUNKS[c]
                act.wait_ge(q_scaled, QT * (c + 1))
                act.activation(m.cq_hi[:, :, t0:t0 + w], cq[:, :, t0:t0 + w], ACT.Copy).then_inc(cq_hi, 1)
            run_norm_act(k, act, q_norm, cq_hi_chunk)

        @block.vector
        def _(dve):
            run_norm_dve(k, dve, entry.norm, stat,
                         lambda c: entry.dve(k, dve, c, k.banks[3 + c], h_hi, h_lo))

            def split(j):
                dve.wait_ge(hi_ready, j + 1)
                dve.tensor_tensor(w_lo[j % 2][:], raw[j % 2][:], w_hi[j % 2][:], ALU.subtract).then_inc(lo_ready, 1)
            split(0)
            dve.wait_ge(const_in, 32)
            steps = 0
            for j in range(UNITS):
                if j + 1 < UNITS:
                    split(j + 1)
                if j != ROPE_UNIT:
                    continue
                for c, (t0, w) in enumerate(CHUNKS):
                    bank = banks[j % 2][c]
                    cols = slice(t0, t0 + w)
                    dve.wait_ge(done, NC * j + c + 1)
                    if c:
                        dve.wait_ge(rot, 3 * c)
                    dve.tensor_tensor(rot_tmp[64:P, 0:w], bank[0:64, 0:w], ktab[0:64, cols], ALU.mult)\
                       .then_inc(rot, 1)
                    dve.tensor_tensor(m.kr[64:P, cols], bank[64:P, 0:w], ktab[64:P, cols], ALU.mult)\
                       .then_inc(rot, 1)
                    dve.wait_ge(rot, 3 * c + 2)
                    dve.tensor_tensor(m.kr[64:P, cols], m.kr[64:P, cols], rot_tmp[64:P, 0:w], ALU.add)\
                       .then_inc(rot, 1)
            dve.wait_ge(rot, 3 * NC)
            dve.tensor_copy(m.kr[0:64, :], m.kr[64:P, :]).then_inc(rot, 1)

            def kv_chunk(c):
                t0, w = CHUNKS[c]
                dve.wait_ge(kv_norm.spread, c + 1)
                for t in range(LT):
                    part = m.ckv[:, t, t0:t0 + w]
                    dve.scalar_tensor_tensor(part, part, gain[:, t:t + 1], k.banks[c][:, 0:w], ALU.mult, ALU.mult)\
                       .then_inc(kv_scaled, 1)
            run_norm_dve(k, dve, kv_norm, stat, kv_chunk)

            def q_chunk(c):
                t0, w = CHUNKS[c]
                dve.wait_ge(q_norm.spread, c + 1)
                for t in range(QT):
                    part = cq[:, t, t0:t0 + w]
                    dve.scalar_tensor_tensor(part, part, gain[:, LT + t:LT + t + 1], k.banks[3 + c][:, 0:w],
                                             ALU.mult, ALU.mult).then_inc(q_scaled, 1)
                dve.wait_ge(cq_hi, c + 1)
                dve.tensor_tensor(m.cq_lo[:, :, t0:t0 + w], cq[:, :, t0:t0 + w], m.cq_hi[:, :, t0:t0 + w],
                                  ALU.subtract).then_inc(cq_lo, 1)
            run_norm_dve(k, dve, q_norm, stat, q_chunk)

        @block.tensor
        def _(pe):
            run_norm_pe(k, pe, entry.norm, stat, k.banks[3:6])
            for j in range(UNITS):
                pe.wait_ge(lo_ready, j + 1)
                for c, (t0, w) in enumerate(CHUNKS):
                    if j == 0:
                        entry.ready(pe, c)
                    if j >= 2:
                        if j - 2 == ROPE_UNIT:
                            pe.wait_ge(rot, 3 * c + 2)
                        else:
                            pe.wait_ge(evac_a, NC * (j - 2 - (j - 2 > ROPE_UNIT)) + c + 1)
                    for kt in range(KT):
                        o = slice(kt * P, kt * P + P)
                        bank = banks[j % 2][c][:, 0:w]
                        hh, hl = h_hi[:, kt, t0:t0 + w], h_lo[:, kt, t0:t0 + w]
                        pe.matmul(bank, w_hi[j % 2][:, o], hh, start=kt == 0, stop=False)
                        pe.matmul(bank, w_hi[j % 2][:, o], hl, start=False, stop=False)
                        last = pe.matmul(bank, w_lo[j % 2][:, o], hh, start=False, stop=kt == KT - 1)
                    last.then_inc(done, 1)
            pe.wait_ge(evac_a, NC * (UNITS - 1))
            pe.wait_ge(rot, 3 * NC)
            run_norm_pe(k, pe, kv_norm, stat, k.banks[0:3])
            pe.wait_ge(kv_norm.var, NC)
            run_norm_pe(k, pe, q_norm, stat, k.banks[3:6])


def mla_prompt_stage(k, m):
    nc, io = k.nc, k.io
    STEPS = 2 * QB
    with ExitStack() as own:
        raw = [k.sbuf(own, f"pair_raw{s}", [P, PAIR_W]) for s in range(2)]
        wq_hi = k.sbuf(own, "wq_hi", [P, 2 * QT * P], F32R)
        wq_lo = k.sbuf(own, "wq_lo", [P, 2 * QT * P], F32R)
        rot = k.sbuf(own, "rot", [P, 2, NT])
        mask = k.sbuf(own, "mask", [P, P])
        by_parity = lambda name, shape: [k.sbuf(own, f"{name}{s}", shape) for s in range(2)]
        q = by_parity("q", [P, 2, SEQ])
        keys = by_parity("keys", [P, 2, SEQ])
        vals = by_parity("vals", [P, QB, P])
        prob = by_parity("prob", [P, SEQ])
        prob_t = by_parity("prob_t", [P, SEQ])
        stats = k.sbuf(own, "softmax_stats", [P, 2, 3])
        scores = [k.psum[:, 0:2, :].rearrange("p b n -> p (b n)"), k.psum[:, 2:4, :].rearrange("p b n -> p (b n)")]
        turn_bank = k.psum[:, 4:6, :].rearrange("p b n -> p (b n)")
        o_bank, job_bank = k.banks[6], k.banks[7]
        const_in = k.sem("attn_const_in")
        raw_in = [k.sem(f"pair_raw_in{s}") for s in range(2)]
        wq_hi_ready, wq_lo_ready = k.sem("wq_hi_ready"), k.sem("wq_lo_ready")
        keys_init = k.sem("keys_init")
        job_done = k.sem("job_done")
        job_d, job_a = k.sem("job_d"), k.sem("job_a")
        samples_q = k.sem("samples_q")
        s_done, masked, max_done = k.sem("s_done"), k.sem("masked"), k.sem("max_done")
        exp_done, sum_inv, normed = k.sem("exp_done"), k.sem("sum_inv"), k.sem("normed")
        turned, turned_a, turned_d = k.sem("turned"), k.sem("turned_a"), k.sem("turned_d")
        o_done, o_out = k.sem("o_done"), k.sem("o_out")
        block = own.enter_context(nc.Block())

        Q_JOBS = [(hh, c) for hh in range(2) for c in range(NC)]
        JOBS = [("q", *x) for x in Q_JOBS] + [("k", 0), ("k", 1), ("v", 0), ("v", 1)]
        SLOT_OF_JOB = {2 + i: i for i in range(len(JOBS))}
        n_blocks = lambda n: n % QB + 1
        LATE = QB // 2

        @block.sync
        def _(sp):
            sp.dma_start(rot[:], io["rot"]).then_inc(const_in, 16)
            sp.dma_start(mask[:], io["mask"]).then_inc(const_in, 16)

            def load(i, s, wait):
                if wait:
                    sp.wait_ge(job_done, 10 * (i - 1))
                src = io["pair_w"][bass.ds(i, 1)].rearrange("a p n -> p (a n)")
                sp.dma_start(raw[s][:], src).then_inc(raw_in[s], 16)
            load(0, 0, False)
            load(1, 1, False)
            with sp.Fori(1, HP // 2) as j:
                load(2 * j, 0, True)
                load(2 * j + 1, 1, True)

        def job_counts(i, job):
            return (6 * i + min(job, 6), 4 * i + max(job - 6, 0))

        @block.scalar
        def _(act):
            act.wait_ge(const_in, 32)

            def split(i, s, n):
                act.wait_ge(raw_in[s], n)
                act.wait_ge(job_done, 10 * i)
                act.activation(wq_hi[:], raw[s][:, 0:2 * QT * P], ACT.Copy).then_inc(wq_hi_ready, 1)

            def job(i, j, s):
                if j < 6:
                    return
                kind, half = JOBS[j]
                act.wait_ge(job_done, 10 * i + j + 1)
                if kind == "k":
                    for hh in range(2):
                        r = slice(64 * hh, 64 * hh + 64)
                        last = act.activation(keys[s][r, hh, half * 512:(half + 1) * 512], job_bank[r, :], ACT.Copy)
                else:
                    last = act.activation(vals[s][:, half * 4:half * 4 + 4, :],
                                          job_bank.rearrange("p (j n) -> p j n", n=P), ACT.Copy)
                last.then_inc(job_a, 1)

            def exps(N, n, early=False):
                s, w = n % 2, n_blocks(n) * P
                act.wait_ge(max_done, N + 1)
                if not early:
                    act.wait_ge(turned, N - 1)
                    act.wait_ge(sum_inv, N - 1)
                act.activation(prob[s][:, 0:w], scores[s][:, 0:w], ACT.Exp, bias=stats[:, s, 0:1],
                               accum_out=stats[:, s, 1:2]).then_inc(exp_done, 1)

            def turned_part(N, n, early=False):
                s, w = n % 2, min(n_blocks(n), 4) * P
                act.wait_ge(turned, N + 1)
                if not early:
                    act.wait_ge(o_done, N - 1)
                act.activation(prob_t[s][:, 0:w], turn_bank[:, 0:w], ACT.Copy).then_inc(turned_a, 1)

            def pair(i, s, turn, first=False, last=False):
                for n in range(STEPS):
                    N = STEPS * i + n
                    if n == 0 and not last:
                        split(i + 1, 1 - s, turn)
                    if not (last and n == STEPS - 1):
                        exps(N + 1, (n + 1) % STEPS, first and n == 0)
                    if n in SLOT_OF_JOB and not last:
                        job(i + 1, SLOT_OF_JOB[n], 1 - s)
                    turned_part(N, n, first and n < 2)

            act.wait_ge(raw_in[0], 16)
            act.activation(wq_hi[:], raw[0][:, 0:2 * QT * P], ACT.Copy).then_inc(wq_hi_ready, 1)
            for j in range(len(JOBS)):
                job(0, j, 0)
            exps(0, 0, True)
            pair(0, 0, 16, first=True)
            with act.Fori(0, HP // 2 - 1) as j:
                pair(2 * j + 1, 1, 16 * j + 32)
                pair(2 * j + 2, 0, 16 * j + 32)
            pair(HP - 1, 1, None, last=True)

        @block.vector
        def _(dve):
            for s in range(2):
                dve.tensor_copy(keys[s][64:P, 0, :], m.kr[64:P, 0:SEQ])
                last = dve.tensor_copy(keys[s][0:64, 1, :], m.kr[0:64, 0:SEQ])
            last.then_inc(keys_init, 1)
            dve.wait_ge(const_in, 32)

            def split(i, s):
                dve.wait_ge(wq_hi_ready, i + 1)
                dve.tensor_tensor(wq_lo[:], raw[s][:, 0:2 * QT * P], wq_hi[:], ALU.subtract).then_inc(wq_lo_ready, 1)

            def job(i, j, s):
                if j >= 6:
                    return
                _, hh, c = JOBS[j]
                t0, w = prompt_cols(c)
                dve.wait_ge(job_done, 10 * i + j + 1)
                if c == NC - 1:
                    dve.tensor_tensor(m.qs[:, bass.ds(2 * i + hh, 1), :], job_bank[:, w:w + NS].unsqueeze(1),
                                      rot[:, hh, SEQ:NT].unsqueeze(1), ALU.mult).then_inc(samples_q, 1)
                dve.tensor_tensor(q[s][:, hh, t0:t0 + w], job_bank[:, 0:w], rot[:, hh, t0:t0 + w], ALU.mult)\
                   .then_inc(job_d, 1)

            def maxes(N, n, early=False):
                s, w = n % 2, n_blocks(n) * P
                diag = scores[s][:, w - P:w]
                dve.wait_ge(s_done, N + 1)
                dve.tensor_tensor(diag, diag, mask[:], ALU.add).then_inc(masked, 1)
                dve.wait_ge(masked, N + 1)
                if not early:
                    dve.wait_ge(exp_done, N - 1)
                dve.tensor_reduce(stats[:, s, 0:1], scores[s][:, 0:w], AX.X, ALU.max, negate=True)\
                   .then_inc(max_done, 1)

            def normalise(N, n, early=False):
                s, w = n % 2, n_blocks(n) * P
                if not early:
                    dve.wait_ge(normed, N - 1)
                dve.wait_ge(exp_done, N + 1)
                dve.reciprocal(stats[:, s, 2:3], stats[:, s, 1:2]).then_inc(sum_inv, 1)
                dve.wait_ge(sum_inv, N + 1)
                dve.tensor_scalar(prob[s][:, 0:w], prob[s][:, 0:w], stats[:, s, 2:3], None, ALU.mult)\
                   .then_inc(normed, 1)

            def turned_part(N, n, late, early=False):
                s, w = n % 2, n_blocks(n) * P
                if n_blocks(n) <= 4:
                    return
                dve.wait_ge(turned, N + 1)
                if not early:
                    dve.wait_ge(o_done, N - 1)
                dve.tensor_copy(prob_t[s][:, 512:w], turn_bank[:, 512:w]).then_inc(turned_d, 1)

            def attended(i, n):
                if n % 4 != 3:
                    return
                hh, half = n // QB, n % QB // 4
                r = slice(64 * hh, 64 * hh + 64)
                dve.wait_ge(o_done, STEPS * i + n + 1)
                dve.tensor_scalar(m.o[r, bass.ds(i, 1), half * 512:(half + 1) * 512],
                                  o_bank[r, :].unsqueeze(1), 1.0, None, ALU.mult).then_inc(o_out, 1)

            def pair(i, s, first=False, last=False):
                for n in range(STEPS):
                    N = STEPS * i + n
                    if n == 0 and not last:
                        split(i + 1, 1 - s)
                    if not (last and n == STEPS - 1):
                        maxes(N + 1, (n + 1) % STEPS, first and n == 0)
                    turned_part(N, n, None)
                    if not (last and n == STEPS - 1):
                        normalise(N + 1, (n + 1) % STEPS, first and n == 0)
                    if n in SLOT_OF_JOB and not last:
                        job(i + 1, SLOT_OF_JOB[n], 1 - s)
                    if n:
                        attended(i, n - 1)
                    elif not first:
                        attended(i - 1, STEPS - 1)

            split(0, 0)
            for j in range(len(JOBS)):
                job(0, j, 0)
            maxes(0, 0, True)
            normalise(0, 0, True)
            pair(0, 0, first=True)
            with dve.Fori(0, HP // 2 - 1) as j:
                pair(2 * j + 1, 1)
                pair(2 * j + 2, 0)
            pair(HP - 1, 1, last=True)
            attended(HP - 1, STEPS - 1)

        @block.tensor
        def _(pe):
            def job(i, j, s):
                d, a = job_counts(i, j)
                if j == 0:
                    pe.wait_ge(wq_lo_ready, i + 1)
                pe.wait_ge(job_a, a)
                pe.wait_ge(job_d, d)
                kind = JOBS[j][0]
                if kind == "q":
                    _, hh, c = JOBS[j]
                    t0, w = CHUNKS[c]
                    for t in range(QT):
                        o = slice((hh * QT + t) * P, (hh * QT + t + 1) * P)
                        ah, al = m.cq_hi[:, t, t0:t0 + w], m.cq_lo[:, t, t0:t0 + w]
                        pe.matmul(job_bank[:, 0:w], wq_hi[:, o], ah, start=t == 0, stop=False)
                        pe.matmul(job_bank[:, 0:w], wq_hi[:, o], al, start=False, stop=False)
                        last = pe.matmul(job_bank[:, 0:w], wq_lo[:, o], ah, start=False, stop=t == QT - 1)
                elif kind == "k":
                    half = JOBS[j][1]
                    for t in range(LT):
                        o = 2 * QT * P + t * P
                        last = pe.matmul(job_bank, raw[s][:, o:o + P], m.ckv[:, t, half * 512:(half + 1) * 512],
                                         start=t == 0, stop=t == LT - 1)
                else:
                    half = JOBS[j][1]
                    for b in range(4):
                        key = (half * 4 + b) * P
                        for t in range(LT):
                            o = (2 * QT + LT) * P + t * P
                            last = pe.matmul(job_bank[:, b * P:(b + 1) * P], m.ckv[:, t, key:key + P],
                                             raw[s][:, o:o + P], start=t == 0, stop=t == LT - 1)
                last.then_inc(job_done, 1)

            def score(N, i, n, s, early=False):
                hh, b = divmod(n, QB)
                out = scores[n % 2]
                if n == 0:
                    d, a = job_counts(i + 1, 0)
                    pe.wait_ge(job_a, a)
                    pe.wait_ge(job_d, d)
                if not early:
                    pe.wait_ge(exp_done, N - 1)
                w = n_blocks(n) * P
                for o in range(0, w, 512):
                    e = min(o + 512, w)
                    last = pe.matmul(out[:, o:e], q[s][:, hh, b * P:(b + 1) * P], keys[s][:, hh, o:e],
                                     start=True, stop=True)
                last.then_inc(s_done, 1)

            def turn(N, n, late):
                s = n % 2
                pe.wait_ge(normed, N + 1)
                if not (type(N) is int and N == 0):
                    pe.wait_ge(turned_a, N)
                if late is not None:
                    pe.wait_ge(turned_d, late)
                for b in range(n_blocks(n)):
                    last = pe.transpose(turn_bank[:, b * P:(b + 1) * P], prob[s][:, b * P:(b + 1) * P], k.ident[:])
                last.then_inc(turned, 1)

            def late_before(i, n):
                return 2 * LATE * i + sum(n_blocks(x) > 4 for x in range(n))

            def values(N, i, n, s):
                hh, b = divmod(n, QB)
                r = slice(64 * hh, 64 * hh + 64)
                pe.wait_ge(turned_a, N + 1)
                if n_blocks(n) > 4:
                    pe.wait_ge(turned_d, late_before(i, n) + 1)
                if n % 4 == 0 and not (type(i) is int and i == 0 and n == 0):
                    pe.wait_ge(o_out, 4 * i + n // 4)
                for kb in range(n_blocks(n)):
                    last = pe.matmul(o_bank[r, b % 4 * P:(b % 4 + 1) * P], vals[s][:, kb, r],
                                     prob_t[n % 2][:, kb * P:(kb + 1) * P], start=kb == 0, stop=kb == n_blocks(n) - 1)
                last.then_inc(o_done, 1)

            def pair(i, s, first=False, last=False):
                for n in range(STEPS):
                    N = STEPS * i + n
                    if n < STEPS - 1:
                        score(N + 1, i, n + 1, s, first and n == 0)
                    elif not last:
                        score(N + 1, i + 1, 0, 1 - s)
                    if n in SLOT_OF_JOB and not last:
                        job(i + 1, SLOT_OF_JOB[n], 1 - s)
                    late = late_before(i, n)
                    turn(N, n, None if type(late) is int and late == 0 else late)
                    if n:
                        values(N - 1, i, n - 1, s)
                    elif not first:
                        values(N - 1, i - 1, STEPS - 1, 1 - s)

            pe.wait_ge(keys_init, 1)
            for j in range(len(JOBS)):
                job(0, j, 0)
            score(0, 0, 0, 0, True)
            pair(0, 0, first=True)
            with pe.Fori(0, HP // 2 - 1) as j:
                pair(2 * j + 1, 1)
                pair(2 * j + 2, 0)
            pair(HP - 1, 1, last=True)
            values(STEPS * HP - 1, HP - 1, STEPS - 1, 1)


def mla_sample_stage(k, m):
    nc, io = k.nc, k.io
    KEYS = PAST + NS
    with ExitStack() as own:
        wuk = k.sbuf(own, "wuk", [P, HP, KV_LORA])
        wuv = k.sbuf(own, "wuv", [P, LT, HEADS * V_DIM])
        q_lat = k.sbuf(own, "q_lat", [P, LT, DEC_B, P])
        q_rot = k.sbuf(own, "q_rot", [P, DEC_B, P])
        cur = [k.sbuf(own, f"cur{s}", [P, LT + 1, P]) for s in range(2)]
        cache = [k.sbuf(own, f"cache{s}", [P, PAGES, CACHE_W]) for s in range(2)]
        new_rows = k.sbuf(own, "new_rows", [NS, KV_LORA])
        prob = [k.sbuf(own, f"sprob{s}", [P, KEYS]) for s in range(2)]
        prob_t = [k.sbuf(own, f"sprob_t{s}", [P, (PAGES + 1) * P]) for s in range(2)]
        stats = k.sbuf(own, "sstats", [P, 2, 3])
        o_lat = k.sbuf(own, "o_lat", [P, KV_LORA])
        o_lat_t = k.sbuf(own, "o_lat_t", [P, LT, HEADS, NS])
        smask = k.sbuf(own, "smask", [P, DEC_B, NS])
        table = k.sbuf(own, "page_table", [1, DEC_B * PAGES], I32)
        flat = lambda a, b: k.psum[:, a:b, :].rearrange("p b n -> p (b n)")
        scores, turn_bank, o_bank, ot_bank = flat(0, 3), flat(3, 6), k.banks[6], k.banks[7]
        const_in, table_in = k.sem("s_const_in"), k.sem("table_in")
        cache_in = [k.sem(f"cache_in{s}") for s in range(2)]
        ql_done, ql_out = k.sem("ql_done"), k.sem("ql_out")
        zeroed, rot_set = k.sem("q_rot_zeroed"), k.sem("q_rot_set")
        new_done, new_out = k.sem("new_done"), k.sem("new_out")
        cur_set = k.sem("cur_set")
        s_done, masked, max_done = k.sem("ss_done"), k.sem("smasked"), k.sem("smax_done")
        exp_done, sum_inv, normed = k.sem("sexp_done"), k.sem("ssum_inv"), k.sem("snormed")
        turned, turned_a, turned_d = k.sem("sturned"), k.sem("sturned_a"), k.sem("sturned_d")
        o_done, o_out, ot_done, ot_out = k.sem("so_done"), k.sem("so_out"), k.sem("ot_done"), k.sem("ot_out")
        final, final_out = k.sem("s_final"), k.sem("s_final_out")
        block = own.enter_context(nc.Block())

        @block.sync
        def _(sp):
            sp.dma_start(table[:], io["page_table"]).then_inc(table_in, 16)
            sp.wait_ge(table_in, 16)

            pool_rows = io["cache"].rearrange("g p n -> (g p n)")
            size = P * CACHE_W

            def load(b, s, wait):
                at = [sp.snap(sp.value_load(table[0:1, bass.ds(b * PAGES + j, 1)], min_val=0, max_val=N_POOL - 1)
                              * size) for j in range(PAGES)]
                if wait:
                    sp.wait_ge(o_done, b - 1)
                for j in range(PAGES):
                    sp.dma_start(cache[s][:, j, :], pool_rows[bass.ds(at[j], size)].rearrange("(p n) -> p n", p=P))\
                      .then_inc(cache_in[s], 16)
            load(0, 0, False)
            load(1, 1, False)
            with sp.Fori(1, DEC_B // 2) as i:
                load(2 * i, 0, True)
                load(2 * i + 1, 1, True)

        @block.scalar
        def _(act):
            act.dma_start(wuk[:], io["wuk"]).then_inc(const_in, 16)
            act.dma_start(wuv[:], io["wuv"]).then_inc(const_in, 16)
            act.dma_start(smask[:], io["smask"]).then_inc(const_in, 16)
            act.wait_ge(ql_done, 1)
            for hh in range(2):
                for t in range(LT):
                    dst = q_lat[:, t].rearrange("p s (a h t) -> p s a h t", h=2, t=DEC_S)[:, :, :, hh, :]
                    src = k.banks[2 * hh + t].rearrange("p (a s t) -> p s a t", s=DEC_B, t=DEC_S)
                    act.activation(dst, src, ACT.Copy).then_inc(ql_out, 1)
            act.wait_ge(new_done, 1)
            act.activation(new_rows[:], ot_bank[0:NS, 0:KV_LORA], ACT.Copy).then_inc(new_out, 1)
            act.wait_ge(const_in, 48)

            def step(b, s, early, edge):
                act.wait_ge(max_done, b + 1)
                if not early:
                    act.wait_ge(turned, b - 1)
                    act.wait_ge(sum_inv, b - 1)
                act.activation(prob[s][:], scores[:, 0:KEYS], ACT.Exp, bias=stats[:, s, 0:1],
                               accum_out=stats[:, s, 1:2]).then_inc(exp_done, 1)
                act.wait_ge(turned, b + 1)
                if not early:
                    act.wait_ge(o_done, b - 1)
                act.activation(prob_t[s][:, 0:512], turn_bank[:, 0:512], ACT.Copy)
                act.activation(prob_t[s][0:NS, PAST:PAST + P], turn_bank[0:NS, PAST:PAST + P], ACT.Copy)\
                   .then_inc(turned_a, 1)
                act.wait_ge(o_done, b + 1)
                if edge is not True:
                    act.wait_ge(ot_done, b)
                act.activation(o_lat[:], o_bank[:, 0:KV_LORA], ACT.Copy).then_inc(o_out, 1)

            step(0, 0, True, True)
            step(1, 1, True, False)
            with act.Fori(1, DEC_B // 2) as i:
                step(2 * i, 0, False, False)
                step(2 * i + 1, 1, False, False)

        @block.vector
        def _(dve):
            dve.memset(q_rot[:], 0.0).then_inc(zeroed, 1)
            dve.wait_ge(zeroed, 1)
            for hh, r in ((0, slice(64, P)), (1, slice(0, 64))):
                src = m.qs[r].rearrange("p (a h) (s t) -> p s a h t", h=2, t=DEC_S)[:, :, :, hh, :]
                dst = q_rot[r].rearrange("p s (a h t) -> p s a h t", h=2, t=DEC_S)[:, :, :, hh, :]
                last = dve.tensor_copy(dst, src)
            last.then_inc(rot_set, 1)
            dve.wait_ge(rot_set, 1)
            dve.wait_ge(ql_out, 4)
            dve.wait_ge(const_in, 48)

            def set_cur(b, s, early=False):
                if not early:
                    dve.wait_ge(s_done, b - 1)
                for t in range(LT):
                    dve.tensor_scalar(cur[s][:, t:t + 1, :], q_lat[:, t, bass.ds(b, 1), :], 1.0, None, ALU.mult)
                dve.tensor_scalar(cur[s][:, LT:LT + 1, :], q_rot[:, bass.ds(b, 1), :], 1.0, None, ALU.mult)\
                   .then_inc(cur_set, 1)

            def soft(b, s, early=False):
                new = scores[:, PAST:KEYS].unsqueeze(1)
                dve.wait_ge(s_done, b + 1)
                dve.tensor_tensor(new, new, smask[:, bass.ds(b, 1), :], ALU.add).then_inc(masked, 1)
                dve.wait_ge(masked, b + 1)
                if not early:
                    dve.wait_ge(exp_done, b - 1)
                dve.tensor_reduce(stats[:, s, 0:1], scores[:, 0:KEYS], AX.X, ALU.max, negate=True)\
                   .then_inc(max_done, 1)
                if not early:
                    dve.wait_ge(normed, b - 1)
                dve.wait_ge(exp_done, b + 1)
                dve.reciprocal(stats[:, s, 2:3], stats[:, s, 1:2]).then_inc(sum_inv, 1)
                dve.wait_ge(sum_inv, b + 1)
                dve.tensor_scalar(prob[s][:], prob[s][:], stats[:, s, 2:3], None, ALU.mult).then_inc(normed, 1)

            def rest(b, s, early=False):
                dve.wait_ge(turned, b + 1)
                if not early:
                    dve.wait_ge(o_done, b - 1)
                dve.tensor_copy(prob_t[s][:, 512:PAST], turn_bank[:, 512:PAST]).then_inc(turned_d, 1)
                dve.wait_ge(ot_done, b + 1)
                for t in range(LT):
                    dst = o_lat_t[:, t].rearrange("p h (s t) -> p h s t", t=DEC_S)[:, :, bass.ds(b, 1), :]
                    src = ot_bank[:, t * P:(t + 1) * P].rearrange("p (h a t) -> p h a t", a=1, t=DEC_S)
                    last = dve.tensor_scalar(dst, src, 1.0, None, ALU.mult)
                last.then_inc(ot_out, 1)

            def step(b, s, early=False, last=False):
                if not last:
                    set_cur(b + 1, 1 - s, early and s == 0)
                soft(b, s, early)
                rest(b, s, early)

            set_cur(0, 0, True)
            step(0, 0, True)
            step(1, 1, True)
            with dve.Fori(1, DEC_B // 2 - 1) as i:
                step(2 * i, 0)
                step(2 * i + 1, 1)
            step(DEC_B - 2, 0)
            step(DEC_B - 1, 1, last=True)
            dve.wait_ge(final, 1)
            dve.tensor_copy(m.o[:, :, SEQ:NT], o_bank.rearrange("p (a n) -> p a n", n=NS)).then_inc(final_out, 1)

        @block.tensor
        def _(pe):
            pe.wait_ge(const_in, 48)
            for hh in range(2):
                r = slice(64 * hh, 64 * hh + 64)
                for t in range(LT):
                    for a in range(HP):
                        last = pe.matmul(k.banks[2 * hh + t][:, a * NS:(a + 1) * NS], wuk[r, a, t * P:(t + 1) * P],
                                         m.qs[r, 2 * a + hh, :], start=True, stop=True)
            last.then_inc(ql_done, 1)
            for t in range(LT):
                last = pe.transpose(ot_bank[0:NS, t * P:(t + 1) * P], m.ckv[:, t, SEQ:NT], k.ident[:])
            last.then_inc(new_done, 1)
            pe.wait_ge(ql_out, 4)
            pe.wait_ge(new_out, 1)

            def score(b, s, turn, early=False):
                pe.wait_ge(cur_set, b + 1)
                pe.wait_ge(cache_in[s], turn)
                if not early:
                    pe.wait_ge(exp_done, b)
                for half in range(2):
                    pages = slice(half * 4, half * 4 + 4)
                    for t in range(LT + 1):
                        o = KV_LORA + t * PAGE
                        pe.matmul(scores[:, half * 512:(half + 1) * 512], cur[s][:, t, :],
                                  cache[s][:, pages, o:o + PAGE], start=t == 0, stop=t == LT)
                new = scores[:, PAST:KEYS]
                for t in range(LT):
                    pe.matmul(new, cur[s][:, t, :], m.ckv[:, t, SEQ:NT], start=t == 0, stop=False)
                pe.matmul(new, cur[s][:, LT, :], m.kr[:, SEQ:NT], start=False, stop=True).then_inc(s_done, 1)

            def turn_(b, s, early=False):
                pe.wait_ge(normed, b + 1)
                if not early:
                    pe.wait_ge(turned_a, b)
                    pe.wait_ge(turned_d, b)
                for j in range(PAGES):
                    pe.transpose(turn_bank[:, j * P:(j + 1) * P], prob[s][:, j * P:(j + 1) * P], k.ident[:])
                pe.transpose(turn_bank[0:NS, PAST:PAST + P], prob[s][:, PAST:KEYS], k.ident[:]).then_inc(turned, 1)

            def values(b, s, early=False):
                pe.wait_ge(turned_a, b + 1)
                pe.wait_ge(turned_d, b + 1)
                if not early:
                    pe.wait_ge(o_out, b)
                out = o_bank[:, 0:KV_LORA]
                for j in range(PAGES):
                    pe.matmul(out, prob_t[s][:, j * P:(j + 1) * P], cache[s][:, j, 0:KV_LORA],
                              start=j == 0, stop=False)
                pe.matmul(out, prob_t[s][0:NS, PAST:PAST + P], new_rows[:], start=False, stop=True)\
                  .then_inc(o_done, 1)
                pe.wait_ge(o_out, b + 1)
                if not early:
                    pe.wait_ge(ot_out, b)
                for t in range(LT):
                    last = pe.transpose(ot_bank[:, t * P:(t + 1) * P], o_lat[:, t * P:(t + 1) * P], k.ident[:])
                last.then_inc(ot_done, 1)

            def step(b, s, turn, early=False, last=False):
                if not last:
                    score(b + 1, 1 - s, turn)
                turn_(b, s, early)
                values(b, s, early)

            ALL = 16 * PAGES
            score(0, 0, ALL, True)
            step(0, 0, ALL, True)
            step(1, 1, 2 * ALL)
            with pe.Fori(1, DEC_B // 2 - 1) as i:
                step(2 * i, 0, ALL * i + ALL)
                step(2 * i + 1, 1, ALL * i + 2 * ALL)
            step(DEC_B - 2, 0, ALL * DEC_B // 2)
            step(DEC_B - 1, 1, None, last=True)
            pe.wait_ge(ot_out, DEC_B)
            for h in range(HEADS):
                a, hh = divmod(h, 2)
                for t in range(LT):
                    last = pe.matmul(o_bank[64 * hh:64 * hh + 64, a * NS:(a + 1) * NS],
                                     wuv[:, t, h * V_DIM:(h + 1) * V_DIM], o_lat_t[:, t, h, :],
                                     start=t == 0, stop=t == LT - 1)
            last.then_inc(final, 1)


def mla_out_stage(k, m):
    nc, io = k.nc, k.io
    with ExitStack() as own:
        o_hi = k.sbuf(own, "o_hi", [P, KT, NT], F32R)
        o_lo = k.sbuf(own, "o_lo", [P, KT, NT], F32R)
        y = k.sbuf(own, "mla_y", [P, KT, NT])
        raw = [k.sbuf(own, f"wo_raw{s}", [P, D_MODEL]) for s in range(2)]
        w_hi = [k.sbuf(own, f"wo_hi{s}", [P, D_MODEL], F32R) for s in range(2)]
        w_lo = [k.sbuf(own, f"wo_lo{s}", [P, D_MODEL], F32R) for s in range(2)]
        work = k.sbuf(own, "wo_work", [P, 2304])
        k.sq = work[:, 0:4 * MAXC].rearrange("p (k t) -> p k t", k=4)
        k.ss, k.ss2 = work[:, 1536:1536 + MAXC], work[:, 1920:1920 + MAXC]
        exit_ = Exit(k, "mla_out", 0, GATE_MIX, y)
        raw_in = [k.sem(f"wo_raw_in{s}") for s in range(2)]
        hi_ready, lo_ready = k.sem("wo_hi_ready"), k.sem("wo_lo_ready")
        o_hi_ready, o_lo_ready = k.sem("o_hi_ready"), k.sem("o_lo_ready")
        x_in, done, evac = k.sem("x_back"), k.sem("wo_done"), k.sem("wo_evac")
        banks = [k.banks[0:3], k.banks[3:6]]
        block = own.enter_context(nc.Block())

        @block.sync
        def _(sp):
            for j in range(KT):
                if j >= 2:
                    sp.wait_ge(lo_ready, j - 1)
                sp.dma_start(raw[j % 2][:], io["wo"][j]).then_inc(raw_in[j % 2], 16)
                if j == 1:
                    sp.wait_ge(o_lo_ready, KT)
                    sp.dma_start(k.x[:], io["x"]).then_inc(x_in, 16)
            sp.wait_ge(x_in, 16)

        @block.scalar
        def _(act):
            def split(j):
                act.wait_ge(raw_in[j % 2], 16 * (j // 2 + 1))
                if j >= 2:
                    act.wait_ge(done, NC * (j - 1))
                act.activation(w_hi[j % 2][:], raw[j % 2][:], ACT.Copy).then_inc(hi_ready, 1)
            for t in range(KT):
                act.activation(o_hi[:, t], m.o[:, t], ACT.Copy).then_inc(o_hi_ready, 1)
                if t == 0:
                    split(0)
            for j in range(KT):
                if j + 1 < KT:
                    split(j + 1)
                for c, (t0, w) in enumerate(CHUNKS):
                    act.wait_ge(done, NC * j + c + 1)
                    act.activation(y[:, j, t0:t0 + w], banks[j % 2][c][:, 0:w], ACT.Copy).then_inc(evac, 1)
            run_norm_act(k, act, exit_.norm, lambda c: None, lambda eng, c: eng.wait_ge(evac, NC * KT))

        @block.vector
        def _(dve):
            def split(j):
                dve.wait_ge(hi_ready, j + 1)
                dve.tensor_tensor(w_lo[j % 2][:], raw[j % 2][:], w_hi[j % 2][:], ALU.subtract).then_inc(lo_ready, 1)
            for t in range(KT):
                dve.wait_ge(o_hi_ready, t + 1)
                dve.tensor_tensor(o_lo[:, t], m.o[:, t], o_hi[:, t], ALU.subtract).then_inc(o_lo_ready, 1)
                if t == 0:
                    split(0)
            for j in range(1, KT):
                split(j)
            run_norm_dve(k, dve, exit_.norm, k.banks[6], lambda c: exit_.dve(k, dve, c, k.banks[c]))

        @block.gpsimd
        def _(pool):
            pool.wait_ge(x_in, 16)
            for c in range(NC):
                exit_.pool(k, pool, c)

        @block.tensor
        def _(pe):
            for j in range(KT):
                pe.wait_ge(lo_ready, j + 1)
                for c, (t0, w) in enumerate(CHUNKS):
                    if j >= 2:
                        pe.wait_ge(evac, NC * (j - 2) + c + 1)
                    bank = banks[j % 2][c][:, 0:w]
                    for t in range(KT):
                        if j == 0 and c == 0:
                            pe.wait_ge(o_lo_ready, t + 1)
                        o = slice(t * P, t * P + P)
                        oh, ol = o_hi[:, t, t0:t0 + w], o_lo[:, t, t0:t0 + w]
                        pe.matmul(bank, w_hi[j % 2][:, o], oh, start=t == 0, stop=False)
                        pe.matmul(bank, w_hi[j % 2][:, o], ol, start=False, stop=False)
                        last = pe.matmul(bank, w_lo[j % 2][:, o], oh, start=False, stop=t == KT - 1)
                    last.then_inc(done, 1)
            pe.wait_ge(evac, NC * KT)
            run_norm_pe(k, pe, exit_.norm, k.banks[6], k.banks[0:3])


class Latents:

    def __init__(self, k, ctx):
        self.o = k.x
        self.ckv = k.sbuf(ctx, "ckv", [P, LT, NT])
        self.kr = k.sbuf(ctx, "kr", [P, NT])
        self.qs = k.sbuf(ctx, "qs", [P, HEADS, NS])


def mla(k):
    with ExitStack() as own:
        m = Latents(k, own)
        with ExitStack() as latent:
            m.cq_hi = k.sbuf(latent, "cq_hi", [P, QT, NT], F32R)
            m.cq_lo = k.sbuf(latent, "cq_lo", [P, QT, NT], F32R)
            mla_project_stage(k, m)
            k.stage_done()
            mla_prompt_stage(k, m)
            k.stage_done()
        mla_sample_stage(k, m)
        k.stage_done()
        mla_out_stage(k, m)
        k.stage_done()


WINDOWS = (2, 4, 8, 16)
BUF = max(WINDOWS) - 1
GT = KT // len(WINDOWS)
SW = BUF + DEC_S


def pool_stage(k):
    nc, io = k.nc, k.io
    with ExitStack() as own:
        hp = k.sbuf(own, "pool_h", [P, KT, BUF + SEQ])
        hs = k.sbuf(own, "pool_hs", [P, KT, DEC_B, SW])
        sums = [k.sbuf(own, f"pool_sum{s}", [P, BUF + SEQ]) for s in range(2)]
        sums_s = [k.sbuf(own, f"pool_sum_s{s}", [P, KT, DEC_B, SW]) for s in range(2)]
        pooled = k.sbuf(own, "pooled", [P, KT, NT])
        y = k.sbuf(own, "pool_y", [P, KT, NT])
        w = k.sbuf(own, "pool_w", [P, KT, GT * P])
        ls = k.sbuf(own, "pool_scale", [P, KT])
        head = k.sbuf(own, "pool_head", [P, len(WINDOWS), BUF])
        last_rows = k.sbuf(own, "pool_last", [P, KT, N_SEQ, BUF])
        work = k.sbuf(own, "pool_work", [P, 2304])
        k.sq = work[:, 0:4 * MAXC].rearrange("p (k t) -> p k t", k=4)
        k.ss, k.ss2 = work[:, 1536:1536 + MAXC], work[:, 1920:1920 + MAXC]
        entry = Entry(k, "pool_in", 1, SCALE_MIX, SHIFT_MIX,
                      sums[0][:, 0:2 * MAXC].rearrange("p (b t) -> p b t", b=2),
                      sums[1][:, 0:KT * NS].rearrange("p (k t) -> p k t", k=KT), split=False)
        exit_ = Exit(k, "pool_out", 1, GATE_MIX, y)
        const_in, zeroed = k.sem("pool_const_in"), k.sem("pool_zeroed")
        step = k.sem("pool_step")
        pooled_done = k.sem("pooled_done")
        kept, out = k.sem("pool_kept"), k.sem("pool_state_out")
        done, evac = k.sem("pool_done"), k.sem("pool_evac")
        block = own.enter_context(nc.Block())

        @block.sync
        def _(sp):
            sp.dma_start(w[:], io["pool_w"]).then_inc(const_in, 16)
            sp.dma_start(ls[:], io["pool_scale"]).then_inc(const_in, 16)
            sp.dma_start(head[:], io["pool_head"]).then_inc(const_in, 16)
            sp.dma_start(last_rows[:, :, 1:, :], io["pool_state"]).then_inc(const_in, 16)
            sp.wait_ge(kept, 2)
            sp.dma_start(io["pool_out"], last_rows[:]).then_inc(out, 16)
            sp.wait_ge(out, 16)

        @block.gpsimd
        def _(pool):
            pool.memset(hp[:, :, 0:BUF], 0.0).then_inc(zeroed, 1)
            pool.wait_ge(const_in, 64)
            pool.tensor_copy(hs[:, :, :, 0:BUF], last_rows[:, :, 1:, :]).then_inc(zeroed, 1)
            pool.wait_ge(zeroed, 2)
            entry.ready(pool, NC - 1)
            pool.tensor_copy(last_rows[:, :, 0, :], hp[:, :, SEQ:SEQ + BUF]).then_inc(kept, 1)
            pool.tensor_copy(last_rows[:, :, 1:, :], hs[:, :, :, DEC_S:SW]).then_inc(kept, 1)
            for c in range(NC):
                exit_.pool(k, pool, c)

        @block.scalar
        def _(act):
            run_norm_act(k, act, entry.norm,
                         lambda c: entry.act(k, act, c, lambda kt, t0, n: hp[:, kt, BUF + t0:BUF + t0 + n],
                                             hs[:, :, :, BUF:]))
            act.wait_ge(const_in, 64)
            for kt in range(KT):
                for c, (t0, n) in enumerate(CHUNKS):
                    act.wait_ge(done, NC * kt + c + 1)
                    act.activation(y[:, kt, t0:t0 + n], k.banks[(NC * kt + c) % 6][:, 0:n], ACT.Copy,
                                   scale=ls[:, kt:kt + 1]).then_inc(evac, 1)
            run_norm_act(k, act, exit_.norm, lambda c: None, lambda eng, c: eng.wait_ge(evac, NC * KT))

        @block.vector
        def _(dve):
            run_norm_dve(k, dve, entry.norm, k.banks[6], lambda c: entry.dve(k, dve, c, k.banks[3 + c], None, None))
            dve.wait_ge(const_in, 64)
            dve.wait_ge(zeroed, 2)
            entry.ready(dve, NC - 1)
            n = [0]

            def do(ins):
                n[0] += 1
                ins.then_inc(step, 1)
                dve.wait_ge(step, n[0])

            W = BUF + SEQ
            for g, window in enumerate(WINDOWS):
                for kt in range(g * GT, (g + 1) * GT):
                    src, lo, span = hp[:, kt], 0, 1
                    while span < window:
                        dst = sums[(span.bit_length() - 1) % 2]
                        do(dve.tensor_tensor(dst[:, lo + span:W], src[:, lo + span:W], src[:, lo:W - span], ALU.add))
                        src, lo, span = dst, lo + span, 2 * span
                    do(dve.scalar_tensor_tensor(pooled[:, kt, 0:SEQ], src[:, BUF:W], 1.0 / window, hp[:, kt, BUF:W],
                                                ALU.mult, ALU.subtract))
                    do(dve.tensor_tensor(src[:, 0:BUF], src[:, BUF:2 * BUF], head[:, g], ALU.mult))
                    dve.tensor_tensor(pooled[:, kt, 0:BUF], src[:, 0:BUF], hp[:, kt, BUF:2 * BUF], ALU.subtract)\
                       .then_inc(pooled_done, 1)
                    dve.wait_ge(pooled_done, kt + 1)
            src, span = hs, 1
            for g, window in enumerate(WINDOWS):
                while span < window:
                    dst = sums_s[(span.bit_length() - 1) % 2]
                    first = g * GT
                    for kt in range(first, KT):
                        last = dve.tensor_tensor(dst[:, kt, :, 2 * span - 1:], src[:, kt, :, 2 * span - 1:],
                                                 src[:, kt, :, span - 1:SW - span], ALU.add)
                        do(last)
                    src, span = dst, 2 * span
                for kt in range(g * GT, (g + 1) * GT):
                    do(dve.scalar_tensor_tensor(pooled[:, kt, SEQ:NT].rearrange("p (s t) -> p s t", t=DEC_S),
                                                src[:, kt, :, BUF:], 1.0 / window, hs[:, kt, :, BUF:],
                                                ALU.mult, ALU.subtract))
            dve.memset(work[:, 0:1], 0.0).then_inc(pooled_done, 1)
            run_norm_dve(k, dve, exit_.norm, k.banks[6], lambda c: exit_.dve(k, dve, c, k.banks[c]))

        @block.tensor
        def _(pe):
            run_norm_pe(k, pe, entry.norm, k.banks[6], k.banks[3:6])
            pe.wait_ge(const_in, 64)
            pe.wait_ge(pooled_done, KT + 1)
            for kt in range(KT):
                g, mo = divmod(kt, GT)
                for c, (t0, n) in enumerate(CHUNKS):
                    i = NC * kt + c
                    if i >= 6:
                        pe.wait_ge(evac, i - 5)
                    for t in range(GT):
                        last = pe.matmul(k.banks[i % 6][:, 0:n], w[:, g * GT + t, mo * P:(mo + 1) * P],
                                         pooled[:, g * GT + t, t0:t0 + n], start=t == 0, stop=t == GT - 1)
                    last.then_inc(done, 1)
            pe.wait_ge(evac, NC * KT)
            run_norm_pe(k, pe, exit_.norm, k.banks[6], k.banks[0:3])


G, U, D = range(3)


def ffn_stage(k, layer):
    nc, io = k.nc, k.io
    n = f"ffn{layer}_"
    with ExitStack() as own:
        h_hi = k.sbuf(own, n + "h_hi", [P, KT, NT], F32R)
        h_lo = k.sbuf(own, n + "h_lo", [P, KT, NT], F32R)
        y = k.sbuf(own, n + "y", [P, KT, NT])
        raw = [k.sbuf(own, f"{n}raw{s}", [P, D_MODEL]) for s in range(3)]
        w_hi = [k.sbuf(own, f"{n}w_hi{s}", [P, D_MODEL], F32R) for s in range(3)]
        w_lo = [k.sbuf(own, f"{n}w_lo{s}", [P, D_MODEL], F32R) for s in range(3)]
        PROMPT_W = SEQ + CONV_W - 1
        SAMPLE_W = DEC_S + CONV_W - 1
        u = [k.sbuf(own, f"{n}u{s}", [P, PROMPT_W + DEC_B * SAMPLE_W]) for s in range(2)]
        work = k.sbuf(own, n + "work", [P, 2304])
        conv = [work[:, 0:NT], work[:, NT:2 * NT]]
        g_hi = k.sbuf(own, n + "g_hi", [P, NT], F32R)
        g_lo = k.sbuf(own, n + "g_lo", [P, NT], F32R)
        taps = k.sbuf(own, n + "taps", [P, 2 * PAIRS, 4])
        state = k.sbuf(own, n + "state", [P, 2 * PAIRS, 18])
        k.sq = work[:, 0:4 * MAXC].rearrange("p (k t) -> p k t", k=4)
        k.ss, k.ss2 = work[:, 1536:1536 + MAXC], work[:, 1920:1920 + MAXC]
        entry = Entry(k, n + "in", layer, SCALE_FFN, SHIFT_FFN,
                      u[0][:, 0:2 * MAXC].rearrange("p (b t) -> p b t", b=2),
                      u[1][:, 0:KT * NS].rearrange("p (k t) -> p k t", k=KT))
        exit_ = Exit(k, n + "out", layer, GATE_FFN, y)
        per_half = lambda what: [k.sem(f"{n}{what}_{s}") for s in ("g", "u")]
        per_unit = lambda what: [k.sem(f"{n}{what}_{s}") for s in ("g", "u", "d")]
        raw_in = per_unit("raw_in")
        hi_ready = per_unit("hi_ready")
        lo_ready = per_unit("lo_ready")
        const_in = k.sem(n + "const_in")
        up_done = per_half("up_done")
        evac = per_half("evac")
        prev_in = per_half("prev_in")
        saved = per_half("saved")
        conv_step = per_half("conv_step")
        silu_done = k.sem(n + "silu_done")
        product = k.sem(n + "product")
        g_hi_ready, g_lo_ready = k.sem(n + "g_hi_ready"), k.sem(n + "g_lo_ready")
        down_done = k.sem(n + "down_done")
        acc_done = k.sem(n + "acc_done")
        cleared = k.sem(n + "cleared")
        state_out = k.sem(n + "state_out")
        half_bank = [k.banks[0:3], k.banks[3:6]]
        down_bank = k.banks[6:8]
        block = own.enter_context(nc.Block())

        @block.sync
        def _(sp):
            sp.dma_start(taps[:], io["taps"][:, layer]).then_inc(const_in, 16)
            sp.dma_start(state[:], io["conv_state"][:, layer]).then_inc(const_in, 16)

            def load(p, wait):
                for s in (G, U, D):
                    if wait:
                        sp.wait_ge(lo_ready[s], p)
                    sp.dma_start(raw[s][:], io["ffn_w"][layer, bass.ds(p, 1), s].rearrange("a p n -> p (a n)"))\
                      .then_inc(raw_in[s], 16)

            load(0, False)
            with sp.Fori(1, PAIRS) as p:
                load(p, True)
            for s in (G, U):
                sp.wait_ge(saved[s], PAIRS)
            sp.dma_start(io["conv_out"][:, layer], state[:]).then_inc(state_out, 16)
            sp.wait_ge(state_out, 16)

        @block.gpsimd
        def _(pool):
            pool.memset(y[:], 0.0).then_inc(cleared, 1)
            entry.ready(pool, NC - 1)
            for s in (G, U):
                pool.memset(u[s][:, 0:CONV_W - 1], 0.0).then_inc(cleared, 1)
            for c in range(NC):
                exit_.pool(k, pool, c)

        def split_hi(act, s, p):
            act.wait_ge(raw_in[s], 16 * p + 16)
            if s == D:
                act.wait_ge(down_done, 24 * p)
            else:
                act.wait_ge(up_done[s], 3 * p)
            act.activation(w_hi[s][:], raw[s][:], ACT.Copy).then_inc(hi_ready[s], 1)

        def evacuate(act, s, p):
            m = 2 * p + s
            rows = u[s][:, PROMPT_W:].rearrange("p (s t) -> p s t", t=SAMPLE_W)
            tap2, bias = taps[:, bass.ds(m, 1), 2], taps[:, bass.ds(m, 1), 3]
            act.wait_ge(conv_step[s], 4 * p)
            act.wait_ge(product, p)
            if s == G:
                act.wait_ge(g_lo_ready, p)
            for c, (t0, n_) in enumerate(CHUNKS):
                w = prompt_cols(c)[1]
                bank = half_bank[s][c]
                act.wait_ge(up_done[s], 3 * p + c + 1)
                act.activation(u[s][:, 2 + t0:2 + t0 + w], bank[:, 0:w], ACT.Copy)
                if w < n_:
                    act.activation(rows[:, :, 2:], bank[:, w:n_].rearrange("p (s t) -> p s t", t=DEC_S), ACT.Copy)
                act.activation(conv[s][:, t0:t0 + n_], bank[:, 0:n_], ACT.Identity, bias=bias, scale=tap2)\
                   .then_inc(evac[s], 1)

        @block.scalar
        def _(act):
            run_norm_act(k, act, entry.norm, lambda c: entry.act(k, act, c, *put_in(h_hi)))
            act.wait_ge(const_in, 32)
            entry.ready(act, NC - 1)
            act.wait_ge(cleared, 3)

            def pair(p, first=False, last=False):
                split_hi(act, U, p)
                if not first:
                    split_hi(act, D, p - 1)
                    act.wait_ge(product, p)
                    act.wait_ge(down_done, 24 * (p - 1))
                    act.activation(g_hi[:], conv[G], ACT.Copy).then_inc(g_hi_ready, 1)
                evacuate(act, G, p)
                if not last:
                    split_hi(act, G, p + 1)
                act.wait_ge(conv_step[G], 4 * p + 4)
                act.activation(conv[G], conv[G], ACT.Silu).then_inc(silu_done, 1)
                evacuate(act, U, p)

            split_hi(act, G, 0)
            pair(0, first=True)
            pair(1)
            with act.Fori(2, PAIRS - 1) as p:
                pair(p)
            pair(PAIRS - 1, last=True)
            split_hi(act, D, PAIRS - 1)
            act.wait_ge(product, PAIRS)
            act.wait_ge(down_done, 24 * (PAIRS - 1))
            act.activation(g_hi[:], conv[G], ACT.Copy).then_inc(g_hi_ready, 1)
            run_norm_act(k, act, exit_.norm, lambda c: None,
                         lambda eng, c: (eng.wait_ge(acc_done, 24 * PAIRS), eng.wait_ge(g_lo_ready, PAIRS)))

        def split_lo(dve, s, p):
            dve.wait_ge(hi_ready[s], p + 1)
            dve.tensor_tensor(w_lo[s][:], raw[s][:], w_hi[s][:], ALU.subtract).then_inc(lo_ready[s], 1)

        def conv_steps(dve, s, p):
            m = 2 * p + s
            rows = u[s][:, PROMPT_W:].rearrange("p (s t) -> p s t", t=SAMPLE_W)
            cp, cs = conv[s][:, 0:SEQ], conv[s][:, SEQ:NT].rearrange("p (s t) -> p s t", t=DEC_S)

            mine = state[:, bass.ds(m, 1), :]
            mine_s = mine[:, :, 0:16].rearrange("p a (s t) -> p (a s) t", t=2)

            def prompt(tap):
                dve.scalar_tensor_tensor(cp, u[s][:, tap:tap + SEQ], taps[:, bass.ds(m, 1), tap], cp,
                                         ALU.mult, ALU.add).then_inc(conv_step[s], 1)

            def samples(tap):
                dve.scalar_tensor_tensor(cs, rows[:, :, tap:tap + DEC_S], taps[:, bass.ds(m, 1), tap], cs,
                                         ALU.mult, ALU.add).then_inc(conv_step[s], 1)

            def tap_1():
                dve.tensor_copy(rows[:, :, 0:2], mine_s).then_inc(prev_in[s], 1)
                dve.wait_ge(evac[s], 3 * p + 3)
                prompt(1)
                dve.wait_ge(prev_in[s], p + 1)
                samples(1)
                dve.tensor_copy(mine_s, rows[:, :, DEC_S:SAMPLE_W])
                dve.tensor_copy(mine[:, :, 16:18], u[s][:, SEQ:SEQ + 2].unsqueeze(1)).then_inc(saved[s], 1)

            def tap_0():
                dve.wait_ge(conv_step[s], 4 * p + 2)
                prompt(0)
                samples(0)
            return [tap_1, tap_0]

        def accumulate(dve, p, i):
            kt, c = divmod(i, NC)
            t0, n_ = CHUNKS[c]
            dve.wait_ge(down_done, 24 * p + i + 1)
            dst = y[:, kt, t0:t0 + n_]
            dve.tensor_tensor(dst, down_bank[i % 2][:, 0:n_], dst, ALU.add).then_inc(acc_done, 1)

        @block.vector
        def _(dve):
            run_norm_dve(k, dve, entry.norm, down_bank[0],
                         lambda c: entry.dve(k, dve, c, half_bank[U][c], h_hi, h_lo))
            dve.wait_ge(const_in, 32)
            dve.wait_ge(cleared, 3)

            def finish_g(p):
                for f in conv_steps(dve, U, p):
                    f()
                dve.wait_ge(conv_step[U], 4 * p + 4)
                dve.wait_ge(silu_done, p + 1)
                dve.tensor_tensor(conv[G], conv[G], conv[U], ALU.mult).then_inc(product, 1)

            def split_g(p):
                dve.wait_ge(g_hi_ready, p + 1)
                dve.tensor_tensor(g_lo[:], conv[G], g_hi[:], ALU.subtract).then_inc(g_lo_ready, 1)

            def pair(p, first=False, last=False):
                if not first:
                    finish_g(p - 1)
                split_lo(dve, U, p)
                if not first:
                    split_lo(dve, D, p - 1)
                    split_g(p - 1)
                side = conv_steps(dve, G, p)
                if not last:
                    side = [lambda: split_lo(dve, G, p + 1)] + side
                for i in range(24):
                    if not first:
                        accumulate(dve, p - 1, i)
                    if i % 3 == 2 and side:
                        side.pop(0)()

            split_lo(dve, G, 0)
            pair(0, first=True)
            pair(1)
            with dve.Fori(2, PAIRS - 1) as p:
                pair(p)
            pair(PAIRS - 1, last=True)
            finish_g(PAIRS - 1)
            split_lo(dve, D, PAIRS - 1)
            split_g(PAIRS - 1)
            for i in range(24):
                accumulate(dve, PAIRS - 1, i)
            run_norm_dve(k, dve, exit_.norm, down_bank[0],
                         lambda c: exit_.dve(k, dve, c, half_bank[U][c]))

        @block.tensor
        def _(pe):
            run_norm_pe(k, pe, entry.norm, down_bank[0], half_bank[U])

            def products(bank, s, kt, c, act_hi, act_lo, first, last):
                w = slice(kt * P, kt * P + P)
                a = slice(0, CHUNKS[c][1])
                pe.matmul(bank[:, a], w_hi[s][:, w], act_hi, start=first, stop=False)
                pe.matmul(bank[:, a], w_hi[s][:, w], act_lo, start=False, stop=False)
                return pe.matmul(bank[:, a], w_lo[s][:, w], act_hi, start=False, stop=last)

            def down(p, i):
                kt, c = divmod(i, NC)
                t0, n_ = CHUNKS[c]
                if i == 0:
                    pe.wait_ge(lo_ready[D], p + 1)
                    pe.wait_ge(g_lo_ready, p + 1)
                pe.wait_ge(acc_done, 24 * p + max(i - 1, 0))
                last = products(down_bank[i % 2], D, kt, c, g_hi[:, t0:t0 + n_], g_lo[:, t0:t0 + n_], True, True)
                last.then_inc(down_done, 1)
                return last

            def up(s, p, first, with_down):
                pe.wait_ge(lo_ready[s], p + 1)
                for c, (t0, n_) in enumerate(CHUNKS):
                    if s == G and first:
                        entry.ready(pe, c)
                    if s == U and first and c == 0:
                        entry.ready(pe, NC - 1)
                    if not first:
                        pe.wait_ge(evac[s], 3 * (p - 1) + c + 1)
                    for kt in range(KT):
                        last = products(half_bank[s][c], s, kt, c, h_hi[:, kt, t0:t0 + n_],
                                        h_lo[:, kt, t0:t0 + n_], kt == 0, kt == KT - 1)
                        if kt == KT - 1:
                            last.then_inc(up_done[s], 1)
                        if with_down:
                            down(p - 1, c * KT + kt)

            def pair(p, first=False):
                up(G, p, first, False)
                up(U, p, first, not first)

            pair(0, first=True)
            pair(1)
            with pe.Fori(2, PAIRS) as p:
                pair(p)
            for i in range(24):
                down(PAIRS - 1, i)
            run_norm_pe(k, pe, exit_.norm, down_bank[0], half_bank[U])


def output_stage(k):
    with ExitStack() as own:
        x_out = k.sem("x_out")
        block = own.enter_context(k.nc.Block())

        @block.sync
        def _(sp):
            sp.dma_start(k.io["x_out"], k.x[:]).then_inc(x_out, 16)
            sp.wait_ge(x_out, 16)


def program(nc, io):
    with ExitStack() as ctx:
        k = Kernel(nc, ctx, io)
        adaln_stage(k)
        k.stage_done()
        mla(k)
        ffn_stage(k, 0)
        k.stage_done()
        pool_stage(k)
        k.stage_done()
        ffn_stage(k, 1)
        k.stage_done()
        output_stage(k)


def columns(prompt, sample):
    rows = np.concatenate([prompt, sample.reshape(NS, -1)], axis=0)
    return np.ascontiguousarray(rows.T.reshape(-1, P, NT).transpose(1, 0, 2))


def units(w):
    kt = w.shape[0] // P
    return w.reshape(kt, P, w.shape[1] // P, P).transpose(2, 1, 0, 3).reshape(-1, P, kt * P)


def rotation():
    half = ROPE // 2
    inv = np.float32(10000.0) ** (-np.arange(half, dtype=np.float32) / half)
    pos = np.concatenate([np.arange(SEQ), PAST + np.tile(np.arange(DEC_S), DEC_B)]).astype(np.float32)
    ang = inv[:, None] * pos[None, :]
    cos, sin = np.cos(ang), np.sin(ang)
    return np.concatenate([cos, cos]), np.concatenate([-sin, sin])


def swapped(w):
    return np.concatenate([w[..., ROPE // 2:], w[..., :ROPE // 2]], axis=-1)


def attention_inputs(a):
    w_dkv, w_uq, w_uk, w_uv = (a[n][0] for n in ("mla_w_dkv", "mla_w_uq", "mla_w_uk", "mla_w_uv"))
    kr = w_dkv[:, KV_LORA:]
    proj = np.concatenate([units(w_dkv[:, :KV_LORA]), units(np.concatenate([swapped(kr)] * 2 + [kr] * 2, axis=1)),
                           units(a["mla_w_dq"][0])])
    uq = w_uq.reshape(Q_LORA, HEADS, NOPE + ROPE)
    nope, rope = uq[..., :NOPE], uq[..., NOPE:]
    rope = np.concatenate([rope, swapped(rope)], axis=-1)
    even = np.concatenate([nope, rope], axis=-1)[:, 0::2]
    odd = np.concatenate([rope, nope], axis=-1)[:, 1::2]
    heads = np.stack([even, odd], axis=2).reshape(QT, P, HP, 2, P).transpose(2, 1, 3, 0, 4).reshape(HP, P, -1)
    pairs = lambda w: w.reshape(LT, P, HP, P).transpose(2, 1, 0, 3).reshape(HP, P, -1)
    cos, sin = rotation()
    one = np.ones((NOPE, NT), np.float32)
    rot = np.stack([np.concatenate([one, cos, sin]), np.concatenate([cos, sin, one])], axis=1)
    lat, krope = a["cache_kv_latent"][0], a["cache_k_rope"][0]
    pages = lat.shape[0]
    lat_t = lat.reshape(pages, PAGE, LT, P).transpose(0, 3, 2, 1).reshape(pages, P, LT * PAGE)
    kr_t = np.tile(krope.transpose(0, 2, 1), (1, P // ROPE, 1))
    t = np.arange(DEC_S)
    own = np.eye(DEC_B, dtype=bool)[None, :, :, None] & (t[:, None, None, None] >= t)
    smask = np.where(own, 0.0, NEG).astype(np.float32).reshape(DEC_S, DEC_B, NS)
    tile = np.arange(P)
    return {
        "proj_w": proj,
        "ktab": np.concatenate([sin, sin, cos, cos]),
        "latent_gain": np.concatenate([a["mla_kv_norm"][0], a["mla_q_norm"][0]]).reshape(LT + QT, P).T,
        "pair_w": np.concatenate([heads, pairs(w_uk), pairs(w_uv)], axis=2),
        "rot": (rot * np.float32(SCALE)).astype(np.float32),
        "mask": np.where(tile[:, None] >= tile, 0.0, NEG).astype(np.float32),
        "cache": np.concatenate([lat, lat_t, kr_t], axis=2),
        "page_table": a["page_table"].astype(np.int32).reshape(1, -1),
        "wuk": w_uk.transpose(1, 2, 0).reshape(HP, P, KV_LORA).transpose(1, 0, 2),
        "wuv": w_uv.reshape(LT, P, HEADS * V_DIM).transpose(1, 0, 2),
        "smask": np.tile(smask, (HEADS, 1, 1)),
        "wo": units(a["mla_w_o"][0]),
    }


def pool_inputs(a):
    pos = np.arange(BUF)
    head = np.stack([1.0 / np.minimum(pos + 1, w) for w in WINDOWS]).astype(np.float32)
    return {
        "pool_w": a["pool_w"][0].reshape(KT, P, GT * P).transpose(1, 0, 2),
        "pool_scale": a["pool_scale"][0].reshape(KT, P).T,
        "pool_head": np.tile(head[None], (P, 1, 1)),
        "pool_state": a["state_pool"][0].reshape(DEC_B, BUF, KT, P).transpose(3, 2, 0, 1),
    }


def laid_out(a):
    f = D_FF
    pair_units = []
    for l in range(2):
        up = units(a["ffn_w_up"][l]).reshape(2, PAIRS, P, D_MODEL)
        down = a["ffn_w_down"][l].reshape(1, PAIRS, P, D_MODEL)
        pair_units.append(np.concatenate([up, down]).transpose(1, 0, 2, 3))
    by_pair = lambda v: v.reshape(2, PAIRS, P).transpose(2, 1, 0).reshape(P, 2 * PAIRS)
    taps = np.stack([np.stack([by_pair(a["ffn_conv_w"][l, t]) for t in range(CONV_W)]
                              + [by_pair(a["ffn_conv_b"][l])], axis=-1) for l in range(2)], axis=1)
    state = a["state_conv"].reshape(2, DEC_B, 2, 2, PAIRS, P).transpose(5, 0, 4, 3, 1, 2)
    state = state.reshape(P, 2, 2 * PAIRS, 16)
    state = np.concatenate([state, np.zeros((P, 2, 2 * PAIRS, 2), np.float32)], axis=-1)
    gains = np.stack([a["norm_mix_pre"], a["norm_mix_post"], a["norm_ffn_pre"], a["norm_ffn_post"]], axis=1)
    cond = np.concatenate([a["c_prompt"], a["c_sample"]])
    return {
        "x": columns(a["x_prompt"][0], a["x_sample"]),
        "cond": cond.T.reshape(KT, P, N_SEQ).transpose(1, 0, 2),
        "ada_w": a["ada_w"].reshape(2, KT, P, SIX // ADA_GROUP, ADA_GROUP * P).transpose(0, 3, 2, 1, 4)
        .reshape(2 * SIX // ADA_GROUP, P, ADA_GROUP * D_MODEL),
        "ada_b": a["ada_b"].reshape(2, SIX, P).transpose(2, 0, 1),
        "gains": gains.reshape(2, 4, KT, P).transpose(3, 0, 1, 2),
        "ident": np.eye(P, dtype=np.float32),
        "ffn_w": np.stack(pair_units),
        "taps": taps,
        "conv_state": state,
        **attention_inputs(a),
        **pool_inputs(a),
    }


OUTPUTS = {
    "x_out": [P, KT, NT],
    "conv_out": [P, 2, 2 * PAIRS, 18],
    "ckv_out": [P, LT, NT],
    "kr_out": [ROPE, NT],
    "pool_out": [P, KT, N_SEQ, BUF],
}


def kernel(**inputs):
    import concourse.bacc as bacc
    from concourse.bass_utils import run_bass_kernel_spmd

    a = {name: np.asarray(v) for name, v in inputs.items()}
    nc = bacc.Bacc("TRN2", target_bir_lowering=False, num_devices=1)
    arrays = {f"in_{n}": np.ascontiguousarray(v) for n, v in laid_out(a).items()}
    io = {n[3:]: nc.dram_tensor(n, list(v.shape), mybir.dt.from_np(v.dtype), kind="ExternalInput").ap()
          for n, v in arrays.items()}
    for n, shape in OUTPUTS.items():
        io[n] = nc.dram_tensor(f"out_{n}", shape, F32, kind="ExternalOutput").ap()
    program(nc, io)
    r = run_bass_kernel_spmd(nc, [arrays], core_ids=[0]).results[0]
    out = {n: np.asarray(r[f"out_{n}"]) for n in OUTPUTS}

    def rows(v, width):
        return v.transpose(1, 0, 2).reshape(width, -1).T

    x = rows(out["x_out"], D_MODEL)
    conv = out["conv_out"]
    conv_s = conv[..., 0:16].reshape(P, 2, PAIRS, 2, DEC_B, 2).transpose(1, 4, 5, 3, 2, 0)
    conv_p = conv[..., 16:18].reshape(P, 2, PAIRS, 2, 2).transpose(1, 4, 3, 2, 0)
    conv_s = conv_s.reshape(2, DEC_B, 2, 2 * D_FF)
    conv_p = conv_p.reshape(2, 1, 2, 2 * D_FF)
    ckv, kr = rows(out["ckv_out"], KV_LORA), out["kr_out"].T
    state = out["pool_out"].transpose(2, 3, 1, 0).reshape(N_SEQ, BUF, D_MODEL)
    sample = lambda v: v[SEQ:].reshape(DEC_B, DEC_S, -1)
    return (x[None, :SEQ], sample(x), ckv[None, None, :SEQ], kr[None, None, :SEQ], sample(ckv)[None],
            sample(kr)[None], state[None, :1], state[None, 1:], conv_p, conv_s)
```

```python
import numpy as np

import concourse.bass as bass
from concourse import mybir
from contextlib import ExitStack

F32 = mybir.dt.float32
F32R = mybir.dt.float32r
I32 = mybir.dt.int32
ALU = mybir.AluOpType
ACT = mybir.ActivationFunctionType
AX = mybir.AxisListType

P = 128
D_MODEL, SEQ, DEC_B, DEC_S = 1024, 1024, 8, 8
D_FF, CONV_W = 2816, 3
KT = D_MODEL // P
NS = DEC_B * DEC_S
NT = SEQ + NS
CHUNKS = [(0, 384), (384, 384), (768, NT - 768)]
NC = len(CHUNKS)
MAXC = 384
PAIRS = D_FF // P
N_SEQ = 1 + DEC_B
SIX = 6 * KT
SHIFT_MIX, SCALE_MIX, GATE_MIX, SHIFT_FFN, SCALE_FFN, GATE_FFN = range(0, SIX, KT)
EPS = 1e-6
ADA_GROUP = 4
ADA_SLOTS = 4


def col_tiles(c):
    n = CHUNKS[c][1]
    return [(o, min(P, n - o)) for o in range(0, n, P)]


class Norm:

    def __init__(self, k, name, jobs):
        self.jobs = jobs
        s = lambda what: k.sem(f"{name}_{what}")
        self.squared = s("squared")
        self.summed = s("summed")
        self.std = s("std")
        self.turned = s("turned")
        self.rstd = s("rstd")
        self.spread_done = s("spread")
        self.groups = []
        last, n = [0, 0], 0
        for src, _, _ in jobs:
            mine = []
            for slot, g, w in NORM_GROUPS[src.shape[1]]:
                n += 1
                mine.append((g, w, slot, last[slot]))
                last[slot] = n
            self.groups.append(mine)
        self.groups_to = [sum(len(x) for x in self.groups[:j + 1]) for j in range(len(jobs))]

    def act(self, k, act, j, ready=None):
        src, c, _ = self.jobs[j]
        t0, n = CHUNKS[c]
        for g, w, slot, before in self.groups[j]:
            if ready:
                ready(j, g + w)
            if before:
                act.wait_ge(self.summed, before)
            act.activation(k.sq[:, 3 * slot:3 * slot + w, 0:n], src[:, g:g + w, t0:t0 + n], ACT.Square)\
               .then_inc(self.squared, 1)
        act.wait_ge(self.summed, self.groups_to[j])
        if j:
            act.wait_ge(self.turned, j)
        act.activation(k.row[:, 0:n], k.stat_bank[0:1, 0:n], ACT.Sqrt, scale=1.0 / (src.shape[1] * P),
                       bias=k.eps[0:1, :]).then_inc(self.std, 1)

    def pe(self, k, pe, j):
        self.pe_sum(k, pe, j)
        self.pe_turn(k, pe, j)

    def pe_sum(self, k, pe, j):
        n = CHUNKS[self.jobs[j][1]][1]
        first = self.groups_to[j - 1] if j else 0
        tiles = sum(w for _, w, _, _ in self.groups[j])
        if j:
            pe.wait_ge(self.rstd, j)
        for i, (g, w, slot, _) in enumerate(self.groups[j]):
            pe.wait_ge(self.squared, first + i + 1)
            for t in range(w):
                last = pe.matmul(k.stat_bank[0:1, 0:n], k.ones[:, 0:1], k.sq[:, 3 * slot + t, 0:n],
                                 start=g + t == 0, stop=g + t == tiles - 1)
            last.then_inc(self.summed, 1)

    def pe_turn(self, k, pe, j):
        pe.wait_ge(self.std, j + 1)
        for i, (o, w) in enumerate(col_tiles(self.jobs[j][1])):
            last = pe.matmul(k.stat_bank[0:w, MAXC + i:MAXC + i + 1], k.row[0:1, o:o + w], k.ones[0:1, 0:1],
                             start=True, stop=True)
        last.then_inc(self.turned, 1)

    def dve(self, k, dve, j):
        dve.wait_ge(self.turned, j + 1)
        dve.reciprocal(self.jobs[j][2], k.stat_bank[:, MAXC:MAXC + 3]).then_inc(self.rstd, 1)

    def pe_spread(self, k, pe, j, bank):
        pe.wait_ge(self.rstd, j + 1)
        spread(k, pe, self.jobs[j][1], self.jobs[j][2], bank).then_inc(self.spread_done, 1)


NORM_GROUPS = {8: [(0, 0, 3), (1, 3, 2), (0, 5, 3)], 4: [(0, 0, 3), (1, 3, 1)], 2: [(0, 0, 2)]}
NORM_WORK = 5 * MAXC


def spread(k, pe, c, rstd, bank):
    for j, (o, w) in enumerate(col_tiles(c)):
        last = pe.matmul(bank[:, o:o + w], rstd[0:w, j:j + 1].to_broadcast([w, P]), k.ident[0:w, 0:w],
                         start=True, stop=True)
    return last


class Kernel:

    def __init__(self, nc, ctx, io):
        self.nc, self.ctx, self.io, self.sems = nc, ctx, io, []
        self.x = self.sbuf(ctx, "x", [P, KT, NT])
        self.ada = self.sbuf(ctx, "ada", [P, 2, SIX, N_SEQ])
        self.ident = self.sbuf(ctx, "ident", [P, P])
        self.ones = self.sbuf(ctx, "ones", [P, 1])
        self.eps = self.sbuf(ctx, "eps", [P, 1])
        self.rstd = self.sbuf(ctx, "rstd", [P, 3, NC, 3])
        self.psum = ctx.enter_context(nc.psum_tensor("psum", [P, 8, 512], F32))
        self.banks = [self.psum[:, i, :] for i in range(8)]
        self.stat_bank = self.banks[6]

    def norm_work(self, flat):
        self.sq = flat[:, 0:NORM_WORK].rearrange("p (k t) -> p k t", k=5)
        self.row = flat[0:1, NORM_WORK:NORM_WORK + MAXC]

    def sbuf(self, ctx, name, shape, dt=F32):
        return ctx.enter_context(self.nc.sbuf_tensor(name, shape, dt))

    def sem(self, name):
        self.sems.append(self.nc.alloc_semaphore(name=name))
        return self.sems[-1]

    def stage_done(self):
        self.nc.clear_and_free_semaphores(self.sems)
        self.nc.all_engine_barrier()
        self.sems = []


def adaln_stage(k):
    nc, io = k.nc, k.io
    GROUPS = 2 * SIX // ADA_GROUP
    with ExitStack() as own:
        w = k.sbuf(own, "ada_w", [P, ADA_SLOTS, ADA_GROUP * D_MODEL])
        w_hi = k.sbuf(own, "ada_w_hi", [P, 2, ADA_GROUP * D_MODEL], F32R)
        w_lo = k.sbuf(own, "ada_w_lo", [P, 2, ADA_GROUP * D_MODEL], F32R)
        c = k.sbuf(own, "cond", [P, KT, N_SEQ])
        c_silu = k.sbuf(own, "cond_silu", [P, KT, N_SEQ])
        c_parts = k.sbuf(own, "cond_parts", [P, KT, 2 * N_SEQ], F32R)
        fold = k.sbuf(own, "fold", [2 * N_SEQ, N_SEQ])
        rows = k.sbuf(own, "ada_rows", [2 * N_SEQ, ADA_SLOTS, ADA_GROUP * P])
        bias = k.sbuf(own, "ada_bias", [P, 2, SIX])
        gains = k.sbuf(own, "gains", [P, 2, 4, KT])
        k.norm_work(k.sbuf(own, "ada_norm_work", [P, NORM_WORK + MAXC]))
        x_norm = Norm(k, "x0", [(k.x, c_, k.rstd[:, 0, c_, :]) for c_ in range(NC)])
        small_in, const_in, x_in = k.sem("ada_small_in"), k.sem("const_in"), k.sem("x_in")
        w_in = [k.sem(f"ada_w_in{s}") for s in range(ADA_SLOTS)]
        silu_done, parts = k.sem("cond_silu_done"), k.sem("cond_parts_done")
        constants = k.sem("constants")
        hi_ready, lo_ready = k.sem("ada_hi"), k.sem("ada_lo")
        used = k.sem("ada_used")
        rows_done = k.sem("ada_rows_done")
        turned = k.sem("ada_turned")
        evac = k.sem("ada_evac")
        folded = k.sem("ada_folded")
        block = own.enter_context(nc.Block())

        def run(step, eng):
            for s in range(ADA_SLOTS):
                step(s, s, True)

            def rest(n):
                for s in range(ADA_SLOTS):
                    step(n * ADA_SLOTS + s, s, False)
            with eng.Fori(1, GROUPS // ADA_SLOTS) as n:
                rest(n)

        def wait(eng, sem, value, first):
            if not first or value > 0:
                eng.wait_ge(sem, value)

        @block.sync
        def _(sp):
            sp.dma_start(c[:], io["cond"]).then_inc(small_in, 16)

            def load(m, s, first):
                wait(sp, lo_ready, m - ADA_SLOTS + 1, first)
                sp.dma_start(w[:, s, :], io["ada_w"][bass.ds(m, 1)]
                             .rearrange("a p n -> p (a n)")).then_inc(w_in[s], 16)
            run(load, sp)

        @block.scalar
        def _(act):
            act.dma_start(k.ident[:], io["ident"]).then_inc(const_in, 16)
            act.dma_start(bias[:], io["ada_b"]).then_inc(const_in, 16)
            act.dma_start(gains[:], io["gains"]).then_inc(const_in, 16)
            act.dma_start(k.x[:], io["x"]).then_inc(x_in, 16)
            act.wait_ge(small_in, 16)
            act.activation(c_silu[:], c[:], ACT.Silu).then_inc(silu_done, 1)
            act.wait_ge(silu_done, 1)
            act.activation(c_parts[:, :, 0:N_SEQ], c_silu[:], ACT.Copy).then_inc(parts, 1)

            def copy_rows(m, s, first):
                wait(act, used, m + 1, first)
                wait(act, turned, m - 3, first)
                act.activation(rows[:, s, :], k.banks[s][0:2 * N_SEQ, :], ACT.Copy).then_inc(rows_done, 1)

            def step(m, s, first):
                if first:
                    act.wait_ge(w_in[s], 16)
                else:
                    act.wait_ge(w_in[s], 4 * (m - s) + 16)
                wait(act, used, m - 1, first)
                act.activation(w_hi[:, s % 2, :], w[:, s, :], ACT.Copy).then_inc(hi_ready, 1)
                if not (first and s == 0):
                    copy_rows(m - 1, (s - 1) % ADA_SLOTS, first)
                if first and s == ADA_SLOTS - 1:
                    act.wait_ge(x_in, 16)
                    act.wait_ge(constants, 2)
                    for j in range(NC):
                        x_norm.act(k, act, j)
            run(step, act)
            copy_rows(GROUPS - 1, ADA_SLOTS - 1, False)

        @block.tensor
        def _(pe):
            def turn(m, s, first):
                wait(pe, rows_done, m + 1, first)
                wait(pe, evac, m - 1, first)
                for a in range(ADA_GROUP):
                    last = pe.matmul(k.banks[4 + s % 2][:, a * N_SEQ:(a + 1) * N_SEQ],
                                     rows[:, s, a * P:(a + 1) * P], fold[:], start=True, stop=True)
                last.then_inc(turned, 1)

            def step(m, s, first):
                wait(pe, lo_ready, m + 1, first)
                wait(pe, rows_done, m - 3, first)
                out = k.banks[s][0:2 * N_SEQ, :]
                for kt in range(KT):
                    cols = slice(kt * ADA_GROUP * P, (kt + 1) * ADA_GROUP * P)
                    pe.matmul(out, c_parts[:, kt, :], w_hi[:, s % 2, cols], start=kt == 0, stop=False)
                    last = pe.matmul(out, c_parts[:, kt, :], w_lo[:, s % 2, cols], start=False, stop=kt == KT - 1)
                last.then_inc(used, 1)
                if not (first and s == 0):
                    turn(m - 1, (s - 1) % ADA_SLOTS, first)
                if first and s == ADA_SLOTS - 1:
                    for j in range(NC):
                        x_norm.pe(k, pe, j)
            pe.wait_ge(parts, 2)
            pe.wait_ge(constants, 3)
            run(step, pe)
            turn(GROUPS - 1, ADA_SLOTS - 1, False)

        @block.vector
        def _(dve):
            dve.memset(k.ones[:], 1.0).then_inc(constants, 1)
            dve.memset(k.eps[:], EPS).then_inc(constants, 1)
            dve.wait_ge(parts, 1)
            dve.tensor_tensor(c_parts[:, :, N_SEQ:], c_silu[:], c_parts[:, :, 0:N_SEQ], ALU.subtract).then_inc(parts, 1)
            dve.wait_ge(const_in, 48)
            dve.tensor_tensor(fold[:], k.ident[0:2 * N_SEQ, 0:N_SEQ], k.ident[0:2 * N_SEQ, N_SEQ:2 * N_SEQ], ALU.add)\
               .then_inc(constants, 1)
            flat, flat_bias = k.ada[:].rearrange("p l m s -> p (l m) s"), bias[:].rearrange("p l m -> p (l m)")

            def take(m, s, first):
                wait(dve, turned, m + 1, first)
                tiles = bass.ds(m * ADA_GROUP, ADA_GROUP)
                dve.tensor_tensor(flat[:, tiles, :],
                                  k.banks[4 + s % 2][:, 0:ADA_GROUP * N_SEQ].rearrange("p (m s) -> p m s", s=N_SEQ),
                                  flat_bias[:, tiles].unsqueeze(2).to_broadcast([P, ADA_GROUP, N_SEQ]), ALU.add)\
                   .then_inc(evac, 1)

            def step(m, s, first):
                wait(dve, hi_ready, m + 1, first)
                dve.tensor_tensor(w_lo[:, s % 2, :], w[:, s, :], w_hi[:, s % 2, :], ALU.subtract).then_inc(lo_ready, 1)
                if not (first and s < 2):
                    take(m - 2, (s - 2) % ADA_SLOTS, first)
                if first and s == ADA_SLOTS - 1:
                    for j in range(NC):
                        x_norm.dve(k, dve, j)
            run(step, dve)
            for m in (GROUPS - 2, GROUPS - 1):
                take(m, m % ADA_SLOTS, False)
            dve.wait_ge(evac, GROUPS)
            for l in range(2):
                for which, (first, one) in enumerate([(SCALE_MIX, 1.0), (GATE_MIX, 0.0),
                                                      (SCALE_FFN, 1.0), (GATE_FFN, 0.0)]):
                    part = k.ada[:, l, first:first + KT, :]
                    dve.scalar_tensor_tensor(part, part, one,
                                             gains[:, l, which, :].unsqueeze(2).to_broadcast([P, KT, N_SEQ]),
                                             ALU.add, ALU.mult).then_inc(folded, 1)
            dve.wait_ge(folded, 8)


def prompt_cols(c):
    t0, n = CHUNKS[c]
    return t0, min(n, SEQ - t0)


class Entry:

    def __init__(self, k, name, layer, scale, shift, scaled, scaled_s, split=True):
        self.split = split
        self.a = k.ada[:, layer, scale:scale + KT, :]
        self.s = k.ada[:, layer, shift:shift + KT, :]
        self.t, self.ts = scaled, scaled_s
        self.spread_done = k.sem(f"{name}_spread")
        self.scaled = k.sem(f"{name}_scaled")
        self.scaled_s = k.sem(f"{name}_scaled_s")
        self.hi = k.sem(f"{name}_hi")
        self.lo = k.sem(f"{name}_lo")

    def pe(self, k, pe, banks):
        for c in range(NC):
            spread(k, pe, c, k.rstd[:, 0, c, :], banks[c]).then_inc(self.spread_done, 1)

    def dve(self, k, dve, c, bank, h_hi, h_lo):
        t0, n = prompt_cols(c)
        dve.wait_ge(self.spread_done, c + 1)
        samples = c == NC - 1
        o = SEQ - CHUNKS[c][0]
        seqs = lambda ap: ap.rearrange("p k (s t) -> p k s t", t=DEC_S)
        by_seq = lambda ap: ap[:, :, 1:].unsqueeze(3).to_broadcast([P, KT, DEC_B, DEC_S])
        steps = {
            0: lambda: dve.tensor_tensor(self.ts[:], k.x[:, :, SEQ:NT],
                                         bank[:, o:o + NS].unsqueeze(1).to_broadcast([P, KT, NS]), ALU.mult),
            1: lambda: dve.tensor_tensor(seqs(self.ts[:]), seqs(self.ts[:]), by_seq(self.a), ALU.mult),
            2: lambda: dve.tensor_tensor(seqs(self.ts[:]), seqs(self.ts[:]), by_seq(self.s), ALU.add),
        }
        for kt in range(KT + 1):
            i = c * KT + kt
            if kt < KT:
                if i >= 2:
                    dve.wait_ge(self.hi, i - 1)
                    if self.split:
                        dve.wait_ge(self.lo, i - 1)
                dve.scalar_tensor_tensor(self.t[:, kt % 2, 0:n], k.x[:, kt, t0:t0 + n], self.a[:, kt, 0:1],
                                         bank[:, 0:n], ALU.mult, ALU.mult).then_inc(self.scaled, 1)
            if samples and kt in steps:
                if kt:
                    dve.wait_ge(self.scaled_s, kt)
                steps[kt]().then_inc(self.scaled_s, 1)
            if kt >= 1 and self.split:
                j = kt - 1
                dve.wait_ge(self.hi, i)
                dve.scalar_tensor_tensor(h_lo[:, j, t0:t0 + n], self.t[:, j % 2, 0:n], self.s[:, j, 0:1],
                                         h_hi[:, j, t0:t0 + n], ALU.add, ALU.subtract).then_inc(self.lo, 1)
        if samples and self.split:
            dve.wait_ge(self.hi, NC * KT + 1)
            dve.tensor_tensor(h_lo[:, :, SEQ:NT], self.ts[:], h_hi[:, :, SEQ:NT], ALU.subtract)\
               .then_inc(self.lo, 1)

    def act(self, k, act, c, put, put_s):
        t0, n = prompt_cols(c)
        for kt in range(KT):
            act.wait_ge(self.scaled, c * KT + kt + 1)
            act.activation(put(kt, t0, n), self.t[:, kt % 2, 0:n], ACT.Identity,
                           bias=self.s[:, kt, 0:1]).then_inc(self.hi, 1)
        if c == NC - 1:
            act.wait_ge(self.scaled_s, 3)
            act.activation(put_s, self.ts[:].rearrange("p k (s t) -> p k s t", t=DEC_S), ACT.Copy)\
               .then_inc(self.hi, 1)

    def ready(self, eng, c):
        eng.wait_ge(self.lo if self.split else self.hi, (c + 1) * KT + (c == NC - 1))


POOL_TILES = (2, 4, 6)


class Exit:

    def __init__(self, k, name, layer, gate, y, stats=True):
        self.y, self.stats = y, stats
        jobs = [(y, c, k.rstd[:, 1, c, :]) for c in range(NC)]
        if stats:
            jobs += [(k.x, c, k.rstd[:, 0, c, :]) for c in range(NC)]
        self.norm = Norm(k, name, jobs)
        self.b = k.ada[:, layer, gate:gate + KT, :]
        self.scaled = k.sem(f"{name}_scaled")
        self.scaled_s = k.sem(f"{name}_scaled_s")
        self.added_d = k.sem(f"{name}_added_d")
        self.added_p = k.sem(f"{name}_added_p")

    def added(self, eng, c, tiles):
        p = sum(kt in POOL_TILES for kt in range(tiles))
        eng.wait_ge(self.added_d, c * (KT - len(POOL_TILES)) + tiles - p + (c == NC - 1))
        if c or p:
            eng.wait_ge(self.added_p, c * len(POOL_TILES) + p)

    def dve(self, k, dve, banks):
        norm = self.norm
        norm.dve(k, dve, 0)
        for c in range(NC):
            if c + 1 < NC:
                norm.dve(k, dve, c + 1)
            self.apply(k, dve, c, banks[c])
            if c and self.stats:
                norm.dve(k, dve, NC + c - 1)
        if self.stats:
            norm.dve(k, dve, 2 * NC - 1)

    def apply(self, k, dve, c, bank):
        t0, n = prompt_cols(c)
        dve.wait_ge(self.norm.spread_done, c + 1)
        if c == NC - 1:
            o = SEQ - CHUNKS[c][0]
            seqs = lambda ap: ap.rearrange("p k (s t) -> p k s t", t=DEC_S)
            y, x = self.y[:, :, SEQ:NT], k.x[:, :, SEQ:NT]
            dve.tensor_tensor(y, y, bank[:, o:o + NS].unsqueeze(1).to_broadcast([P, KT, NS]), ALU.mult)\
               .then_inc(self.scaled_s, 1)
            dve.wait_ge(self.scaled_s, 1)
            dve.tensor_tensor(seqs(y), seqs(y), self.b[:, :, 1:].unsqueeze(3).to_broadcast([P, KT, DEC_B, DEC_S]),
                              ALU.mult).then_inc(self.scaled_s, 1)
            dve.wait_ge(self.scaled_s, 2)
            dve.tensor_tensor(x, x, y, ALU.add).then_inc(self.added_d, 1)
        for kt in range(KT + 1):
            if kt < KT:
                y = self.y[:, kt, t0:t0 + n]
                dve.scalar_tensor_tensor(y, y, self.b[:, kt, 0:1], bank[:, 0:n], ALU.mult, ALU.mult)\
                   .then_inc(self.scaled, 1)
            if kt and kt - 1 not in POOL_TILES:
                x = k.x[:, kt - 1, t0:t0 + n]
                dve.wait_ge(self.scaled, c * KT + kt)
                dve.tensor_tensor(x, x, self.y[:, kt - 1, t0:t0 + n], ALU.add).then_inc(self.added_d, 1)

    def pool(self, k, pool):
        for c in range(NC):
            t0, n = prompt_cols(c)
            for kt in POOL_TILES:
                pool.wait_ge(self.scaled, c * KT + kt + 1)
                x = k.x[:, kt, t0:t0 + n]
                pool.tensor_tensor(x, x, self.y[:, kt, t0:t0 + n], ALU.add).then_inc(self.added_p, 1)

    def act_x(self, k, act):
        if self.stats:
            for c in range(NC):
                self.norm.act(k, act, NC + c, lambda j, tiles: self.added(act, j - NC, tiles))

    def pe(self, k, pe, banks):
        for c in range(NC):
            self.norm.pe(k, pe, c)
            self.norm.pe_spread(k, pe, c, banks[c])
        if self.stats:
            for c in range(NC):
                self.norm.pe(k, pe, NC + c)


def put_in(h):
    return (lambda kt, t0, n: h[:, kt, t0:t0 + n],
            h[:, :, SEQ:NT].rearrange("p k (s t) -> p k s t", t=DEC_S))


HEADS, NOPE, ROPE, V_DIM = 16, 64, 32, 64
Q_LORA, KV_LORA = 512, 256
QT, LT = Q_LORA // P, KV_LORA // P
HP = HEADS // 2
QB = SEQ // P
PAGE, PAGES = 128, 8
PAST = PAGE * PAGES
N_POOL = 80
SCALE = float((NOPE + ROPE) ** -0.5)
NEG = -1e30
PAIR_W = 2 * QT * P + 2 * LT * P
CACHE_W = KV_LORA + LT * PAGE + PAGE



def mla_project_stage(k, m):
    nc, io = k.nc, k.io
    UNITS = LT + 1 + QT
    with ExitStack() as own:
        h_hi = k.sbuf(own, "mla_h_hi", [P, KT, NT], F32R)
        h_lo = k.sbuf(own, "mla_h_lo", [P, KT, NT], F32R)
        ktab = k.sbuf(own, "ktab", [P, NT])
        raw = [k.sbuf(own, f"proj_raw{s}", [P, D_MODEL]) for s in range(2)]
        w_hi = [k.sbuf(own, f"proj_w_hi{s}", [P, D_MODEL], F32R) for s in range(2)]
        w_lo = [k.sbuf(own, f"proj_w_lo{s}", [P, D_MODEL], F32R) for s in range(2)]
        work = k.sbuf(own, "proj_work", [P, 2304])
        scaled = k.sbuf(own, "proj_scaled", [P, 2, MAXC])
        scaled_s = k.sbuf(own, "proj_scaled_s", [P, KT, NS])
        gain = k.sbuf(own, "latent_gain", [P, LT + QT])
        k.norm_work(work)
        rot_tmp = work[:, 0:MAXC]
        cq = k.x[:, 0:QT, :]
        entry = Entry(k, "mla_in", 0, SCALE_MIX, SHIFT_MIX, scaled, scaled_s)
        kv_norm = Norm(k, "kv_norm", [(m.ckv[:], c, k.rstd[:, 1, c, :]) for c in range(NC)])
        q_norm = Norm(k, "q_norm", [(cq, c, k.rstd[:, 2, c, :]) for c in range(NC)])
        raw_in = [k.sem(f"proj_raw_in{s}") for s in range(2)]
        const_in = k.sem("proj_const_in")
        hi_ready, lo_ready = k.sem("proj_hi"), k.sem("proj_lo")
        done = k.sem("proj_done")
        evac_a, evac_d = k.sem("proj_evac_a"), k.sem("proj_evac_d")
        rot = k.sem("proj_rot")
        kv_scaled, q_scaled = k.sem("kv_scaled"), k.sem("q_scaled")
        cq_hi, cq_lo = k.sem("cq_hi_ready"), k.sem("cq_lo_ready")
        out = k.sem("latent_out")
        ROPE_UNIT = LT
        banks = [k.banks[0:3], k.banks[3:6]]
        kv_spread, q_spread = k.banks[7], banks[1]
        Q_LAST = UNITS - 1
        block = own.enter_context(nc.Block())

        @block.sync
        def _(sp):
            for j in range(UNITS):
                if j >= 2:
                    sp.wait_ge(lo_ready, j - 1)
                sp.dma_start(raw[j % 2][:], io["proj_w"][j]).then_inc(raw_in[j % 2], 16)
            sp.wait_ge(rot, 3 * NC + 1)
            sp.dma_start(io["kr_out"], m.kr[0:ROPE, :]).then_inc(out, 16)
            sp.wait_ge(kv_scaled, LT * NC)
            sp.dma_start(io["ckv_out"], m.ckv[:]).then_inc(out, 16)
            sp.wait_ge(out, 32)

        @block.scalar
        def _(act):
            act.dma_start(ktab[:], io["ktab"]).then_inc(const_in, 16)
            act.dma_start(gain[:], io["latent_gain"]).then_inc(const_in, 16)

            def split(j):
                act.wait_ge(raw_in[j % 2], 16 * (j // 2 + 1))
                if j >= 2:
                    act.wait_ge(done, NC * (j - 1))
                act.activation(w_hi[j % 2][:], raw[j % 2][:], ACT.Copy).then_inc(hi_ready, 1)
            split(0)
            for c in range(NC):
                entry.act(k, act, c, *put_in(h_hi))
            entry.ready(act, NC - 1)
            n = 0
            for j in range(UNITS):
                if j + 1 < UNITS:
                    split(j + 1)
                if j == ROPE_UNIT:
                    continue
                if j == ROPE_UNIT + 1:
                    act.wait_ge(evac_a, NC * LT)
                    act.wait_ge(rot, 3 * NC)
                dst = m.ckv[:, j] if j < LT else cq[:, j - LT - 1]
                for c, (t0, w) in enumerate(CHUNKS):
                    if j == ROPE_UNIT + 1:
                        kv_norm.act(k, act, c)
                    act.wait_ge(done, NC * j + c + 1)
                    act.activation(dst[:, t0:t0 + w], banks[j % 2][c][:, 0:w], ACT.Copy).then_inc(evac_a, 1)
                    if j == Q_LAST:
                        act.wait_ge(evac_a, NC * (UNITS - 2) + c + 1)
                        q_norm.act(k, act, c)

            def cq_hi_chunk(c):
                t0, w = CHUNKS[c]
                act.wait_ge(q_scaled, QT * (c + 1))
                act.activation(m.cq_hi[:, :, t0:t0 + w], cq[:, :, t0:t0 + w], ACT.Copy).then_inc(cq_hi, 1)
            for c in range(NC):
                cq_hi_chunk(c)

        @block.vector
        def _(dve):

            def split(j):
                dve.wait_ge(hi_ready, j + 1)
                dve.tensor_tensor(w_lo[j % 2][:], raw[j % 2][:], w_hi[j % 2][:], ALU.subtract).then_inc(lo_ready, 1)
            split(0)
            for c in range(NC):
                entry.dve(k, dve, c, banks[1][c], h_hi, h_lo)
            dve.wait_ge(const_in, 32)
            def kv_chunk(c):
                t0, w = CHUNKS[c]
                dve.wait_ge(kv_norm.spread_done, c + 1)
                for t in range(LT):
                    part = m.ckv[:, t, t0:t0 + w]
                    dve.scalar_tensor_tensor(part, part, gain[:, t:t + 1], kv_spread[:, 0:w], ALU.mult, ALU.mult)\
                       .then_inc(kv_scaled, 1)

            for j in range(UNITS):
                if j + 1 < UNITS:
                    split(j + 1)
                if j == ROPE_UNIT + 1:
                    kv_norm.dve(k, dve, 0)
                    for c in range(NC):
                        if c + 1 < NC:
                            kv_norm.dve(k, dve, c + 1)
                        kv_chunk(c)
                if j != ROPE_UNIT:
                    continue
                for c, (t0, w) in enumerate(CHUNKS):
                    bank = banks[j % 2][c]
                    cols = slice(t0, t0 + w)
                    dve.wait_ge(done, NC * j + c + 1)
                    if c:
                        dve.wait_ge(rot, 3 * c)
                    dve.tensor_tensor(rot_tmp[64:P, 0:w], bank[0:64, 0:w], ktab[0:64, cols], ALU.mult)\
                       .then_inc(rot, 1)
                    dve.tensor_tensor(m.kr[64:P, cols], bank[64:P, 0:w], ktab[64:P, cols], ALU.mult)\
                       .then_inc(rot, 1)
                    dve.wait_ge(rot, 3 * c + 2)
                    dve.tensor_tensor(m.kr[64:P, cols], m.kr[64:P, cols], rot_tmp[64:P, 0:w], ALU.add)\
                       .then_inc(rot, 1)
                dve.wait_ge(rot, 3 * NC)
                dve.tensor_copy(m.kr[0:64, :], m.kr[64:P, :]).then_inc(rot, 1)

            def q_chunk(c):
                t0, w = CHUNKS[c]
                dve.wait_ge(q_norm.spread_done, c + 1)
                for t in range(QT):
                    part = cq[:, t, t0:t0 + w]
                    dve.scalar_tensor_tensor(part, part, gain[:, LT + t:LT + t + 1], q_spread[c][:, 0:w],
                                             ALU.mult, ALU.mult).then_inc(q_scaled, 1)
                dve.wait_ge(cq_hi, c + 1)
                dve.tensor_tensor(m.cq_lo[:, :, t0:t0 + w], cq[:, :, t0:t0 + w], m.cq_hi[:, :, t0:t0 + w],
                                  ALU.subtract).then_inc(cq_lo, 1)
            q_norm.dve(k, dve, 0)
            for c in range(NC):
                if c + 1 < NC:
                    q_norm.dve(k, dve, c + 1)
                q_chunk(c)

        @block.tensor
        def _(pe):
            entry.pe(k, pe, banks[1])

            def kv_spread_chunk(c):
                if c:
                    pe.wait_ge(kv_scaled, LT * c)
                kv_norm.pe_spread(k, pe, c, kv_spread)
            first, second = ROPE_UNIT + 1, ROPE_UNIT + 2
            side = {
                (first, 0): lambda: kv_norm.pe_sum(k, pe, 0),
                (first, 1): lambda: (kv_norm.pe_turn(k, pe, 0), kv_norm.pe_sum(k, pe, 1)),
                (first, 2): lambda: (kv_norm.pe_turn(k, pe, 1), kv_norm.pe_sum(k, pe, 2), kv_spread_chunk(0)),
                (second, 0): lambda: (kv_norm.pe_turn(k, pe, 2), kv_spread_chunk(1)),
                (second, 1): lambda: kv_spread_chunk(2),
                (Q_LAST, 0): lambda: (pe.wait_ge(kv_norm.rstd, NC), q_norm.pe_sum(k, pe, 0)),
                (Q_LAST, 1): lambda: (q_norm.pe_turn(k, pe, 0), q_norm.pe_sum(k, pe, 1)),
                (Q_LAST, 2): lambda: (q_norm.pe_turn(k, pe, 1), q_norm.pe_sum(k, pe, 2),
                                      pe.wait_ge(evac_a, NC * (UNITS - 2)),
                                      q_norm.pe_spread(k, pe, 0, q_spread[0]), q_norm.pe_turn(k, pe, 2),
                                      q_norm.pe_spread(k, pe, 1, q_spread[1]), q_norm.pe_spread(k, pe, 2, q_spread[2])),
            }
            for j in range(UNITS):
                pe.wait_ge(lo_ready, j + 1)
                for c, (t0, w) in enumerate(CHUNKS):
                    if j == 0:
                        entry.ready(pe, c)
                    if j == 1 and c == 0:
                        entry.ready(pe, NC - 1)
                    if j >= 2:
                        if j - 2 == ROPE_UNIT:
                            pe.wait_ge(rot, 3 * c + 2)
                        else:
                            pe.wait_ge(evac_a, NC * (j - 2 - (j - 2 > ROPE_UNIT)) + c + 1)
                    for kt in range(KT):
                        o = slice(kt * P, kt * P + P)
                        bank = banks[j % 2][c][:, 0:w]
                        hh, hl = h_hi[:, kt, t0:t0 + w], h_lo[:, kt, t0:t0 + w]
                        pe.matmul(bank, w_hi[j % 2][:, o], hh, start=kt == 0, stop=False)
                        pe.matmul(bank, w_hi[j % 2][:, o], hl, start=False, stop=False)
                        last = pe.matmul(bank, w_lo[j % 2][:, o], hh, start=False, stop=kt == KT - 1)
                    last.then_inc(done, 1)
                    if (j, c) in side:
                        side[j, c]()


def mla_prompt_stage(k, m):
    nc, io = k.nc, k.io
    STEPS = 2 * QB
    with ExitStack() as own:
        raw = [k.sbuf(own, f"pair_raw{s}", [P, PAIR_W]) for s in range(2)]
        wq_hi = k.sbuf(own, "wq_hi", [P, 2 * QT * P], F32R)
        wq_lo = k.sbuf(own, "wq_lo", [P, 2 * QT * P], F32R)
        rot = k.sbuf(own, "rot", [P, 2, NT])
        mask = k.sbuf(own, "mask", [P, P])
        by_parity = lambda name, shape: [k.sbuf(own, f"{name}{s}", shape) for s in range(2)]
        q = by_parity("q", [P, 2, SEQ])
        keys = by_parity("keys", [P, 2, SEQ])
        vals = by_parity("vals", [P, QB, P])
        prob = by_parity("prob", [P, SEQ])
        prob_t = by_parity("prob_t", [P, SEQ])
        stats = k.sbuf(own, "softmax_stats", [P, 2, 3])
        scores = [k.psum[:, 0:2, :].rearrange("p b n -> p (b n)"), k.psum[:, 2:4, :].rearrange("p b n -> p (b n)")]
        turn_bank = k.psum[:, 4:6, :].rearrange("p b n -> p (b n)")
        o_bank, job_bank = k.banks[6], k.banks[7]
        const_in = k.sem("attn_const_in")
        raw_in = [k.sem(f"pair_raw_in{s}") for s in range(2)]
        wq_hi_ready, wq_lo_ready = k.sem("wq_hi_ready"), k.sem("wq_lo_ready")
        keys_init = k.sem("keys_init")
        job_done = k.sem("job_done")
        job_d, job_a = k.sem("job_d"), k.sem("job_a")
        samples_q = k.sem("samples_q")
        s_done, masked, max_done = k.sem("s_done"), k.sem("masked"), k.sem("max_done")
        exp_done, sum_inv, normed = k.sem("exp_done"), k.sem("sum_inv"), k.sem("normed")
        turned, turned_a, turned_d = k.sem("turned"), k.sem("turned_a"), k.sem("turned_d")
        o_done, o_out = k.sem("o_done"), k.sem("o_out")
        block = own.enter_context(nc.Block())

        Q_JOBS = [(hh, c) for hh in range(2) for c in range(NC)]
        JOBS = [("q", *x) for x in Q_JOBS] + [("k", 0), ("k", 1), ("v", 0), ("v", 1)]
        SLOT_OF_JOB = {2 + i: i for i in range(len(JOBS))}
        n_blocks = lambda n: n % QB + 1
        LATE = QB // 2

        @block.sync
        def _(sp):
            sp.dma_start(rot[:], io["rot"]).then_inc(const_in, 16)
            sp.dma_start(mask[:], io["mask"]).then_inc(const_in, 16)

            def load(i, s, wait):
                if wait:
                    sp.wait_ge(job_done, 10 * (i - 1))
                src = io["pair_w"][bass.ds(i, 1)].rearrange("a p n -> p (a n)")
                sp.dma_start(raw[s][:], src).then_inc(raw_in[s], 16)
            load(0, 0, False)
            load(1, 1, False)
            with sp.Fori(1, HP // 2) as j:
                load(2 * j, 0, True)
                load(2 * j + 1, 1, True)

        def job_counts(i, job):
            return (6 * i + min(job, 6), 4 * i + max(job - 6, 0))

        @block.scalar
        def _(act):
            act.wait_ge(const_in, 32)

            def split(i, s, n):
                act.wait_ge(raw_in[s], n)
                act.wait_ge(job_done, 10 * i)
                act.activation(wq_hi[:], raw[s][:, 0:2 * QT * P], ACT.Copy).then_inc(wq_hi_ready, 1)

            def job(i, j, s):
                if j < 6:
                    return
                kind, half = JOBS[j]
                act.wait_ge(job_done, 10 * i + j + 1)
                if kind == "k":
                    for hh in range(2):
                        r = slice(64 * hh, 64 * hh + 64)
                        last = act.activation(keys[s][r, hh, half * 512:(half + 1) * 512], job_bank[r, :], ACT.Copy)
                else:
                    last = act.activation(vals[s][:, half * 4:half * 4 + 4, :],
                                          job_bank.rearrange("p (j n) -> p j n", n=P), ACT.Copy)
                last.then_inc(job_a, 1)

            def exps(N, n, early=False):
                s, w = n % 2, n_blocks(n) * P
                act.wait_ge(max_done, N + 1)
                if not early:
                    act.wait_ge(turned, N - 1)
                    act.wait_ge(sum_inv, N - 1)
                act.activation(prob[s][:, 0:w], scores[s][:, 0:w], ACT.Exp, bias=stats[:, s, 0:1],
                               accum_out=stats[:, s, 1:2]).then_inc(exp_done, 1)

            def turned_part(N, n, early=False):
                s, w = n % 2, min(n_blocks(n), 4) * P
                act.wait_ge(turned, N + 1)
                if not early:
                    act.wait_ge(o_done, N - 1)
                act.activation(prob_t[s][:, 0:w], turn_bank[:, 0:w], ACT.Copy).then_inc(turned_a, 1)

            def pair(i, s, turn, first=False, last=False):
                for n in range(STEPS):
                    N = STEPS * i + n
                    if n == 0 and not last:
                        split(i + 1, 1 - s, turn)
                    if not (last and n == STEPS - 1):
                        exps(N + 1, (n + 1) % STEPS, first and n == 0)
                    if n in SLOT_OF_JOB and not last:
                        job(i + 1, SLOT_OF_JOB[n], 1 - s)
                    turned_part(N, n, first and n < 2)

            act.wait_ge(raw_in[0], 16)
            act.activation(wq_hi[:], raw[0][:, 0:2 * QT * P], ACT.Copy).then_inc(wq_hi_ready, 1)
            for j in range(len(JOBS)):
                job(0, j, 0)
            exps(0, 0, True)
            pair(0, 0, 16, first=True)
            with act.Fori(0, HP // 2 - 1) as j:
                pair(2 * j + 1, 1, 16 * j + 32)
                pair(2 * j + 2, 0, 16 * j + 32)
            pair(HP - 1, 1, None, last=True)

        @block.vector
        def _(dve):
            for s in range(2):
                dve.tensor_copy(keys[s][64:P, 0, :], m.kr[64:P, 0:SEQ])
                last = dve.tensor_copy(keys[s][0:64, 1, :], m.kr[0:64, 0:SEQ])
            last.then_inc(keys_init, 1)
            dve.wait_ge(const_in, 32)

            def split(i, s):
                dve.wait_ge(wq_hi_ready, i + 1)
                dve.tensor_tensor(wq_lo[:], raw[s][:, 0:2 * QT * P], wq_hi[:], ALU.subtract).then_inc(wq_lo_ready, 1)

            def job(i, j, s):
                if j >= 6:
                    return
                _, hh, c = JOBS[j]
                t0, w = prompt_cols(c)
                dve.wait_ge(job_done, 10 * i + j + 1)
                if c == NC - 1:
                    dve.tensor_tensor(m.qs[:, bass.ds(2 * i + hh, 1), :], job_bank[:, w:w + NS].unsqueeze(1),
                                      rot[:, hh, SEQ:NT].unsqueeze(1), ALU.mult).then_inc(samples_q, 1)
                dve.tensor_tensor(q[s][:, hh, t0:t0 + w], job_bank[:, 0:w], rot[:, hh, t0:t0 + w], ALU.mult)\
                   .then_inc(job_d, 1)

            def maxes(N, n, early=False):
                s, w = n % 2, n_blocks(n) * P
                diag = scores[s][:, w - P:w]
                dve.wait_ge(s_done, N + 1)
                dve.tensor_tensor(diag, diag, mask[:], ALU.add).then_inc(masked, 1)
                dve.wait_ge(masked, N + 1)
                if not early:
                    dve.wait_ge(exp_done, N - 1)
                dve.tensor_reduce(stats[:, s, 0:1], scores[s][:, 0:w], AX.X, ALU.max, negate=True)\
                   .then_inc(max_done, 1)

            def normalise(N, n, early=False):
                s, w = n % 2, n_blocks(n) * P
                if not early:
                    dve.wait_ge(normed, N - 1)
                dve.wait_ge(exp_done, N + 1)
                dve.reciprocal(stats[:, s, 2:3], stats[:, s, 1:2]).then_inc(sum_inv, 1)
                dve.wait_ge(sum_inv, N + 1)
                dve.tensor_scalar(prob[s][:, 0:w], prob[s][:, 0:w], stats[:, s, 2:3], None, ALU.mult)\
                   .then_inc(normed, 1)

            def turned_part(N, n, late, early=False):
                s, w = n % 2, n_blocks(n) * P
                if n_blocks(n) <= 4:
                    return
                dve.wait_ge(turned, N + 1)
                if not early:
                    dve.wait_ge(o_done, N - 1)
                dve.tensor_copy(prob_t[s][:, 512:w], turn_bank[:, 512:w]).then_inc(turned_d, 1)

            def attended(i, n):
                if n % 4 != 3:
                    return
                hh, half = n // QB, n % QB // 4
                r = slice(64 * hh, 64 * hh + 64)
                dve.wait_ge(o_done, STEPS * i + n + 1)
                dve.tensor_scalar(m.o[r, bass.ds(i, 1), half * 512:(half + 1) * 512],
                                  o_bank[r, :].unsqueeze(1), 1.0, None, ALU.mult).then_inc(o_out, 1)

            def pair(i, s, first=False, last=False):
                for n in range(STEPS):
                    N = STEPS * i + n
                    if n == 0 and not last:
                        split(i + 1, 1 - s)
                    if not (last and n == STEPS - 1):
                        maxes(N + 1, (n + 1) % STEPS, first and n == 0)
                    turned_part(N, n, None)
                    if not (last and n == STEPS - 1):
                        normalise(N + 1, (n + 1) % STEPS, first and n == 0)
                    if n in SLOT_OF_JOB and not last:
                        job(i + 1, SLOT_OF_JOB[n], 1 - s)
                    if n:
                        attended(i, n - 1)
                    elif not first:
                        attended(i - 1, STEPS - 1)

            split(0, 0)
            for j in range(len(JOBS)):
                job(0, j, 0)
            maxes(0, 0, True)
            normalise(0, 0, True)
            pair(0, 0, first=True)
            with dve.Fori(0, HP // 2 - 1) as j:
                pair(2 * j + 1, 1)
                pair(2 * j + 2, 0)
            pair(HP - 1, 1, last=True)
            attended(HP - 1, STEPS - 1)

        @block.tensor
        def _(pe):
            def job(i, j, s):
                d, a = job_counts(i, j)
                if j == 0:
                    pe.wait_ge(wq_lo_ready, i + 1)
                pe.wait_ge(job_a, a)
                pe.wait_ge(job_d, d)
                kind = JOBS[j][0]
                if kind == "q":
                    _, hh, c = JOBS[j]
                    t0, w = CHUNKS[c]
                    for t in range(QT):
                        o = slice((hh * QT + t) * P, (hh * QT + t + 1) * P)
                        ah, al = m.cq_hi[:, t, t0:t0 + w], m.cq_lo[:, t, t0:t0 + w]
                        pe.matmul(job_bank[:, 0:w], wq_hi[:, o], ah, start=t == 0, stop=False)
                        pe.matmul(job_bank[:, 0:w], wq_hi[:, o], al, start=False, stop=False)
                        last = pe.matmul(job_bank[:, 0:w], wq_lo[:, o], ah, start=False, stop=t == QT - 1)
                elif kind == "k":
                    half = JOBS[j][1]
                    for t in range(LT):
                        o = 2 * QT * P + t * P
                        last = pe.matmul(job_bank, raw[s][:, o:o + P], m.ckv[:, t, half * 512:(half + 1) * 512],
                                         start=t == 0, stop=t == LT - 1)
                else:
                    half = JOBS[j][1]
                    for b in range(4):
                        key = (half * 4 + b) * P
                        for t in range(LT):
                            o = (2 * QT + LT) * P + t * P
                            last = pe.matmul(job_bank[:, b * P:(b + 1) * P], m.ckv[:, t, key:key + P],
                                             raw[s][:, o:o + P], start=t == 0, stop=t == LT - 1)
                last.then_inc(job_done, 1)

            def score(N, i, n, s, early=False):
                hh, b = divmod(n, QB)
                out = scores[n % 2]
                if n == 0:
                    d, a = job_counts(i + 1, 0)
                    pe.wait_ge(job_a, a)
                    pe.wait_ge(job_d, d)
                if not early:
                    pe.wait_ge(exp_done, N - 1)
                w = n_blocks(n) * P
                for o in range(0, w, 512):
                    e = min(o + 512, w)
                    last = pe.matmul(out[:, o:e], q[s][:, hh, b * P:(b + 1) * P], keys[s][:, hh, o:e],
                                     start=True, stop=True)
                last.then_inc(s_done, 1)

            def turn(N, n, late):
                s = n % 2
                pe.wait_ge(normed, N + 1)
                if not (type(N) is int and N == 0):
                    pe.wait_ge(turned_a, N)
                if late is not None:
                    pe.wait_ge(turned_d, late)
                for b in range(n_blocks(n)):
                    last = pe.transpose(turn_bank[:, b * P:(b + 1) * P], prob[s][:, b * P:(b + 1) * P], k.ident[:])
                last.then_inc(turned, 1)

            def late_before(i, n):
                return 2 * LATE * i + sum(n_blocks(x) > 4 for x in range(n))

            def values(N, i, n, s):
                hh, b = divmod(n, QB)
                r = slice(64 * hh, 64 * hh + 64)
                pe.wait_ge(turned_a, N + 1)
                if n_blocks(n) > 4:
                    pe.wait_ge(turned_d, late_before(i, n) + 1)
                if n % 4 == 0 and not (type(i) is int and i == 0 and n == 0):
                    pe.wait_ge(o_out, 4 * i + n // 4)
                for kb in range(n_blocks(n)):
                    last = pe.matmul(o_bank[r, b % 4 * P:(b % 4 + 1) * P], vals[s][:, kb, r],
                                     prob_t[n % 2][:, kb * P:(kb + 1) * P], start=kb == 0, stop=kb == n_blocks(n) - 1)
                last.then_inc(o_done, 1)

            def pair(i, s, first=False, last=False):
                for n in range(STEPS):
                    N = STEPS * i + n
                    if n < STEPS - 1:
                        score(N + 1, i, n + 1, s, first and n == 0)
                    elif not last:
                        score(N + 1, i + 1, 0, 1 - s)
                    if n in SLOT_OF_JOB and not last:
                        job(i + 1, SLOT_OF_JOB[n], 1 - s)
                    late = late_before(i, n)
                    turn(N, n, None if type(late) is int and late == 0 else late)
                    if n:
                        values(N - 1, i, n - 1, s)
                    elif not first:
                        values(N - 1, i - 1, STEPS - 1, 1 - s)

            pe.wait_ge(keys_init, 1)
            for j in range(len(JOBS)):
                job(0, j, 0)
            score(0, 0, 0, 0, True)
            pair(0, 0, first=True)
            with pe.Fori(0, HP // 2 - 1) as j:
                pair(2 * j + 1, 1)
                pair(2 * j + 2, 0)
            pair(HP - 1, 1, last=True)
            values(STEPS * HP - 1, HP - 1, STEPS - 1, 1)


def mla_sample_stage(k, m):
    nc, io = k.nc, k.io
    KEYS = PAST + NS
    with ExitStack() as own:
        wuk = k.sbuf(own, "wuk", [P, HP, KV_LORA])
        wuv = k.sbuf(own, "wuv", [P, LT, HEADS * V_DIM])
        q_lat = k.sbuf(own, "q_lat", [P, LT, DEC_B, P])
        q_rot = k.sbuf(own, "q_rot", [P, DEC_B, P])
        cur = [k.sbuf(own, f"cur{s}", [P, LT + 1, P]) for s in range(2)]
        cache = [k.sbuf(own, f"cache{s}", [P, PAGES, CACHE_W]) for s in range(2)]
        new_rows = k.sbuf(own, "new_rows", [NS, KV_LORA])
        prob = [k.sbuf(own, f"sprob{s}", [P, KEYS]) for s in range(2)]
        prob_t = [k.sbuf(own, f"sprob_t{s}", [P, (PAGES + 1) * P]) for s in range(2)]
        stats = k.sbuf(own, "sstats", [P, 2, 3])
        o_lat = k.sbuf(own, "o_lat", [P, KV_LORA])
        o_lat_t = k.sbuf(own, "o_lat_t", [P, LT, HEADS, NS])
        smask = k.sbuf(own, "smask", [P, DEC_B, NS])
        table = k.sbuf(own, "page_table", [1, DEC_B * PAGES], I32)
        flat = lambda a, b: k.psum[:, a:b, :].rearrange("p b n -> p (b n)")
        scores, turn_bank, o_bank, ot_bank = flat(0, 3), flat(3, 6), k.banks[6], k.banks[7]
        const_in, table_in = k.sem("s_const_in"), k.sem("table_in")
        cache_in = [k.sem(f"cache_in{s}") for s in range(2)]
        ql_done, ql_out = k.sem("ql_done"), k.sem("ql_out")
        zeroed, rot_set = k.sem("q_rot_zeroed"), k.sem("q_rot_set")
        new_done, new_out = k.sem("new_done"), k.sem("new_out")
        cur_set = k.sem("cur_set")
        s_done, masked, max_done = k.sem("ss_done"), k.sem("smasked"), k.sem("smax_done")
        exp_done, sum_inv, normed = k.sem("sexp_done"), k.sem("ssum_inv"), k.sem("snormed")
        turned, turned_a, turned_d = k.sem("sturned"), k.sem("sturned_a"), k.sem("sturned_d")
        o_done, o_out, ot_done, ot_out = k.sem("so_done"), k.sem("so_out"), k.sem("ot_done"), k.sem("ot_out")
        final, final_out = k.sem("s_final"), k.sem("s_final_out")
        block = own.enter_context(nc.Block())

        @block.sync
        def _(sp):
            sp.dma_start(table[:], io["page_table"]).then_inc(table_in, 16)
            sp.wait_ge(table_in, 16)

            pool_rows = io["cache"].rearrange("g p n -> (g p n)")
            size = P * CACHE_W

            def load(b, s, wait):
                at = [sp.snap(sp.value_load(table[0:1, bass.ds(b * PAGES + j, 1)], min_val=0, max_val=N_POOL - 1)
                              * size) for j in range(PAGES)]
                if wait:
                    sp.wait_ge(o_done, b - 1)
                for j in range(PAGES):
                    sp.dma_start(cache[s][:, j, :], pool_rows[bass.ds(at[j], size)].rearrange("(p n) -> p n", p=P))\
                      .then_inc(cache_in[s], 16)
            load(0, 0, False)
            load(1, 1, False)
            with sp.Fori(1, DEC_B // 2) as i:
                load(2 * i, 0, True)
                load(2 * i + 1, 1, True)

        @block.scalar
        def _(act):
            act.dma_start(wuk[:], io["wuk"]).then_inc(const_in, 16)
            act.dma_start(wuv[:], io["wuv"]).then_inc(const_in, 16)
            act.dma_start(smask[:], io["smask"]).then_inc(const_in, 16)
            act.wait_ge(ql_done, 1)
            for hh in range(2):
                for t in range(LT):
                    dst = q_lat[:, t].rearrange("p s (a h t) -> p s a h t", h=2, t=DEC_S)[:, :, :, hh, :]
                    src = k.banks[2 * hh + t].rearrange("p (a s t) -> p s a t", s=DEC_B, t=DEC_S)
                    act.activation(dst, src, ACT.Copy).then_inc(ql_out, 1)
            act.wait_ge(new_done, 1)
            act.activation(new_rows[:], ot_bank[0:NS, 0:KV_LORA], ACT.Copy).then_inc(new_out, 1)
            act.wait_ge(const_in, 48)

            def step(b, s, early, edge):
                act.wait_ge(max_done, b + 1)
                if not early:
                    act.wait_ge(turned, b - 1)
                    act.wait_ge(sum_inv, b - 1)
                act.activation(prob[s][:], scores[:, 0:KEYS], ACT.Exp, bias=stats[:, s, 0:1],
                               accum_out=stats[:, s, 1:2]).then_inc(exp_done, 1)
                act.wait_ge(turned, b + 1)
                if not early:
                    act.wait_ge(o_done, b - 1)
                act.activation(prob_t[s][:, 0:512], turn_bank[:, 0:512], ACT.Copy)
                act.activation(prob_t[s][0:NS, PAST:PAST + P], turn_bank[0:NS, PAST:PAST + P], ACT.Copy)\
                   .then_inc(turned_a, 1)
                act.wait_ge(o_done, b + 1)
                if edge is not True:
                    act.wait_ge(ot_done, b)
                act.activation(o_lat[:], o_bank[:, 0:KV_LORA], ACT.Copy).then_inc(o_out, 1)

            step(0, 0, True, True)
            step(1, 1, True, False)
            with act.Fori(1, DEC_B // 2) as i:
                step(2 * i, 0, False, False)
                step(2 * i + 1, 1, False, False)

        @block.vector
        def _(dve):
            dve.memset(q_rot[:], 0.0).then_inc(zeroed, 1)
            dve.wait_ge(zeroed, 1)
            for hh, r in ((0, slice(64, P)), (1, slice(0, 64))):
                src = m.qs[r].rearrange("p (a h) (s t) -> p s a h t", h=2, t=DEC_S)[:, :, :, hh, :]
                dst = q_rot[r].rearrange("p s (a h t) -> p s a h t", h=2, t=DEC_S)[:, :, :, hh, :]
                last = dve.tensor_copy(dst, src)
            last.then_inc(rot_set, 1)
            dve.wait_ge(rot_set, 1)
            dve.wait_ge(ql_out, 4)
            dve.wait_ge(const_in, 48)

            def set_cur(b, s, early=False):
                if not early:
                    dve.wait_ge(s_done, b - 1)
                for t in range(LT):
                    dve.tensor_scalar(cur[s][:, t:t + 1, :], q_lat[:, t, bass.ds(b, 1), :], 1.0, None, ALU.mult)
                dve.tensor_scalar(cur[s][:, LT:LT + 1, :], q_rot[:, bass.ds(b, 1), :], 1.0, None, ALU.mult)\
                   .then_inc(cur_set, 1)

            def soft(b, s, early=False):
                new = scores[:, PAST:KEYS].unsqueeze(1)
                dve.wait_ge(s_done, b + 1)
                dve.tensor_tensor(new, new, smask[:, bass.ds(b, 1), :], ALU.add).then_inc(masked, 1)
                dve.wait_ge(masked, b + 1)
                if not early:
                    dve.wait_ge(exp_done, b - 1)
                dve.tensor_reduce(stats[:, s, 0:1], scores[:, 0:KEYS], AX.X, ALU.max, negate=True)\
                   .then_inc(max_done, 1)
                if not early:
                    dve.wait_ge(normed, b - 1)
                dve.wait_ge(exp_done, b + 1)
                dve.reciprocal(stats[:, s, 2:3], stats[:, s, 1:2]).then_inc(sum_inv, 1)
                dve.wait_ge(sum_inv, b + 1)
                dve.tensor_scalar(prob[s][:], prob[s][:], stats[:, s, 2:3], None, ALU.mult).then_inc(normed, 1)

            def rest(b, s, early=False):
                dve.wait_ge(turned, b + 1)
                if not early:
                    dve.wait_ge(o_done, b - 1)
                dve.tensor_copy(prob_t[s][:, 512:PAST], turn_bank[:, 512:PAST]).then_inc(turned_d, 1)
                dve.wait_ge(ot_done, b + 1)
                for t in range(LT):
                    dst = o_lat_t[:, t].rearrange("p h (s t) -> p h s t", t=DEC_S)[:, :, bass.ds(b, 1), :]
                    src = ot_bank[:, t * P:(t + 1) * P].rearrange("p (h a t) -> p h a t", a=1, t=DEC_S)
                    last = dve.tensor_scalar(dst, src, 1.0, None, ALU.mult)
                last.then_inc(ot_out, 1)

            def step(b, s, early=False, last=False):
                if not last:
                    set_cur(b + 1, 1 - s, early and s == 0)
                soft(b, s, early)
                rest(b, s, early)

            set_cur(0, 0, True)
            step(0, 0, True)
            step(1, 1, True)
            with dve.Fori(1, DEC_B // 2 - 1) as i:
                step(2 * i, 0)
                step(2 * i + 1, 1)
            step(DEC_B - 2, 0)
            step(DEC_B - 1, 1, last=True)
            dve.wait_ge(final, 1)
            dve.tensor_copy(m.o[:, :, SEQ:NT], o_bank.rearrange("p (a n) -> p a n", n=NS)).then_inc(final_out, 1)

        @block.tensor
        def _(pe):
            pe.wait_ge(const_in, 48)
            for hh in range(2):
                r = slice(64 * hh, 64 * hh + 64)
                for t in range(LT):
                    for a in range(HP):
                        last = pe.matmul(k.banks[2 * hh + t][:, a * NS:(a + 1) * NS], wuk[r, a, t * P:(t + 1) * P],
                                         m.qs[r, 2 * a + hh, :], start=True, stop=True)
            last.then_inc(ql_done, 1)
            for t in range(LT):
                last = pe.transpose(ot_bank[0:NS, t * P:(t + 1) * P], m.ckv[:, t, SEQ:NT], k.ident[:])
            last.then_inc(new_done, 1)
            pe.wait_ge(ql_out, 4)
            pe.wait_ge(new_out, 1)

            def score(b, s, turn, early=False):
                pe.wait_ge(cur_set, b + 1)
                pe.wait_ge(cache_in[s], turn)
                if not early:
                    pe.wait_ge(exp_done, b)
                for half in range(2):
                    pages = slice(half * 4, half * 4 + 4)
                    for t in range(LT + 1):
                        o = KV_LORA + t * PAGE
                        pe.matmul(scores[:, half * 512:(half + 1) * 512], cur[s][:, t, :],
                                  cache[s][:, pages, o:o + PAGE], start=t == 0, stop=t == LT)
                new = scores[:, PAST:KEYS]
                for t in range(LT):
                    pe.matmul(new, cur[s][:, t, :], m.ckv[:, t, SEQ:NT], start=t == 0, stop=False)
                pe.matmul(new, cur[s][:, LT, :], m.kr[:, SEQ:NT], start=False, stop=True).then_inc(s_done, 1)

            def turn_(b, s, early=False):
                pe.wait_ge(normed, b + 1)
                if not early:
                    pe.wait_ge(turned_a, b)
                    pe.wait_ge(turned_d, b)
                for j in range(PAGES):
                    pe.transpose(turn_bank[:, j * P:(j + 1) * P], prob[s][:, j * P:(j + 1) * P], k.ident[:])
                pe.transpose(turn_bank[0:NS, PAST:PAST + P], prob[s][:, PAST:KEYS], k.ident[:]).then_inc(turned, 1)

            def values(b, s, early=False):
                pe.wait_ge(turned_a, b + 1)
                pe.wait_ge(turned_d, b + 1)
                if not early:
                    pe.wait_ge(o_out, b)
                out = o_bank[:, 0:KV_LORA]
                for j in range(PAGES):
                    pe.matmul(out, prob_t[s][:, j * P:(j + 1) * P], cache[s][:, j, 0:KV_LORA],
                              start=j == 0, stop=False)
                pe.matmul(out, prob_t[s][0:NS, PAST:PAST + P], new_rows[:], start=False, stop=True)\
                  .then_inc(o_done, 1)
                pe.wait_ge(o_out, b + 1)
                if not early:
                    pe.wait_ge(ot_out, b)
                for t in range(LT):
                    last = pe.transpose(ot_bank[:, t * P:(t + 1) * P], o_lat[:, t * P:(t + 1) * P], k.ident[:])
                last.then_inc(ot_done, 1)

            def step(b, s, turn, early=False, last=False):
                if not last:
                    score(b + 1, 1 - s, turn)
                turn_(b, s, early)
                values(b, s, early)

            ALL = 16 * PAGES
            score(0, 0, ALL, True)
            step(0, 0, ALL, True)
            step(1, 1, 2 * ALL)
            with pe.Fori(1, DEC_B // 2 - 1) as i:
                step(2 * i, 0, ALL * i + ALL)
                step(2 * i + 1, 1, ALL * i + 2 * ALL)
            step(DEC_B - 2, 0, ALL * DEC_B // 2)
            step(DEC_B - 1, 1, None, last=True)
            pe.wait_ge(ot_out, DEC_B)
            for h in range(HEADS):
                a, hh = divmod(h, 2)
                for t in range(LT):
                    last = pe.matmul(o_bank[64 * hh:64 * hh + 64, a * NS:(a + 1) * NS],
                                     wuv[:, t, h * V_DIM:(h + 1) * V_DIM], o_lat_t[:, t, h, :],
                                     start=t == 0, stop=t == LT - 1)
            last.then_inc(final, 1)


def mla_out_stage(k, m):
    nc, io = k.nc, k.io
    with ExitStack() as own:
        o_hi = k.sbuf(own, "o_hi", [P, KT, NT], F32R)
        o_lo = k.sbuf(own, "o_lo", [P, KT, NT], F32R)
        y = k.sbuf(own, "mla_y", [P, KT, NT])
        raw = [k.sbuf(own, f"wo_raw{s}", [P, D_MODEL]) for s in range(2)]
        w_hi = [k.sbuf(own, f"wo_hi{s}", [P, D_MODEL], F32R) for s in range(2)]
        w_lo = [k.sbuf(own, f"wo_lo{s}", [P, D_MODEL], F32R) for s in range(2)]
        work = k.sbuf(own, "wo_work", [P, 2304])
        k.norm_work(work)
        exit_ = Exit(k, "mla_out", 0, GATE_MIX, y)
        raw_in = [k.sem(f"wo_raw_in{s}") for s in range(2)]
        hi_ready, lo_ready = k.sem("wo_hi_ready"), k.sem("wo_lo_ready")
        o_hi_ready, o_lo_ready = k.sem("o_hi_ready"), k.sem("o_lo_ready")
        x_in, done, evac = k.sem("x_back"), k.sem("wo_done"), k.sem("wo_evac")
        banks = [k.banks[0:3], k.banks[3:6]]
        block = own.enter_context(nc.Block())

        @block.sync
        def _(sp):
            for j in range(KT):
                if j >= 2:
                    sp.wait_ge(lo_ready, j - 1)
                sp.dma_start(raw[j % 2][:], io["wo"][j]).then_inc(raw_in[j % 2], 16)
                if j == 1:
                    sp.wait_ge(o_lo_ready, KT)
                    sp.dma_start(k.x[:], io["x"]).then_inc(x_in, 16)
            sp.wait_ge(x_in, 16)

        @block.scalar
        def _(act):
            def split(j):
                act.wait_ge(raw_in[j % 2], 16 * (j // 2 + 1))
                if j >= 2:
                    act.wait_ge(done, NC * (j - 1))
                act.activation(w_hi[j % 2][:], raw[j % 2][:], ACT.Copy).then_inc(hi_ready, 1)
            for t in range(KT):
                act.activation(o_hi[:, t], m.o[:, t], ACT.Copy).then_inc(o_hi_ready, 1)
                if t == 0:
                    split(0)
            for j in range(KT):
                if j + 1 < KT:
                    split(j + 1)
                for c, (t0, w) in enumerate(CHUNKS):
                    act.wait_ge(done, NC * j + c + 1)
                    act.activation(y[:, j, t0:t0 + w], banks[j % 2][c][:, 0:w], ACT.Copy).then_inc(evac, 1)
                    if j == KT - 1:
                        act.wait_ge(evac, NC * j + c + 1)
                        exit_.norm.act(k, act, c)
            exit_.act_x(k, act)

        @block.vector
        def _(dve):
            def split(j):
                dve.wait_ge(hi_ready, j + 1)
                dve.tensor_tensor(w_lo[j % 2][:], raw[j % 2][:], w_hi[j % 2][:], ALU.subtract).then_inc(lo_ready, 1)
            for t in range(KT):
                dve.wait_ge(o_hi_ready, t + 1)
                dve.tensor_tensor(o_lo[:, t], m.o[:, t], o_hi[:, t], ALU.subtract).then_inc(o_lo_ready, 1)
                if t == 0:
                    split(0)
            for j in range(1, KT):
                split(j)
            dve.wait_ge(x_in, 16)
            exit_.dve(k, dve, banks[0])

        @block.gpsimd
        def _(pool):
            pool.wait_ge(x_in, 16)
            exit_.pool(k, pool)

        @block.tensor
        def _(pe):
            for j in range(KT):
                pe.wait_ge(lo_ready, j + 1)
                for c, (t0, w) in enumerate(CHUNKS):
                    if j >= 2:
                        pe.wait_ge(evac, NC * (j - 2) + c + 1)
                    bank = banks[j % 2][c][:, 0:w]
                    for t in range(KT):
                        if j == 0 and c == 0:
                            pe.wait_ge(o_lo_ready, t + 1)
                        o = slice(t * P, t * P + P)
                        oh, ol = o_hi[:, t, t0:t0 + w], o_lo[:, t, t0:t0 + w]
                        pe.matmul(bank, w_hi[j % 2][:, o], oh, start=t == 0, stop=False)
                        pe.matmul(bank, w_hi[j % 2][:, o], ol, start=False, stop=False)
                        last = pe.matmul(bank, w_lo[j % 2][:, o], oh, start=False, stop=t == KT - 1)
                    last.then_inc(done, 1)
            exit_.pe(k, pe, banks[0])


class Latents:

    def __init__(self, k, ctx):
        self.o = k.x
        self.ckv = k.sbuf(ctx, "ckv", [P, LT, NT])
        self.kr = k.sbuf(ctx, "kr", [P, NT])
        self.qs = k.sbuf(ctx, "qs", [P, HEADS, NS])


def mla(k):
    with ExitStack() as own:
        m = Latents(k, own)
        with ExitStack() as latent:
            m.cq_hi = k.sbuf(latent, "cq_hi", [P, QT, NT], F32R)
            m.cq_lo = k.sbuf(latent, "cq_lo", [P, QT, NT], F32R)
            mla_project_stage(k, m)
            k.stage_done()
            mla_prompt_stage(k, m)
            k.stage_done()
        mla_sample_stage(k, m)
        k.stage_done()
        mla_out_stage(k, m)
        k.stage_done()


WINDOWS = (2, 4, 8, 16)
BUF = max(WINDOWS) - 1
GT = KT // len(WINDOWS)
SW = BUF + DEC_S


def pool_stage(k):
    nc, io = k.nc, k.io
    with ExitStack() as own:
        hp = k.sbuf(own, "pool_h", [P, KT, BUF + SEQ])
        hs = k.sbuf(own, "pool_hs", [P, KT, DEC_B, SW])
        sums = [k.sbuf(own, f"pool_sum{s}", [P, BUF + SEQ]) for s in range(2)]
        sums_s = [k.sbuf(own, f"pool_sum_s{s}", [P, KT, DEC_B, SW]) for s in range(2)]
        pooled = k.sbuf(own, "pooled", [P, KT, NT])
        y = k.sbuf(own, "pool_y", [P, KT, NT])
        w = k.sbuf(own, "pool_w", [P, KT, GT * P])
        ls = k.sbuf(own, "pool_scale", [P, KT])
        head = k.sbuf(own, "pool_head", [P, len(WINDOWS), BUF])
        last_rows = k.sbuf(own, "pool_last", [P, KT, N_SEQ, BUF])
        work = k.sbuf(own, "pool_work", [P, 2304])
        k.norm_work(work)
        entry = Entry(k, "pool_in", 1, SCALE_MIX, SHIFT_MIX,
                      sums[0][:, 0:2 * MAXC].rearrange("p (b t) -> p b t", b=2),
                      sums[1][:, 0:KT * NS].rearrange("p (k t) -> p k t", k=KT), split=False)
        exit_ = Exit(k, "pool_out", 1, GATE_MIX, y)
        const_in, zeroed = k.sem("pool_const_in"), k.sem("pool_zeroed")
        step = k.sem("pool_step")
        pooled_done = k.sem("pooled_done")
        kept, out = k.sem("pool_kept"), k.sem("pool_state_out")
        done, evac = k.sem("pool_done"), k.sem("pool_evac")
        block = own.enter_context(nc.Block())

        @block.sync
        def _(sp):
            sp.dma_start(w[:], io["pool_w"]).then_inc(const_in, 16)
            sp.dma_start(ls[:], io["pool_scale"]).then_inc(const_in, 16)
            sp.dma_start(head[:], io["pool_head"]).then_inc(const_in, 16)
            sp.dma_start(last_rows[:, :, 1:, :], io["pool_state"]).then_inc(const_in, 16)
            sp.wait_ge(kept, 2)
            sp.dma_start(io["pool_out"], last_rows[:]).then_inc(out, 16)
            sp.wait_ge(out, 16)

        @block.gpsimd
        def _(pool):
            pool.memset(hp[:, :, 0:BUF], 0.0).then_inc(zeroed, 1)
            pool.wait_ge(const_in, 64)
            pool.tensor_copy(hs[:, :, :, 0:BUF], last_rows[:, :, 1:, :]).then_inc(zeroed, 1)
            pool.wait_ge(zeroed, 2)
            entry.ready(pool, NC - 1)
            pool.tensor_copy(last_rows[:, :, 0, :], hp[:, :, SEQ:SEQ + BUF]).then_inc(kept, 1)
            pool.tensor_copy(last_rows[:, :, 1:, :], hs[:, :, :, DEC_S:SW]).then_inc(kept, 1)
            exit_.pool(k, pool)

        @block.scalar
        def _(act):
            for c in range(NC):
                entry.act(k, act, c, lambda kt, t0, n: hp[:, kt, BUF + t0:BUF + t0 + n], hs[:, :, :, BUF:])
            act.wait_ge(const_in, 64)
            for kt in range(KT):
                for c, (t0, n) in enumerate(CHUNKS):
                    act.wait_ge(done, NC * kt + c + 1)
                    act.activation(y[:, kt, t0:t0 + n], k.banks[(NC * kt + c) % 6][:, 0:n], ACT.Copy,
                                   scale=ls[:, kt:kt + 1]).then_inc(evac, 1)
            for c in range(NC):
                act.wait_ge(evac, NC * KT)
                exit_.norm.act(k, act, c)
            exit_.act_x(k, act)

        @block.vector
        def _(dve):
            for c in range(NC):
                entry.dve(k, dve, c, k.banks[3 + c], None, None)
            dve.wait_ge(const_in, 64)
            dve.wait_ge(zeroed, 2)
            entry.ready(dve, NC - 1)
            n = [0]

            def do(ins):
                n[0] += 1
                ins.then_inc(step, 1)
                dve.wait_ge(step, n[0])

            W = BUF + SEQ
            for g, window in enumerate(WINDOWS):
                for kt in range(g * GT, (g + 1) * GT):
                    src, lo, span = hp[:, kt], 0, 1
                    while span < window:
                        dst = sums[(span.bit_length() - 1) % 2]
                        do(dve.tensor_tensor(dst[:, lo + span:W], src[:, lo + span:W], src[:, lo:W - span], ALU.add))
                        src, lo, span = dst, lo + span, 2 * span
                    do(dve.scalar_tensor_tensor(pooled[:, kt, 0:SEQ], src[:, BUF:W], 1.0 / window, hp[:, kt, BUF:W],
                                                ALU.mult, ALU.subtract))
                    do(dve.tensor_tensor(src[:, 0:BUF], src[:, BUF:2 * BUF], head[:, g], ALU.mult))
                    dve.tensor_tensor(pooled[:, kt, 0:BUF], src[:, 0:BUF], hp[:, kt, BUF:2 * BUF], ALU.subtract)\
                       .then_inc(pooled_done, 1)
                    dve.wait_ge(pooled_done, kt + 1)
            src, span = hs, 1
            for g, window in enumerate(WINDOWS):
                while span < window:
                    dst = sums_s[(span.bit_length() - 1) % 2]
                    first = g * GT
                    for kt in range(first, KT):
                        last = dve.tensor_tensor(dst[:, kt, :, 2 * span - 1:], src[:, kt, :, 2 * span - 1:],
                                                 src[:, kt, :, span - 1:SW - span], ALU.add)
                        do(last)
                    src, span = dst, 2 * span
                for kt in range(g * GT, (g + 1) * GT):
                    do(dve.scalar_tensor_tensor(pooled[:, kt, SEQ:NT].rearrange("p (s t) -> p s t", t=DEC_S),
                                                src[:, kt, :, BUF:], 1.0 / window, hs[:, kt, :, BUF:],
                                                ALU.mult, ALU.subtract))
            dve.memset(work[:, 0:1], 0.0).then_inc(pooled_done, 1)
            exit_.dve(k, dve, k.banks[0:3])

        @block.tensor
        def _(pe):
            entry.pe(k, pe, k.banks[3:6])
            pe.wait_ge(const_in, 64)
            pe.wait_ge(pooled_done, KT + 1)
            for kt in range(KT):
                g, mo = divmod(kt, GT)
                for c, (t0, n) in enumerate(CHUNKS):
                    i = NC * kt + c
                    if i >= 6:
                        pe.wait_ge(evac, i - 5)
                    for t in range(GT):
                        last = pe.matmul(k.banks[i % 6][:, 0:n], w[:, g * GT + t, mo * P:(mo + 1) * P],
                                         pooled[:, g * GT + t, t0:t0 + n], start=t == 0, stop=t == GT - 1)
                    last.then_inc(done, 1)
            pe.wait_ge(evac, NC * KT)
            exit_.pe(k, pe, k.banks[0:3])


G, U, D = range(3)


def ffn_stage(k, layer):
    nc, io = k.nc, k.io
    n = f"ffn{layer}_"
    with ExitStack() as own:
        h_hi = k.sbuf(own, n + "h_hi", [P, KT, NT], F32R)
        h_lo = k.sbuf(own, n + "h_lo", [P, KT, NT], F32R)
        y = k.sbuf(own, n + "y", [P, KT, NT])
        raw = [k.sbuf(own, f"{n}raw{s}", [P, D_MODEL]) for s in range(3)]
        w_hi = [k.sbuf(own, f"{n}w_hi{s}", [P, D_MODEL], F32R) for s in range(3)]
        w_lo = [k.sbuf(own, f"{n}w_lo{s}", [P, D_MODEL], F32R) for s in range(3)]
        PROMPT_W = SEQ + CONV_W - 1
        SAMPLE_W = DEC_S + CONV_W - 1
        u = [k.sbuf(own, f"{n}u{s}", [P, PROMPT_W + DEC_B * SAMPLE_W]) for s in range(2)]
        work = k.sbuf(own, n + "work", [P, 2304])
        conv = [work[:, 0:NT], work[:, NT:2 * NT]]
        g_hi = k.sbuf(own, n + "g_hi", [P, NT], F32R)
        g_lo = k.sbuf(own, n + "g_lo", [P, NT], F32R)
        taps = k.sbuf(own, n + "taps", [P, 2 * PAIRS, 4])
        state = k.sbuf(own, n + "state", [P, 2 * PAIRS, 18])
        k.norm_work(work)
        entry = Entry(k, n + "in", layer, SCALE_FFN, SHIFT_FFN,
                      u[0][:, 0:2 * MAXC].rearrange("p (b t) -> p b t", b=2),
                      u[1][:, 0:KT * NS].rearrange("p (k t) -> p k t", k=KT))
        exit_ = Exit(k, n + "out", layer, GATE_FFN, y, stats=layer == 0)
        x_out = k.sem(n + "x_out")
        per_half = lambda what: [k.sem(f"{n}{what}_{s}") for s in ("g", "u")]
        per_unit = lambda what: [k.sem(f"{n}{what}_{s}") for s in ("g", "u", "d")]
        raw_in = per_unit("raw_in")
        hi_ready = per_unit("hi_ready")
        lo_ready = per_unit("lo_ready")
        const_in = k.sem(n + "const_in")
        up_done = per_half("up_done")
        evac = per_half("evac")
        prev_in = per_half("prev_in")
        saved = per_half("saved")
        conv_step = per_half("conv_step")
        silu_done = k.sem(n + "silu_done")
        product = k.sem(n + "product")
        g_hi_ready, g_lo_ready = k.sem(n + "g_hi_ready"), k.sem(n + "g_lo_ready")
        down_done = k.sem(n + "down_done")
        acc_done = k.sem(n + "acc_done")
        cleared = k.sem(n + "cleared")
        state_out = k.sem(n + "state_out")
        half_bank = [k.banks[0:3], k.banks[3:6]]
        down_bank = k.banks[6:8]
        block = own.enter_context(nc.Block())

        @block.sync
        def _(sp):
            sp.dma_start(taps[:], io["taps"][:, layer]).then_inc(const_in, 16)
            sp.dma_start(state[:], io["conv_state"][:, layer]).then_inc(const_in, 16)

            def load(p, wait):
                for s in (G, U, D):
                    if wait:
                        sp.wait_ge(lo_ready[s], p)
                    sp.dma_start(raw[s][:], io["ffn_w"][layer, bass.ds(p, 1), s].rearrange("a p n -> p (a n)"))\
                      .then_inc(raw_in[s], 16)

            load(0, False)
            with sp.Fori(1, PAIRS) as p:
                load(p, True)
            for s in (G, U):
                sp.wait_ge(saved[s], PAIRS)
            sp.dma_start(io["conv_out"][:, layer], state[:]).then_inc(state_out, 16)
            if layer == 1:
                for c, (t0, n_) in enumerate(CHUNKS):
                    exit_.added(sp, c, KT)
                    sp.dma_start(io["x_out"][:, :, t0:t0 + n_], k.x[:, :, t0:t0 + n_]).then_inc(x_out, 16)
                sp.wait_ge(x_out, 16 * NC)
            sp.wait_ge(state_out, 16)

        @block.gpsimd
        def _(pool):
            pool.memset(y[:], 0.0).then_inc(cleared, 1)
            entry.ready(pool, NC - 1)
            for s in (G, U):
                pool.memset(u[s][:, 0:CONV_W - 1], 0.0).then_inc(cleared, 1)
            exit_.pool(k, pool)

        def split_hi(act, s, p):
            act.wait_ge(raw_in[s], 16 * p + 16)
            if s == D:
                act.wait_ge(down_done, 24 * p)
            else:
                act.wait_ge(up_done[s], 3 * p)
            act.activation(w_hi[s][:], raw[s][:], ACT.Copy).then_inc(hi_ready[s], 1)

        def evacuate(act, s, p):
            m = 2 * p + s
            rows = u[s][:, PROMPT_W:].rearrange("p (s t) -> p s t", t=SAMPLE_W)
            tap2, bias = taps[:, bass.ds(m, 1), 2], taps[:, bass.ds(m, 1), 3]
            act.wait_ge(conv_step[s], 4 * p)
            act.wait_ge(product, p)
            if s == G:
                act.wait_ge(g_lo_ready, p)
            for c, (t0, n_) in enumerate(CHUNKS):
                w = prompt_cols(c)[1]
                bank = half_bank[s][c]
                act.wait_ge(up_done[s], 3 * p + c + 1)
                act.activation(u[s][:, 2 + t0:2 + t0 + w], bank[:, 0:w], ACT.Copy)
                if w < n_:
                    act.activation(rows[:, :, 2:], bank[:, w:n_].rearrange("p (s t) -> p s t", t=DEC_S), ACT.Copy)
                act.activation(conv[s][:, t0:t0 + n_], bank[:, 0:n_], ACT.Identity, bias=bias, scale=tap2)\
                   .then_inc(evac[s], 1)

        @block.scalar
        def _(act):
            split_hi(act, G, 0)
            for c in range(NC):
                entry.act(k, act, c, *put_in(h_hi))
            act.wait_ge(const_in, 32)
            entry.ready(act, NC - 1)
            act.wait_ge(cleared, 3)

            def pair(p, first=False, last=False):
                split_hi(act, U, p)
                if not first:
                    split_hi(act, D, p - 1)
                    act.wait_ge(product, p)
                    act.wait_ge(down_done, 24 * (p - 1))
                    act.activation(g_hi[:], conv[G], ACT.Copy).then_inc(g_hi_ready, 1)
                evacuate(act, G, p)
                if not last:
                    split_hi(act, G, p + 1)
                act.wait_ge(conv_step[G], 4 * p + 4)
                act.activation(conv[G], conv[G], ACT.Silu).then_inc(silu_done, 1)
                evacuate(act, U, p)

            pair(0, first=True)
            pair(1)
            with act.Fori(2, PAIRS - 1) as p:
                pair(p)
            pair(PAIRS - 1, last=True)
            split_hi(act, D, PAIRS - 1)
            act.wait_ge(product, PAIRS)
            act.wait_ge(down_done, 24 * (PAIRS - 1))
            act.activation(g_hi[:], conv[G], ACT.Copy).then_inc(g_hi_ready, 1)
            act.wait_ge(g_lo_ready, PAIRS)
            for c in range(NC):
                act.wait_ge(acc_done, 24 * (PAIRS - 1) + KT * (c + 1))
                exit_.norm.act(k, act, c)
            exit_.act_x(k, act)

        def split_lo(dve, s, p):
            dve.wait_ge(hi_ready[s], p + 1)
            dve.tensor_tensor(w_lo[s][:], raw[s][:], w_hi[s][:], ALU.subtract).then_inc(lo_ready[s], 1)

        def conv_steps(dve, s, p):
            m = 2 * p + s
            rows = u[s][:, PROMPT_W:].rearrange("p (s t) -> p s t", t=SAMPLE_W)
            cp, cs = conv[s][:, 0:SEQ], conv[s][:, SEQ:NT].rearrange("p (s t) -> p s t", t=DEC_S)

            mine = state[:, bass.ds(m, 1), :]
            mine_s = mine[:, :, 0:16].rearrange("p a (s t) -> p (a s) t", t=2)

            def prompt(tap):
                dve.scalar_tensor_tensor(cp, u[s][:, tap:tap + SEQ], taps[:, bass.ds(m, 1), tap], cp,
                                         ALU.mult, ALU.add).then_inc(conv_step[s], 1)

            def samples(tap):
                dve.scalar_tensor_tensor(cs, rows[:, :, tap:tap + DEC_S], taps[:, bass.ds(m, 1), tap], cs,
                                         ALU.mult, ALU.add).then_inc(conv_step[s], 1)

            def tap_1():
                dve.tensor_copy(rows[:, :, 0:2], mine_s).then_inc(prev_in[s], 1)
                dve.wait_ge(evac[s], 3 * p + 3)
                prompt(1)
                dve.wait_ge(prev_in[s], p + 1)
                samples(1)
                dve.tensor_copy(mine_s, rows[:, :, DEC_S:SAMPLE_W])
                dve.tensor_copy(mine[:, :, 16:18], u[s][:, SEQ:SEQ + 2].unsqueeze(1)).then_inc(saved[s], 1)

            def tap_0():
                dve.wait_ge(conv_step[s], 4 * p + 2)
                prompt(0)
                samples(0)
            return [tap_1, tap_0]

        def product_of(i, last):
            return divmod(i, KT)[::-1] if last else divmod(i, NC)

        def accumulate(dve, p, i, last=False):
            kt, c = product_of(i, last)
            t0, n_ = CHUNKS[c]
            dve.wait_ge(down_done, 24 * p + i + 1)
            dst = y[:, kt, t0:t0 + n_]
            dve.tensor_tensor(dst, down_bank[i % 2][:, 0:n_], dst, ALU.add).then_inc(acc_done, 1)

        @block.vector
        def _(dve):
            split_lo(dve, G, 0)
            for c in range(NC):
                entry.dve(k, dve, c, half_bank[U][c], h_hi, h_lo)
            dve.wait_ge(const_in, 32)
            dve.wait_ge(cleared, 3)

            def finish_g(p):
                for f in conv_steps(dve, U, p):
                    f()
                dve.wait_ge(conv_step[U], 4 * p + 4)
                dve.wait_ge(silu_done, p + 1)
                dve.tensor_tensor(conv[G], conv[G], conv[U], ALU.mult).then_inc(product, 1)

            def split_g(p):
                dve.wait_ge(g_hi_ready, p + 1)
                dve.tensor_tensor(g_lo[:], conv[G], g_hi[:], ALU.subtract).then_inc(g_lo_ready, 1)

            def pair(p, first=False, last=False):
                if not first:
                    finish_g(p - 1)
                split_lo(dve, U, p)
                if not first:
                    split_lo(dve, D, p - 1)
                    split_g(p - 1)
                side = conv_steps(dve, G, p)
                if not last:
                    side = [lambda: split_lo(dve, G, p + 1)] + side
                for i in range(24):
                    if not first:
                        accumulate(dve, p - 1, i)
                    if i % 3 == 2 and side:
                        side.pop(0)()

            pair(0, first=True)
            pair(1)
            with dve.Fori(2, PAIRS - 1) as p:
                pair(p)
            pair(PAIRS - 1, last=True)
            finish_g(PAIRS - 1)
            split_lo(dve, D, PAIRS - 1)
            split_g(PAIRS - 1)
            for i in range(24):
                accumulate(dve, PAIRS - 1, i, last=True)
            exit_.dve(k, dve, half_bank[U])

        @block.tensor
        def _(pe):
            entry.pe(k, pe, half_bank[U])

            def products(bank, s, kt, c, act_hi, act_lo, first, last):
                w = slice(kt * P, kt * P + P)
                a = slice(0, CHUNKS[c][1])
                pe.matmul(bank[:, a], w_hi[s][:, w], act_hi, start=first, stop=False)
                pe.matmul(bank[:, a], w_hi[s][:, w], act_lo, start=False, stop=False)
                return pe.matmul(bank[:, a], w_lo[s][:, w], act_hi, start=False, stop=last)

            def down(p, i, last_pair=False):
                kt, c = product_of(i, last_pair)
                t0, n_ = CHUNKS[c]
                if i == 0:
                    pe.wait_ge(lo_ready[D], p + 1)
                    pe.wait_ge(g_lo_ready, p + 1)
                pe.wait_ge(acc_done, 24 * p + max(i - 1, 0))
                last = products(down_bank[i % 2], D, kt, c, g_hi[:, t0:t0 + n_], g_lo[:, t0:t0 + n_], True, True)
                last.then_inc(down_done, 1)
                return last

            def up(s, p, first, with_down):
                pe.wait_ge(lo_ready[s], p + 1)
                for c, (t0, n_) in enumerate(CHUNKS):
                    if s == G and first:
                        entry.ready(pe, c)
                    if s == U and first and c == 0:
                        entry.ready(pe, NC - 1)
                    if not first:
                        pe.wait_ge(evac[s], 3 * (p - 1) + c + 1)
                    for kt in range(KT):
                        last = products(half_bank[s][c], s, kt, c, h_hi[:, kt, t0:t0 + n_],
                                        h_lo[:, kt, t0:t0 + n_], kt == 0, kt == KT - 1)
                        if kt == KT - 1:
                            last.then_inc(up_done[s], 1)
                        if with_down:
                            down(p - 1, c * KT + kt)

            def pair(p, first=False):
                up(G, p, first, False)
                up(U, p, first, not first)

            pair(0, first=True)
            pair(1)
            with pe.Fori(2, PAIRS) as p:
                pair(p)
            for i in range(24):
                down(PAIRS - 1, i, last_pair=True)
            pe.wait_ge(acc_done, 24 * PAIRS)
            exit_.pe(k, pe, half_bank[U])


def program(nc, io):
    with ExitStack() as ctx:
        k = Kernel(nc, ctx, io)
        adaln_stage(k)
        k.stage_done()
        mla(k)
        ffn_stage(k, 0)
        k.stage_done()
        pool_stage(k)
        k.stage_done()
        ffn_stage(k, 1)
        k.stage_done()


def columns(prompt, sample):
    rows = np.concatenate([prompt, sample.reshape(NS, -1)], axis=0)
    return np.ascontiguousarray(rows.T.reshape(-1, P, NT).transpose(1, 0, 2))


def units(w):
    kt = w.shape[0] // P
    return w.reshape(kt, P, w.shape[1] // P, P).transpose(2, 1, 0, 3).reshape(-1, P, kt * P)


def rotation():
    half = ROPE // 2
    inv = np.float32(10000.0) ** (-np.arange(half, dtype=np.float32) / half)
    pos = np.concatenate([np.arange(SEQ), PAST + np.tile(np.arange(DEC_S), DEC_B)]).astype(np.float32)
    ang = inv[:, None] * pos[None, :]
    cos, sin = np.cos(ang), np.sin(ang)
    return np.concatenate([cos, cos]), np.concatenate([-sin, sin])


def swapped(w):
    return np.concatenate([w[..., ROPE // 2:], w[..., :ROPE // 2]], axis=-1)


def attention_inputs(a):
    w_dkv, w_uq, w_uk, w_uv = (a[n][0] for n in ("mla_w_dkv", "mla_w_uq", "mla_w_uk", "mla_w_uv"))
    kr = w_dkv[:, KV_LORA:]
    proj = np.concatenate([units(w_dkv[:, :KV_LORA]), units(np.concatenate([swapped(kr)] * 2 + [kr] * 2, axis=1)),
                           units(a["mla_w_dq"][0])])
    uq = w_uq.reshape(Q_LORA, HEADS, NOPE + ROPE)
    nope, rope = uq[..., :NOPE], uq[..., NOPE:]
    rope = np.concatenate([rope, swapped(rope)], axis=-1)
    even = np.concatenate([nope, rope], axis=-1)[:, 0::2]
    odd = np.concatenate([rope, nope], axis=-1)[:, 1::2]
    heads = np.stack([even, odd], axis=2).reshape(QT, P, HP, 2, P).transpose(2, 1, 3, 0, 4).reshape(HP, P, -1)
    pairs = lambda w: w.reshape(LT, P, HP, P).transpose(2, 1, 0, 3).reshape(HP, P, -1)
    cos, sin = rotation()
    one = np.ones((NOPE, NT), np.float32)
    rot = np.stack([np.concatenate([one, cos, sin]), np.concatenate([cos, sin, one])], axis=1)
    lat, krope = a["cache_kv_latent"][0], a["cache_k_rope"][0]
    pages = lat.shape[0]
    lat_t = lat.reshape(pages, PAGE, LT, P).transpose(0, 3, 2, 1).reshape(pages, P, LT * PAGE)
    kr_t = np.tile(krope.transpose(0, 2, 1), (1, P // ROPE, 1))
    t = np.arange(DEC_S)
    own = np.eye(DEC_B, dtype=bool)[None, :, :, None] & (t[:, None, None, None] >= t)
    smask = np.where(own, 0.0, NEG).astype(np.float32).reshape(DEC_S, DEC_B, NS)
    tile = np.arange(P)
    return {
        "proj_w": proj,
        "ktab": np.concatenate([sin, sin, cos, cos]),
        "latent_gain": np.concatenate([a["mla_kv_norm"][0], a["mla_q_norm"][0]]).reshape(LT + QT, P).T,
        "pair_w": np.concatenate([heads, pairs(w_uk), pairs(w_uv)], axis=2),
        "rot": (rot * np.float32(SCALE)).astype(np.float32),
        "mask": np.where(tile[:, None] >= tile, 0.0, NEG).astype(np.float32),
        "cache": np.concatenate([lat, lat_t, kr_t], axis=2),
        "page_table": a["page_table"].astype(np.int32).reshape(1, -1),
        "wuk": w_uk.transpose(1, 2, 0).reshape(HP, P, KV_LORA).transpose(1, 0, 2),
        "wuv": w_uv.reshape(LT, P, HEADS * V_DIM).transpose(1, 0, 2),
        "smask": np.tile(smask, (HEADS, 1, 1)),
        "wo": units(a["mla_w_o"][0]),
    }


def pool_inputs(a):
    pos = np.arange(BUF)
    head = np.stack([1.0 / np.minimum(pos + 1, w) for w in WINDOWS]).astype(np.float32)
    return {
        "pool_w": a["pool_w"][0].reshape(KT, P, GT * P).transpose(1, 0, 2),
        "pool_scale": a["pool_scale"][0].reshape(KT, P).T,
        "pool_head": np.tile(head[None], (P, 1, 1)),
        "pool_state": a["state_pool"][0].reshape(DEC_B, BUF, KT, P).transpose(3, 2, 0, 1),
    }


def laid_out(a):
    f = D_FF
    pair_units = []
    for l in range(2):
        up = units(a["ffn_w_up"][l]).reshape(2, PAIRS, P, D_MODEL)
        down = a["ffn_w_down"][l].reshape(1, PAIRS, P, D_MODEL)
        pair_units.append(np.concatenate([up, down]).transpose(1, 0, 2, 3))
    by_pair = lambda v: v.reshape(2, PAIRS, P).transpose(2, 1, 0).reshape(P, 2 * PAIRS)
    taps = np.stack([np.stack([by_pair(a["ffn_conv_w"][l, t]) for t in range(CONV_W)]
                              + [by_pair(a["ffn_conv_b"][l])], axis=-1) for l in range(2)], axis=1)
    state = a["state_conv"].reshape(2, DEC_B, 2, 2, PAIRS, P).transpose(5, 0, 4, 3, 1, 2)
    state = state.reshape(P, 2, 2 * PAIRS, 16)
    state = np.concatenate([state, np.zeros((P, 2, 2 * PAIRS, 2), np.float32)], axis=-1)
    gains = np.stack([a["norm_mix_pre"], a["norm_mix_post"], a["norm_ffn_pre"], a["norm_ffn_post"]], axis=1)
    cond = np.concatenate([a["c_prompt"], a["c_sample"]])
    return {
        "x": columns(a["x_prompt"][0], a["x_sample"]),
        "cond": cond.T.reshape(KT, P, N_SEQ).transpose(1, 0, 2),
        "ada_w": a["ada_w"].reshape(2, KT, P, SIX // ADA_GROUP, ADA_GROUP * P).transpose(0, 3, 2, 1, 4)
        .reshape(2 * SIX // ADA_GROUP, P, ADA_GROUP * D_MODEL),
        "ada_b": a["ada_b"].reshape(2, SIX, P).transpose(2, 0, 1),
        "gains": gains.reshape(2, 4, KT, P).transpose(3, 0, 1, 2),
        "ident": np.eye(P, dtype=np.float32),
        "ffn_w": np.stack(pair_units),
        "taps": taps,
        "conv_state": state,
        **attention_inputs(a),
        **pool_inputs(a),
    }


OUTPUTS = {
    "x_out": [P, KT, NT],
    "conv_out": [P, 2, 2 * PAIRS, 18],
    "ckv_out": [P, LT, NT],
    "kr_out": [ROPE, NT],
    "pool_out": [P, KT, N_SEQ, BUF],
}


def kernel(**inputs):
    import concourse.bacc as bacc
    from concourse.bass_utils import run_bass_kernel_spmd

    a = {name: np.asarray(v) for name, v in inputs.items()}
    nc = bacc.Bacc("TRN2", target_bir_lowering=False, num_devices=1)
    arrays = {f"in_{n}": np.ascontiguousarray(v) for n, v in laid_out(a).items()}
    io = {n[3:]: nc.dram_tensor(n, list(v.shape), mybir.dt.from_np(v.dtype), kind="ExternalInput").ap()
          for n, v in arrays.items()}
    for n, shape in OUTPUTS.items():
        io[n] = nc.dram_tensor(f"out_{n}", shape, F32, kind="ExternalOutput").ap()
    program(nc, io)
    r = run_bass_kernel_spmd(nc, [arrays], core_ids=[0]).results[0]
    out = {n: np.asarray(r[f"out_{n}"]) for n in OUTPUTS}

    def rows(v, width):
        return v.transpose(1, 0, 2).reshape(width, -1).T

    x = rows(out["x_out"], D_MODEL)
    conv = out["conv_out"]
    conv_s = conv[..., 0:16].reshape(P, 2, PAIRS, 2, DEC_B, 2).transpose(1, 4, 5, 3, 2, 0)
    conv_p = conv[..., 16:18].reshape(P, 2, PAIRS, 2, 2).transpose(1, 4, 3, 2, 0)
    conv_s = conv_s.reshape(2, DEC_B, 2, 2 * D_FF)
    conv_p = conv_p.reshape(2, 1, 2, 2 * D_FF)
    ckv, kr = rows(out["ckv_out"], KV_LORA), out["kr_out"].T
    state = out["pool_out"].transpose(2, 3, 1, 0).reshape(N_SEQ, BUF, D_MODEL)
    sample = lambda v: v[SEQ:].reshape(DEC_B, DEC_S, -1)
    return (x[None, :SEQ], sample(x), ckv[None, None, :SEQ], kr[None, None, :SEQ], sample(ckv)[None],
            sample(kr)[None], state[None, :1], state[None, 1:], conv_p, conv_s)
```

```python
import numpy as np

import concourse.bass as bass
from concourse import mybir
from contextlib import ExitStack

F32 = mybir.dt.float32
F32R = mybir.dt.float32r
I32 = mybir.dt.int32
ALU = mybir.AluOpType
ACT = mybir.ActivationFunctionType
AX = mybir.AxisListType

P = 128
D_MODEL, SEQ, DEC_B, DEC_S = 1024, 1024, 8, 8
D_FF, CONV_W = 2816, 3
KT = D_MODEL // P
NS = DEC_B * DEC_S
NT = SEQ + NS
CHUNKS = [(0, 384), (384, 384), (768, NT - 768)]
NC = len(CHUNKS)
MAXC = 384
PAIRS = D_FF // P
N_SEQ = 1 + DEC_B
SIX = 6 * KT
SHIFT_MIX, SCALE_MIX, GATE_MIX, SHIFT_FFN, SCALE_FFN, GATE_FFN = range(0, SIX, KT)
EPS = 1e-6
ADA_GROUP = 4
ADA_SLOTS = 4


def col_tiles(c):
    n = CHUNKS[c][1]
    return [(o, min(P, n - o)) for o in range(0, n, P)]


class Norm:

    def __init__(self, k, name, jobs):
        self.jobs = jobs
        s = lambda what: k.sem(f"{name}_{what}")
        self.squared = s("squared")
        self.summed = s("summed")
        self.std = s("std")
        self.turned = s("turned")
        self.rstd = s("rstd")
        self.spread_done = s("spread")
        self.groups = []
        last, n = [0, 0], 0
        for src, _, _ in jobs:
            mine = []
            for slot, g, w in NORM_GROUPS[src.shape[1]]:
                n += 1
                mine.append((g, w, slot, last[slot]))
                last[slot] = n
            self.groups.append(mine)
        self.groups_to = [sum(len(x) for x in self.groups[:j + 1]) for j in range(len(jobs))]

    def act(self, k, act, j, ready=None):
        self.act_squares(k, act, j, ready)
        self.act_root(k, act, j)

    def act_squares(self, k, act, j, ready=None, groups=slice(None)):
        src, c, _ = self.jobs[j]
        t0, n = CHUNKS[c]
        for g, w, slot, before in self.groups[j][groups]:
            if ready:
                ready(j, g + w)
            if before:
                act.wait_ge(self.summed, before)
            act.activation(k.sq[:, 3 * slot:3 * slot + w, 0:n], src[:, g:g + w, t0:t0 + n], ACT.Square)\
               .then_inc(self.squared, 1)

    def act_root(self, k, act, j):
        src, c, _ = self.jobs[j]
        n = CHUNKS[c][1]
        act.wait_ge(self.summed, self.groups_to[j])
        if j:
            act.wait_ge(self.turned, j)
        act.activation(k.row[:, 0:n], k.stat_bank[0:1, 0:n], ACT.Sqrt, scale=1.0 / (src.shape[1] * P),
                       bias=k.eps[0:1, :]).then_inc(self.std, 1)

    def pe(self, k, pe, j):
        self.pe_sum(k, pe, j)
        self.pe_turn(k, pe, j)

    def pe_sum(self, k, pe, j):
        n = CHUNKS[self.jobs[j][1]][1]
        first = self.groups_to[j - 1] if j else 0
        tiles = sum(w for _, w, _, _ in self.groups[j])
        if j and k.col_bank is k.stat_bank:
            pe.wait_ge(self.rstd, j)
        elif j:
            pe.wait_ge(self.std, j)
        for i, (g, w, slot, _) in enumerate(self.groups[j]):
            pe.wait_ge(self.squared, first + i + 1)
            for t in range(w):
                last = pe.matmul(k.stat_bank[0:1, 0:n], k.ones[:, 0:1], k.sq[:, 3 * slot + t, 0:n],
                                 start=g + t == 0, stop=g + t == tiles - 1)
            last.then_inc(self.summed, 1)

    def pe_turn(self, k, pe, j):
        pe.wait_ge(self.std, j + 1)
        if j:
            pe.wait_ge(self.rstd, j)
        for i, (o, w) in enumerate(col_tiles(self.jobs[j][1])):
            last = pe.matmul(k.col_bank[0:w, MAXC + i:MAXC + i + 1], k.row[0:1, o:o + w], k.ones[0:1, 0:1],
                             start=True, stop=True)
        last.then_inc(self.turned, 1)

    def dve(self, k, dve, j):
        dve.wait_ge(self.turned, j + 1)
        dve.reciprocal(self.jobs[j][2], k.col_bank[:, MAXC:MAXC + 3]).then_inc(self.rstd, 1)

    def pe_spread(self, k, pe, j, bank):
        pe.wait_ge(self.rstd, j + 1)
        spread(k, pe, self.jobs[j][1], self.jobs[j][2], bank).then_inc(self.spread_done, 1)


NORM_GROUPS = {8: [(0, 0, 3), (1, 3, 2), (0, 5, 3)], 4: [(0, 0, 3), (1, 3, 1)], 2: [(0, 0, 2)]}
NORM_WORK = 5 * MAXC


def spread(k, pe, c, rstd, bank):
    for j, (o, w) in enumerate(col_tiles(c)):
        last = pe.matmul(bank[:, o:o + w], rstd[0:w, j:j + 1].to_broadcast([w, P]), k.ident[0:w, 0:w],
                         start=True, stop=True)
    return last


class Kernel:

    def __init__(self, nc, ctx, io):
        self.nc, self.ctx, self.io, self.sems = nc, ctx, io, []
        self.x = self.sbuf(ctx, "x", [P, KT, NT])
        self.ada = self.sbuf(ctx, "ada", [P, 2, SIX, N_SEQ])
        self.ident = self.sbuf(ctx, "ident", [P, P])
        self.ones = self.sbuf(ctx, "ones", [P, 1])
        self.eps = self.sbuf(ctx, "eps", [P, 1])
        self.rstd = self.sbuf(ctx, "rstd", [P, 3, NC, 3])
        self.psum = ctx.enter_context(nc.psum_tensor("psum", [P, 8, 512], F32))
        self.banks = [self.psum[:, i, :] for i in range(8)]
        self.stat_bank, self.col_bank = self.banks[6:8]

    def norm_work(self, flat):
        self.sq = flat[:, 0:NORM_WORK].rearrange("p (k t) -> p k t", k=5)
        self.row = flat[0:1, NORM_WORK:NORM_WORK + MAXC]

    def sbuf(self, ctx, name, shape, dt=F32):
        return ctx.enter_context(self.nc.sbuf_tensor(name, shape, dt))

    def sem(self, name):
        self.sems.append(self.nc.alloc_semaphore(name=name))
        return self.sems[-1]

    def stage_done(self):
        self.nc.clear_and_free_semaphores(self.sems)
        self.nc.all_engine_barrier()
        self.sems = []


def adaln_stage(k):
    nc, io = k.nc, k.io
    GROUPS = 2 * SIX // ADA_GROUP
    HALF = ADA_GROUP * D_MODEL // 2
    X_JOBS = 2
    with ExitStack() as own:
        w = k.sbuf(own, "ada_w", [P, ADA_SLOTS, ADA_GROUP * D_MODEL])
        w_hi = k.sbuf(own, "ada_w_hi", [P, 2, ADA_GROUP * D_MODEL], F32R)
        w_lo = k.sbuf(own, "ada_w_lo", [P, 2, ADA_GROUP * D_MODEL], F32R)
        c = k.sbuf(own, "cond", [P, KT, N_SEQ])
        c_silu = k.sbuf(own, "cond_silu", [P, KT, N_SEQ])
        c_parts = k.sbuf(own, "cond_parts", [P, KT, 2 * N_SEQ], F32R)
        fold = k.sbuf(own, "fold", [2 * N_SEQ, N_SEQ])
        rows = k.sbuf(own, "ada_rows", [2 * N_SEQ, ADA_SLOTS, ADA_GROUP * P])
        bias = k.sbuf(own, "ada_bias", [P, 2, SIX])
        gains = k.sbuf(own, "gains", [P, 2, 4, KT])
        k.norm_work(k.sbuf(own, "ada_norm_work", [P, NORM_WORK + MAXC]))
        x_norm = Norm(k, "x0", [(k.x, c_, k.rstd[:, 0, c_, :]) for c_ in range(NC)])
        small_in, const_in, x_in = k.sem("ada_small_in"), k.sem("const_in"), k.sem("x_in")
        w_in = [k.sem(f"ada_w_in{s}") for s in range(ADA_SLOTS)]
        silu_done, parts = k.sem("cond_silu_done"), k.sem("cond_parts_done")
        constants = k.sem("constants")
        hi_ready, lo_ready = k.sem("ada_hi"), k.sem("ada_lo")
        used = k.sem("ada_used")
        rows_done = k.sem("ada_rows_done")
        turned = k.sem("ada_turned")
        evac = k.sem("ada_evac")
        folded = k.sem("ada_folded")
        block = own.enter_context(nc.Block())

        def run(step, eng, between=lambda: None):
            for s in range(ADA_SLOTS):
                step(s, s, True)
            between()

            def rest(n):
                for s in range(ADA_SLOTS):
                    step(n * ADA_SLOTS + s, s, False)
            with eng.Fori(1, GROUPS // ADA_SLOTS) as n:
                rest(n)

        def wait(eng, sem, value, first):
            if not first or value > 0:
                eng.wait_ge(sem, value)

        @block.sync
        def _(sp):
            sp.dma_start(c[:], io["cond"]).then_inc(small_in, 16)

            def load(m, s, first):
                wait(sp, lo_ready, 2 * (m - ADA_SLOTS + 1), first)
                sp.dma_start(w[:, s, :], io["ada_w"][bass.ds(m, 1)]
                             .rearrange("a p n -> p (a n)")).then_inc(w_in[s], 16)
                if first and s == X_JOBS - 1:
                    sp.dma_start(k.x[:], io["x"]).then_inc(x_in, 16)
            run(load, sp)

        @block.scalar
        def _(act):
            act.dma_start(k.ident[:], io["ident"]).then_inc(const_in, 16)
            act.dma_start(bias[:], io["ada_b"]).then_inc(const_in, 16)
            act.dma_start(gains[:], io["gains"]).then_inc(const_in, 16)
            act.wait_ge(small_in, 16)
            act.activation(c_silu[:], c[:], ACT.Silu).then_inc(silu_done, 1)
            act.wait_ge(silu_done, 1)
            act.activation(c_parts[:, :, 0:N_SEQ], c_silu[:], ACT.Copy).then_inc(parts, 1)

            def copy_rows(m, s, first):
                wait(act, used, 2 * m + 2, first)
                wait(act, turned, m - 3, first)
                act.activation(rows[:, s, :], k.banks[s][0:2 * N_SEQ, :], ACT.Copy).then_inc(rows_done, 1)

            def step(m, s, first):
                if first:
                    act.wait_ge(w_in[s], 16)
                else:
                    act.wait_ge(w_in[s], 4 * (m - s) + 16)
                for h in range(2):
                    cols = slice(h * HALF, (h + 1) * HALF)
                    wait(act, used, 2 * m + h - 3, first)
                    act.activation(w_hi[:, s % 2, cols], w[:, s, cols], ACT.Copy).then_inc(hi_ready, 1)
                if not (first and s == 0):
                    copy_rows(m - 1, (s - 1) % ADA_SLOTS, first)
                if first and s >= X_JOBS:
                    act.wait_ge(x_in, 16)
                    act.wait_ge(constants, 2)
                    x_norm.act(k, act, s - X_JOBS)
            run(step, act, lambda: x_norm.act(k, act, NC - 1))
            copy_rows(GROUPS - 1, ADA_SLOTS - 1, False)

        @block.tensor
        def _(pe):
            def turn(m, s, first):
                wait(pe, rows_done, m + 1, first)
                wait(pe, evac, m - 1, first)
                for a in range(ADA_GROUP):
                    last = pe.matmul(k.banks[4 + s % 2][:, a * N_SEQ:(a + 1) * N_SEQ],
                                     rows[:, s, a * P:(a + 1) * P], fold[:], start=True, stop=True)
                last.then_inc(turned, 1)

            def step(m, s, first):
                if first and s >= X_JOBS:
                    x_norm.pe_sum(k, pe, s - X_JOBS)
                wait(pe, rows_done, m - 3, first)
                out = k.banks[s][0:2 * N_SEQ, :]
                for kt in range(KT):
                    cols = slice(kt * ADA_GROUP * P, (kt + 1) * ADA_GROUP * P)
                    if kt % (KT // 2) == 0:
                        wait(pe, lo_ready, 2 * m + kt // (KT // 2) + 1, first)
                    pe.matmul(out, c_parts[:, kt, :], w_hi[:, s % 2, cols], start=kt == 0, stop=False)
                    last = pe.matmul(out, c_parts[:, kt, :], w_lo[:, s % 2, cols], start=False, stop=kt == KT - 1)
                    if kt % (KT // 2) == KT // 2 - 1:
                        last.then_inc(used, 1)
                if not (first and s == 0):
                    turn(m - 1, (s - 1) % ADA_SLOTS, first)
                if first and s >= X_JOBS:
                    x_norm.pe_turn(k, pe, s - X_JOBS)
            pe.wait_ge(parts, 2)
            pe.wait_ge(constants, 3)
            run(step, pe, lambda: x_norm.pe(k, pe, NC - 1))
            turn(GROUPS - 1, ADA_SLOTS - 1, False)

        @block.vector
        def _(dve):
            dve.memset(k.ones[:], 1.0).then_inc(constants, 1)
            dve.memset(k.eps[:], EPS).then_inc(constants, 1)
            dve.wait_ge(parts, 1)
            dve.tensor_tensor(c_parts[:, :, N_SEQ:], c_silu[:], c_parts[:, :, 0:N_SEQ], ALU.subtract).then_inc(parts, 1)
            dve.wait_ge(const_in, 48)
            dve.tensor_tensor(fold[:], k.ident[0:2 * N_SEQ, 0:N_SEQ], k.ident[0:2 * N_SEQ, N_SEQ:2 * N_SEQ], ALU.add)\
               .then_inc(constants, 1)
            flat, flat_bias = k.ada[:].rearrange("p l m s -> p (l m) s"), bias[:].rearrange("p l m -> p (l m)")

            def take(m, s, first):
                wait(dve, turned, m + 1, first)
                tiles = bass.ds(m * ADA_GROUP, ADA_GROUP)
                dve.tensor_tensor(flat[:, tiles, :],
                                  k.banks[4 + s % 2][:, 0:ADA_GROUP * N_SEQ].rearrange("p (m s) -> p m s", s=N_SEQ),
                                  flat_bias[:, tiles].unsqueeze(2).to_broadcast([P, ADA_GROUP, N_SEQ]), ALU.add)\
                   .then_inc(evac, 1)

            def step(m, s, first):
                for h in range(2):
                    cols = slice(h * HALF, (h + 1) * HALF)
                    wait(dve, hi_ready, 2 * m + h + 1, first)
                    dve.tensor_tensor(w_lo[:, s % 2, cols], w[:, s, cols], w_hi[:, s % 2, cols], ALU.subtract)\
                       .then_inc(lo_ready, 1)
                if not (first and s < 2):
                    take(m - 2, (s - 2) % ADA_SLOTS, first)
                if first and s > X_JOBS:
                    x_norm.dve(k, dve, s - X_JOBS - 1)

            def x_rest():
                for j in range(ADA_SLOTS - X_JOBS - 1, NC):
                    x_norm.dve(k, dve, j)
            run(step, dve, x_rest)
            for m in (GROUPS - 2, GROUPS - 1):
                take(m, m % ADA_SLOTS, False)
            dve.wait_ge(evac, GROUPS)
            for l in range(2):
                for which, (first, one) in enumerate([(SCALE_MIX, 1.0), (GATE_MIX, 0.0),
                                                      (SCALE_FFN, 1.0), (GATE_FFN, 0.0)]):
                    part = k.ada[:, l, first:first + KT, :]
                    dve.scalar_tensor_tensor(part, part, one,
                                             gains[:, l, which, :].unsqueeze(2).to_broadcast([P, KT, N_SEQ]),
                                             ALU.add, ALU.mult).then_inc(folded, 1)
            dve.wait_ge(folded, 8)


def prompt_cols(c):
    t0, n = CHUNKS[c]
    return t0, min(n, SEQ - t0)


class Entry:

    def __init__(self, k, name, layer, scale, shift, scaled, scaled_s, late=True):
        self.late = last_x_norm(k, name) if late else None
        self.a = k.ada[:, layer, scale:scale + KT, :]
        self.s = k.ada[:, layer, shift:shift + KT, :]
        self.t, self.ts = scaled, scaled_s
        self.spread_done = k.sem(f"{name}_spread")
        self.scaled = k.sem(f"{name}_scaled")
        self.scaled_s = k.sem(f"{name}_scaled_s")
        self.hi = k.sem(f"{name}_hi")
        self.lo = k.sem(f"{name}_lo")

    def pe(self, k, pe, banks):
        for c in range(NC):
            if self.late and c == NC - 1:
                self.late.pe(k, pe, 0)
                pe.wait_ge(self.late.rstd, 1)
            spread(k, pe, c, k.rstd[:, 0, c, :], banks[c]).then_inc(self.spread_done, 1)

    def dve(self, k, dve, c, bank, h_hi, h_lo):
        t0, n = prompt_cols(c)
        if self.late and c == 1:
            self.late.dve(k, dve, 0)
        dve.wait_ge(self.spread_done, c + 1)
        samples = c == NC - 1
        o = SEQ - CHUNKS[c][0]
        seqs = lambda ap: ap.rearrange("p k (s t) -> p k s t", t=DEC_S)
        by_seq = lambda ap: ap[:, :, 1:].unsqueeze(3).to_broadcast([P, KT, DEC_B, DEC_S])
        steps = {
            0: lambda: dve.tensor_tensor(self.ts[:], k.x[:, :, SEQ:NT],
                                         bank[:, o:o + NS].unsqueeze(1).to_broadcast([P, KT, NS]), ALU.mult),
            1: lambda: dve.tensor_tensor(seqs(self.ts[:]), seqs(self.ts[:]), by_seq(self.a), ALU.mult),
            2: lambda: dve.tensor_tensor(seqs(self.ts[:]), seqs(self.ts[:]), by_seq(self.s), ALU.add),
        }
        for kt in range(KT + 1):
            i = c * KT + kt
            if kt < KT:
                if i >= 2:
                    dve.wait_ge(self.hi, i - 1)
                    dve.wait_ge(self.lo, i - 1)
                dve.scalar_tensor_tensor(self.t[:, kt % 2, 0:n], k.x[:, kt, t0:t0 + n], self.a[:, kt, 0:1],
                                         bank[:, 0:n], ALU.mult, ALU.mult).then_inc(self.scaled, 1)
            if samples and kt in steps:
                if kt:
                    dve.wait_ge(self.scaled_s, kt)
                steps[kt]().then_inc(self.scaled_s, 1)
            if kt >= 1:
                j = kt - 1
                dve.wait_ge(self.hi, i)
                dve.scalar_tensor_tensor(h_lo[:, j, t0:t0 + n], self.t[:, j % 2, 0:n], self.s[:, j, 0:1],
                                         h_hi[:, j, t0:t0 + n], ALU.add, ALU.subtract).then_inc(self.lo, 1)
        if samples:
            dve.wait_ge(self.hi, NC * KT + 1)
            dve.tensor_tensor(h_lo[:, :, SEQ:NT], self.ts[:], h_hi[:, :, SEQ:NT], ALU.subtract)\
               .then_inc(self.lo, 1)

    def act(self, k, act, c, put, put_s):
        t0, n = prompt_cols(c)
        late = self.late if c == 0 else None
        if late:
            late.act_squares(k, act, 0, groups=slice(0, 2))
        for kt in range(KT):
            act.wait_ge(self.scaled, c * KT + kt + 1)
            act.activation(put(kt, t0, n), self.t[:, kt % 2, 0:n], ACT.Identity,
                           bias=self.s[:, kt, 0:1]).then_inc(self.hi, 1)
            if late and kt == KT // 2:
                late.act_squares(k, act, 0, groups=slice(2, None))
        if late:
            late.act_root(k, act, 0)
        if c == NC - 1:
            act.wait_ge(self.scaled_s, 3)
            act.activation(put_s, self.ts[:].rearrange("p k (s t) -> p k s t", t=DEC_S), ACT.Copy)\
               .then_inc(self.hi, 1)

    def ready(self, eng, c):
        eng.wait_ge(self.lo, (c + 1) * KT + (c == NC - 1))

    def tile_ready(self, eng, c, kt):
        if c < NC - 1:
            eng.wait_ge(self.lo, c * KT + kt + 1)
        elif kt == 0:
            self.ready(eng, c)


POOL_TILES = (0, 2, 4, 6)


class Exit:

    def __init__(self, k, name, layer, gate, y, stats=True):
        self.y, self.stats = y, stats
        jobs = [(y, c, k.rstd[:, 1, c, :]) for c in range(NC)]
        if stats:
            jobs += [(k.x, c, k.rstd[:, 0, c, :]) for c in range(NC - 1)]
        self.norm = Norm(k, name, jobs)
        self.b = k.ada[:, layer, gate:gate + KT, :]
        self.scaled = k.sem(f"{name}_scaled")
        self.scaled_s = k.sem(f"{name}_scaled_s")
        self.added_d = k.sem(f"{name}_added_d")
        self.added_p = k.sem(f"{name}_added_p")

    def added(self, eng, c, tiles):
        p = sum(kt in POOL_TILES for kt in range(tiles))
        eng.wait_ge(self.added_d, c * (KT - len(POOL_TILES)) + tiles - p + (c == NC - 1))
        if c or p:
            eng.wait_ge(self.added_p, c * len(POOL_TILES) + p)

    def dve(self, k, dve, banks):
        norm = self.norm
        norm.dve(k, dve, 0)
        for c in range(NC):
            if c + 1 < NC:
                norm.dve(k, dve, c + 1)
            self.apply(k, dve, c, banks[c])
            if c and self.stats:
                norm.dve(k, dve, NC + c - 1)

    def apply(self, k, dve, c, bank):
        t0, n = prompt_cols(c)
        dve.wait_ge(self.norm.spread_done, c + 1)
        if c == NC - 1:
            o = SEQ - CHUNKS[c][0]
            seqs = lambda ap: ap.rearrange("p k (s t) -> p k s t", t=DEC_S)
            y, x = self.y[:, :, SEQ:NT], k.x[:, :, SEQ:NT]
            dve.tensor_tensor(y, y, bank[:, o:o + NS].unsqueeze(1).to_broadcast([P, KT, NS]), ALU.mult)\
               .then_inc(self.scaled_s, 1)
            dve.wait_ge(self.scaled_s, 1)
            dve.tensor_tensor(seqs(y), seqs(y), self.b[:, :, 1:].unsqueeze(3).to_broadcast([P, KT, DEC_B, DEC_S]),
                              ALU.mult).then_inc(self.scaled_s, 1)
            dve.wait_ge(self.scaled_s, 2)
            dve.tensor_tensor(x, x, y, ALU.add).then_inc(self.added_d, 1)
        for kt in range(KT + 1):
            if kt < KT:
                y = self.y[:, kt, t0:t0 + n]
                dve.scalar_tensor_tensor(y, y, self.b[:, kt, 0:1], bank[:, 0:n], ALU.mult, ALU.mult)\
                   .then_inc(self.scaled, 1)
            if kt and kt - 1 not in POOL_TILES:
                x = k.x[:, kt - 1, t0:t0 + n]
                dve.wait_ge(self.scaled, c * KT + kt)
                dve.tensor_tensor(x, x, self.y[:, kt - 1, t0:t0 + n], ALU.add).then_inc(self.added_d, 1)

    def pool(self, k, pool):
        for c in range(NC):
            t0, n = prompt_cols(c)
            for kt in POOL_TILES:
                pool.wait_ge(self.scaled, c * KT + kt + 1)
                x = k.x[:, kt, t0:t0 + n]
                pool.tensor_tensor(x, x, self.y[:, kt, t0:t0 + n], ALU.add).then_inc(self.added_p, 1)

    def act_x(self, k, act):
        if self.stats:
            for c in range(NC - 1):
                self.norm.act(k, act, NC + c, lambda j, tiles: self.added(act, j - NC, tiles))

    def pe(self, k, pe, banks, summed=False):
        for c in range(NC):
            if not (summed and c == 0):
                self.norm.pe_sum(k, pe, c)
            self.norm.pe_turn(k, pe, c)
            self.norm.pe_spread(k, pe, c, banks[c])
        if self.stats:
            for c in range(NC - 1):
                self.norm.pe(k, pe, NC + c)


def last_x_norm(k, name):
    return Norm(k, name + "_x", [(k.x, NC - 1, k.rstd[:, 0, NC - 1, :])])


def put_in(h):
    return (lambda kt, t0, n: h[:, kt, t0:t0 + n],
            h[:, :, SEQ:NT].rearrange("p k (s t) -> p k s t", t=DEC_S))


HEADS, NOPE, ROPE, V_DIM = 16, 64, 32, 64
Q_LORA, KV_LORA = 512, 256
QT, LT = Q_LORA // P, KV_LORA // P
HP = HEADS // 2
QB = SEQ // P
PAGE, PAGES = 128, 8
PAST = PAGE * PAGES
N_POOL = 80
SCALE = float((NOPE + ROPE) ** -0.5)
NEG = -1e30
PAIR_W = 2 * QT * P + 2 * LT * P
CACHE_W = KV_LORA + LT * PAGE + PAGE



def mla_project_stage(k, m):
    nc, io = k.nc, k.io
    UNITS = LT + 1 + QT
    with ExitStack() as own:
        h_hi = k.sbuf(own, "mla_h_hi", [P, KT, NT], F32R)
        h_lo = k.sbuf(own, "mla_h_lo", [P, KT, NT], F32R)
        ktab = k.sbuf(own, "ktab", [P, NT])
        raw = [k.sbuf(own, f"proj_raw{s}", [P, D_MODEL]) for s in range(2)]
        w_hi = [k.sbuf(own, f"proj_w_hi{s}", [P, D_MODEL], F32R) for s in range(2)]
        w_lo = [k.sbuf(own, f"proj_w_lo{s}", [P, D_MODEL], F32R) for s in range(2)]
        work = k.sbuf(own, "proj_work", [P, 2304])
        scaled = k.sbuf(own, "proj_scaled", [P, 2, MAXC])
        scaled_s = k.sbuf(own, "proj_scaled_s", [P, KT, NS])
        gain = k.sbuf(own, "latent_gain", [P, LT + QT])
        k.norm_work(work)
        rot_tmp = work[:, 0:MAXC]
        cq = k.x[:, 0:QT, :]
        entry = Entry(k, "mla_in", 0, SCALE_MIX, SHIFT_MIX, scaled, scaled_s, late=False)
        kv_norm = Norm(k, "kv_norm", [(m.ckv[:], c, k.rstd[:, 1, c, :]) for c in range(NC)])
        q_norm = Norm(k, "q_norm", [(cq, c, k.rstd[:, 2, c, :]) for c in range(NC)])
        raw_in = [k.sem(f"proj_raw_in{s}") for s in range(2)]
        const_in = k.sem("proj_const_in")
        hi_ready, lo_ready = k.sem("proj_hi"), k.sem("proj_lo")
        done = k.sem("proj_done")
        evac_a = k.sem("proj_evac_a")
        rot = k.sem("proj_rot")
        kv_scaled, q_scaled = k.sem("kv_scaled"), k.sem("q_scaled")
        cq_hi, cq_lo = k.sem("cq_hi_ready"), k.sem("cq_lo_ready")
        out = k.sem("latent_out")
        ROPE_UNIT = LT
        banks = [k.banks[0:3], k.banks[3:6]]
        kv_spread, q_spread = k.banks[7], banks[1]
        k.col_bank = k.stat_bank
        Q_LAST = UNITS - 1
        block = own.enter_context(nc.Block())

        @block.sync
        def _(sp):
            for j in range(UNITS):
                if j >= 2:
                    sp.wait_ge(lo_ready, j - 1)
                sp.dma_start(raw[j % 2][:], io["proj_w"][j]).then_inc(raw_in[j % 2], 16)
            sp.wait_ge(rot, 3 * NC + 1)
            sp.dma_start(io["kr_out"], m.kr[0:ROPE, :]).then_inc(out, 16)
            sp.wait_ge(kv_scaled, LT * NC)
            sp.dma_start(io["ckv_out"], m.ckv[:]).then_inc(out, 16)
            sp.wait_ge(out, 32)

        @block.scalar
        def _(act):
            act.dma_start(ktab[:], io["ktab"]).then_inc(const_in, 16)
            act.dma_start(gain[:], io["latent_gain"]).then_inc(const_in, 16)

            def split(j):
                act.wait_ge(raw_in[j % 2], 16 * (j // 2 + 1))
                if j >= 2:
                    act.wait_ge(done, NC * (j - 1))
                act.activation(w_hi[j % 2][:], raw[j % 2][:], ACT.Copy).then_inc(hi_ready, 1)
            for c in range(NC):
                entry.act(k, act, c, *put_in(h_hi))
                if c == 0:
                    split(0)
            entry.ready(act, NC - 1)
            n = 0
            for j in range(UNITS):
                if j + 1 < UNITS:
                    split(j + 1)
                if j == ROPE_UNIT:
                    continue
                if j == ROPE_UNIT + 1:
                    act.wait_ge(evac_a, NC * LT)
                    act.wait_ge(rot, 3 * NC)
                dst = m.ckv[:, j] if j < LT else cq[:, j - LT - 1]
                for c, (t0, w) in enumerate(CHUNKS):
                    if j == ROPE_UNIT + 1:
                        kv_norm.act(k, act, c)
                    act.wait_ge(done, NC * j + c + 1)
                    act.activation(dst[:, t0:t0 + w], banks[j % 2][c][:, 0:w], ACT.Copy).then_inc(evac_a, 1)
                    if j == Q_LAST:
                        act.wait_ge(evac_a, NC * (UNITS - 2) + c + 1)
                        q_norm.act(k, act, c)

            def cq_hi_chunk(c):
                t0, w = CHUNKS[c]
                act.wait_ge(q_scaled, QT * (c + 1))
                act.activation(m.cq_hi[:, :, t0:t0 + w], cq[:, :, t0:t0 + w], ACT.Copy).then_inc(cq_hi, 1)
            for c in range(NC):
                cq_hi_chunk(c)

        @block.vector
        def _(dve):

            def split(j):
                dve.wait_ge(hi_ready, j + 1)
                dve.tensor_tensor(w_lo[j % 2][:], raw[j % 2][:], w_hi[j % 2][:], ALU.subtract).then_inc(lo_ready, 1)
            for c in range(NC):
                entry.dve(k, dve, c, banks[1][c], h_hi, h_lo)
                if c == 0:
                    split(0)
            dve.wait_ge(const_in, 32)
            def kv_chunk(c):
                t0, w = CHUNKS[c]
                dve.wait_ge(kv_norm.spread_done, c + 1)
                for t in range(LT):
                    part = m.ckv[:, t, t0:t0 + w]
                    dve.scalar_tensor_tensor(part, part, gain[:, t:t + 1], kv_spread[:, 0:w], ALU.mult, ALU.mult)\
                       .then_inc(kv_scaled, 1)

            for j in range(UNITS):
                if j + 1 < UNITS:
                    split(j + 1)
                if j == ROPE_UNIT + 1:
                    kv_norm.dve(k, dve, 0)
                    for c in range(NC):
                        if c + 1 < NC:
                            kv_norm.dve(k, dve, c + 1)
                        kv_chunk(c)
                if j != ROPE_UNIT:
                    continue
                for c, (t0, w) in enumerate(CHUNKS):
                    bank = banks[j % 2][c]
                    cols = slice(t0, t0 + w)
                    dve.wait_ge(done, NC * j + c + 1)
                    if c:
                        dve.wait_ge(rot, 3 * c)
                    dve.tensor_tensor(rot_tmp[64:P, 0:w], bank[0:64, 0:w], ktab[0:64, cols], ALU.mult)\
                       .then_inc(rot, 1)
                    dve.tensor_tensor(m.kr[64:P, cols], bank[64:P, 0:w], ktab[64:P, cols], ALU.mult)\
                       .then_inc(rot, 1)
                    dve.wait_ge(rot, 3 * c + 2)
                    dve.tensor_tensor(m.kr[64:P, cols], m.kr[64:P, cols], rot_tmp[64:P, 0:w], ALU.add)\
                       .then_inc(rot, 1)
                dve.wait_ge(rot, 3 * NC)
                dve.tensor_copy(m.kr[0:64, :], m.kr[64:P, :]).then_inc(rot, 1)

            def q_chunk(c):
                t0, w = CHUNKS[c]
                dve.wait_ge(q_norm.spread_done, c + 1)
                for t in range(QT):
                    part = cq[:, t, t0:t0 + w]
                    dve.scalar_tensor_tensor(part, part, gain[:, LT + t:LT + t + 1], q_spread[c][:, 0:w],
                                             ALU.mult, ALU.mult).then_inc(q_scaled, 1)
                dve.wait_ge(cq_hi, c + 1)
                dve.tensor_tensor(m.cq_lo[:, :, t0:t0 + w], cq[:, :, t0:t0 + w], m.cq_hi[:, :, t0:t0 + w],
                                  ALU.subtract).then_inc(cq_lo, 1)
            q_norm.dve(k, dve, 0)
            for c in range(NC):
                if c + 1 < NC:
                    q_norm.dve(k, dve, c + 1)
                q_chunk(c)

        @block.tensor
        def _(pe):
            entry.pe(k, pe, banks[1])

            def kv_spread_chunk(c):
                if c:
                    pe.wait_ge(kv_scaled, LT * c)
                kv_norm.pe_spread(k, pe, c, kv_spread)
            first, second = ROPE_UNIT + 1, ROPE_UNIT + 2
            side = {
                (first, 0): lambda: kv_norm.pe_sum(k, pe, 0),
                (first, 1): lambda: (kv_norm.pe_turn(k, pe, 0), kv_norm.pe_sum(k, pe, 1)),
                (first, 2): lambda: (kv_norm.pe_turn(k, pe, 1), kv_norm.pe_sum(k, pe, 2), kv_spread_chunk(0)),
                (second, 0): lambda: (kv_norm.pe_turn(k, pe, 2), kv_spread_chunk(1)),
                (second, 1): lambda: kv_spread_chunk(2),
                (Q_LAST, 0): lambda: (pe.wait_ge(kv_norm.rstd, NC), q_norm.pe_sum(k, pe, 0)),
                (Q_LAST, 1): lambda: (q_norm.pe_turn(k, pe, 0), q_norm.pe_sum(k, pe, 1)),
                (Q_LAST, 2): lambda: (q_norm.pe_turn(k, pe, 1), q_norm.pe_sum(k, pe, 2),
                                      pe.wait_ge(evac_a, NC * (UNITS - 2)),
                                      q_norm.pe_spread(k, pe, 0, q_spread[0]), q_norm.pe_turn(k, pe, 2),
                                      q_norm.pe_spread(k, pe, 1, q_spread[1]), q_norm.pe_spread(k, pe, 2, q_spread[2])),
            }
            for j in range(UNITS):
                pe.wait_ge(lo_ready, j + 1)
                for c, (t0, w) in enumerate(CHUNKS):
                    if j == 1 and c == 0:
                        entry.ready(pe, NC - 1)
                    if j >= 2:
                        if j - 2 == ROPE_UNIT:
                            pe.wait_ge(rot, 3 * c + 2)
                        else:
                            pe.wait_ge(evac_a, NC * (j - 2 - (j - 2 > ROPE_UNIT)) + c + 1)
                    for kt in range(KT):
                        if j == 0:
                            entry.tile_ready(pe, c, kt)
                        o = slice(kt * P, kt * P + P)
                        bank = banks[j % 2][c][:, 0:w]
                        hh, hl = h_hi[:, kt, t0:t0 + w], h_lo[:, kt, t0:t0 + w]
                        pe.matmul(bank, w_hi[j % 2][:, o], hh, start=kt == 0, stop=False)
                        pe.matmul(bank, w_hi[j % 2][:, o], hl, start=False, stop=False)
                        last = pe.matmul(bank, w_lo[j % 2][:, o], hh, start=False, stop=kt == KT - 1)
                    last.then_inc(done, 1)
                    if (j, c) in side:
                        side[j, c]()


def mla_prompt_stage(k, m):
    k.col_bank = k.banks[7]
    nc, io = k.nc, k.io
    STEPS = 2 * QB
    with ExitStack() as own:
        raw = [k.sbuf(own, f"pair_raw{s}", [P, PAIR_W]) for s in range(2)]
        wq_hi = k.sbuf(own, "wq_hi", [P, 2 * QT * P], F32R)
        wq_lo = k.sbuf(own, "wq_lo", [P, 2 * QT * P], F32R)
        rot = k.sbuf(own, "rot", [P, 2, NT])
        mask = k.sbuf(own, "mask", [P, P])
        by_parity = lambda name, shape: [k.sbuf(own, f"{name}{s}", shape) for s in range(2)]
        q = by_parity("q", [P, 2, SEQ])
        keys = by_parity("keys", [P, 2, SEQ])
        vals = by_parity("vals", [P, QB, P])
        prob = by_parity("prob", [P, SEQ])
        prob_t = by_parity("prob_t", [P, SEQ])
        stats = k.sbuf(own, "softmax_stats", [P, 2, 3])
        scores = [k.psum[:, 0:2, :].rearrange("p b n -> p (b n)"), k.psum[:, 2:4, :].rearrange("p b n -> p (b n)")]
        turn_bank = k.psum[:, 4:6, :].rearrange("p b n -> p (b n)")
        o_bank, job_bank = k.banks[6], k.banks[7]
        const_in = k.sem("attn_const_in")
        raw_in = [k.sem(f"pair_raw_in{s}") for s in range(2)]
        wq_hi_ready, wq_lo_ready = k.sem("wq_hi_ready"), k.sem("wq_lo_ready")
        keys_init = k.sem("keys_init")
        job_done = k.sem("job_done")
        job_d, job_a = k.sem("job_d"), k.sem("job_a")
        samples_q = k.sem("samples_q")
        s_done, masked, max_done = k.sem("s_done"), k.sem("masked"), k.sem("max_done")
        exp_done, sum_inv, normed = k.sem("exp_done"), k.sem("sum_inv"), k.sem("normed")
        turned, turned_a, turned_d = k.sem("turned"), k.sem("turned_a"), k.sem("turned_d")
        o_done = k.sem("o_done")
        o_out = k.sem("o_out")
        block = own.enter_context(nc.Block())

        Q_JOBS = [("q", hh, c) for hh in range(2) for c in range(NC)]
        JOBS = [("k", 0), ("k", 1), ("v", 0), *Q_JOBS[0:2], ("v", 1), *Q_JOBS[2:]]
        SLOT_OF_JOB = dict(zip((0, 1, 2, 3, 4, 8, 9, 10, 11, 12), range(len(JOBS))))
        BY_DVE = [kind == "q" for kind, *_ in JOBS]
        BY_ACT = [kind != "q" for kind, *_ in JOBS]
        FIRST_Q = JOBS.index(Q_JOBS[0])
        n_blocks = lambda n: n % QB + 1
        turn_at = lambda n: 512 * (n % 2) if n_blocks(n) <= 4 else 0

        @block.sync
        def _(sp):
            def load(i, s, wait):
                if wait:
                    sp.wait_ge(job_done, 10 * (i - 1))
                src = io["pair_w"][bass.ds(i, 1)].rearrange("a p n -> p (a n)")
                sp.dma_start(raw[s][:], src).then_inc(raw_in[s], 16)
            load(0, 0, False)
            sp.dma_start(rot[:], io["rot"]).then_inc(const_in, 16)
            sp.dma_start(mask[:], io["mask"]).then_inc(const_in, 16)
            load(1, 1, False)
            with sp.Fori(1, HP // 2) as j:
                load(2 * j, 0, True)
                load(2 * j + 1, 1, True)

        def at(i, n, ahead):
            over, m = divmod(n + ahead, STEPS)
            return STEPS * i + n + ahead, i + over, m

        def each_step(i, first, last, ahead, do):
            def run(n):
                if not (first and n + ahead < 0) and not (last and n + ahead >= STEPS):
                    do(*at(i, n, ahead))
            return run

        def wait(eng, sem, value):
            if not isinstance(value, int) or value > 0:
                eng.wait_ge(sem, value)

        def bank_of_job(i, j):
            return o_bank if isinstance(i, int) and i == 0 and j % 2 else job_bank

        def job_counts(i, job):
            return (sum(BY_DVE) * i + sum(BY_DVE[:job]), sum(BY_ACT) * i + sum(BY_ACT[:job]))

        @block.scalar
        def _(act):
            act.wait_ge(const_in, 32)

            def split(i, s, n):
                act.wait_ge(raw_in[s], n)
                act.wait_ge(job_done, 10 * i)
                act.activation(wq_hi[:], raw[s][:, 0:2 * QT * P], ACT.Copy).then_inc(wq_hi_ready, 1)

            def job(i, j, s):
                if not BY_ACT[j]:
                    return
                kind, half = JOBS[j]
                bank = bank_of_job(i, j)
                act.wait_ge(job_done, 10 * i + j + 1)
                if kind == "k":
                    for hh in range(2):
                        r = slice(64 * hh, 64 * hh + 64)
                        last = act.activation(keys[s][r, hh, half * 512:(half + 1) * 512], bank[r, :], ACT.Copy)
                else:
                    last = act.activation(vals[s][:, half * 4:half * 4 + 4, :],
                                          bank.rearrange("p (j n) -> p j n", n=P), ACT.Copy)
                last.then_inc(job_a, 1)

            def exps(N, _, n):
                s, w = n % 2, n_blocks(n) * P
                act.wait_ge(max_done, N + 1)
                wait(act, turned, N - 1)
                wait(act, sum_inv, N - 1)
                act.activation(prob[s][:, 0:w], scores[s][:, 0:w], ACT.Exp, bias=stats[:, s, 0:1],
                               accum_out=stats[:, s, 1:2]).then_inc(exp_done, 1)

            def first_half(N, _, n):
                s, w, o = n % 2, min(n_blocks(n), 4) * P, turn_at(n)
                act.wait_ge(turned, N + 1)
                wait(act, o_done, N - 1)
                act.activation(prob_t[s][:, 0:w], turn_bank[:, o:o + w], ACT.Copy).then_inc(turned_a, 1)

            def pair(i, s, turn, first=False, last=False):
                hi, exp = (each_step(i, first, last, *x) for x in ((-1, first_half), (1, exps)))
                for n in range(STEPS):
                    hi(n)
                    if n == 0 and not last:
                        split(i + 1, 1 - s, turn)
                    exp(n)
                    if n in SLOT_OF_JOB and not last:
                        job(i + 1, SLOT_OF_JOB[n], 1 - s)

            act.wait_ge(raw_in[0], 16)
            act.activation(wq_hi[:], raw[0][:, 0:2 * QT * P], ACT.Copy).then_inc(wq_hi_ready, 1)
            for j in range(len(JOBS)):
                job(0, j, 0)
            exps(0, 0, 0)
            pair(0, 0, 16, first=True)
            with act.Fori(0, HP // 2 - 1) as j:
                pair(2 * j + 1, 1, 16 * j + 32)
                pair(2 * j + 2, 0, 16 * j + 32)
            pair(HP - 1, 1, None, last=True)
            first_half(STEPS * HP - 1, HP - 1, STEPS - 1)

        @block.vector
        def _(dve):
            for s in range(2):
                dve.tensor_copy(keys[s][64:P, 0, :], m.kr[64:P, 0:SEQ])
                last = dve.tensor_copy(keys[s][0:64, 1, :], m.kr[0:64, 0:SEQ])
            last.then_inc(keys_init, 1)
            dve.wait_ge(const_in, 32)

            def split(i, s):
                dve.wait_ge(wq_hi_ready, i + 1)
                dve.tensor_tensor(wq_lo[:], raw[s][:, 0:2 * QT * P], wq_hi[:], ALU.subtract).then_inc(wq_lo_ready, 1)

            def job(i, j, s):
                if not BY_DVE[j]:
                    return
                _, hh, c = JOBS[j]
                t0, w = prompt_cols(c)
                bank = bank_of_job(i, j)
                dve.wait_ge(job_done, 10 * i + j + 1)
                if c == NC - 1:
                    dve.tensor_tensor(m.qs[:, bass.ds(2 * i + hh, 1), :], bank[:, w:w + NS].unsqueeze(1),
                                      rot[:, hh, SEQ:NT].unsqueeze(1), ALU.mult).then_inc(samples_q, 1)
                dve.tensor_tensor(q[s][:, hh, t0:t0 + w], bank[:, 0:w], rot[:, hh, t0:t0 + w], ALU.mult)\
                   .then_inc(job_d, 1)

            def maxes(N, _, n):
                s, w = n % 2, n_blocks(n) * P
                diag = scores[s][:, w - P:w]
                dve.wait_ge(s_done, N + 1)
                dve.tensor_tensor(diag, diag, mask[:], ALU.add).then_inc(masked, 1)
                dve.wait_ge(masked, N + 1)
                wait(dve, exp_done, N - 1)
                dve.tensor_reduce(stats[:, s, 0:1], scores[s][:, 0:w], AX.X, ALU.max, negate=True)\
                   .then_inc(max_done, 1)

            def normalise(N, _, n):
                s, w = n % 2, n_blocks(n) * P
                wait(dve, normed, N - 1)
                dve.wait_ge(exp_done, N + 1)
                dve.reciprocal(stats[:, s, 2:3], stats[:, s, 1:2]).then_inc(sum_inv, 1)
                dve.wait_ge(sum_inv, N + 1)
                dve.tensor_scalar(prob[s][:, 0:w], prob[s][:, 0:w], stats[:, s, 2:3], None, ALU.mult)\
                   .then_inc(normed, 1)

            def second_half(N, _, n):
                s, w = n % 2, n_blocks(n) * P
                if n_blocks(n) <= 4:
                    return
                dve.wait_ge(turned, N + 1)
                wait(dve, o_done, N - 1)
                dve.tensor_copy(prob_t[s][:, 512:w], turn_bank[:, 512:w]).then_inc(turned_d, 1)

            def attended(_, i, n):
                if n % 4 != 3:
                    return
                hh, half = n // QB, n % QB // 4
                r = slice(64 * hh, 64 * hh + 64)
                dve.wait_ge(o_done, STEPS * i + n + 1)
                dve.tensor_scalar(m.o[r, bass.ds(i, 1), half * 512:(half + 1) * 512],
                                  o_bank[r, :].unsqueeze(1), 1.0, None, ALU.mult).then_inc(o_out, 1)

            def pair(i, s, first=False, last=False):
                most, norm, take, lo = (each_step(i, first, last, *x) for x in
                                        ((1, maxes), (0, normalise), (-2, attended), (-1, second_half)))
                for n in range(STEPS):
                    if n == 0 and not last:
                        split(i + 1, 1 - s)
                    most(n)
                    norm(n)
                    take(n)
                    lo(n)
                    if n in SLOT_OF_JOB and not last:
                        job(i + 1, SLOT_OF_JOB[n], 1 - s)

            split(0, 0)
            for j in range(len(JOBS)):
                job(0, j, 0)
            maxes(0, 0, 0)
            pair(0, 0, first=True)
            with dve.Fori(0, HP // 2 - 1) as j:
                pair(2 * j + 1, 1)
                pair(2 * j + 2, 0)
            pair(HP - 1, 1, last=True)
            second_half(STEPS * HP - 1, HP - 1, STEPS - 1)
            attended(None, HP - 1, STEPS - 1)

        @block.tensor
        def _(pe):
            def job(i, j, s):
                bank = bank_of_job(i, j)
                d, a = job_counts(i, max(j - 1, 0)) if isinstance(i, int) and i == 0 else job_counts(i, j)
                if j == 0:
                    pe.wait_ge(wq_hi_ready, i + 1)
                if j == FIRST_Q:
                    pe.wait_ge(wq_lo_ready, i + 1)
                wait(pe, job_a, a)
                wait(pe, job_d, d)
                kind = JOBS[j][0]
                if kind == "q":
                    _, hh, c = JOBS[j]
                    t0, w = CHUNKS[c]
                    for t in range(QT):
                        o = slice((hh * QT + t) * P, (hh * QT + t + 1) * P)
                        ah, al = m.cq_hi[:, t, t0:t0 + w], m.cq_lo[:, t, t0:t0 + w]
                        pe.matmul(bank[:, 0:w], wq_hi[:, o], ah, start=t == 0, stop=False)
                        pe.matmul(bank[:, 0:w], wq_hi[:, o], al, start=False, stop=False)
                        last = pe.matmul(bank[:, 0:w], wq_lo[:, o], ah, start=False, stop=t == QT - 1)
                elif kind == "k":
                    half = JOBS[j][1]
                    for t in range(LT):
                        o = 2 * QT * P + t * P
                        last = pe.matmul(bank, raw[s][:, o:o + P], m.ckv[:, t, half * 512:(half + 1) * 512],
                                         start=t == 0, stop=t == LT - 1)
                else:
                    half = JOBS[j][1]
                    for b in range(4):
                        key = (half * 4 + b) * P
                        for t in range(LT):
                            o = (2 * QT + LT) * P + t * P
                            last = pe.matmul(bank[:, b * P:(b + 1) * P], m.ckv[:, t, key:key + P],
                                             raw[s][:, o:o + P], start=t == 0, stop=t == LT - 1)
                last.then_inc(job_done, 1)

            def score(N, i, n, s):
                hh, b = divmod(n, QB)
                out = scores[n % 2]
                if n == 0:
                    d, a = job_counts(i + 1, 0)
                    pe.wait_ge(job_a, a)
                    pe.wait_ge(job_d, d)
                wait(pe, exp_done, N - 1)
                w = n_blocks(n) * P
                for o in range(0, w, 512):
                    e = min(o + 512, w)
                    last = pe.matmul(out[:, o:e], q[s][:, hh, b * P:(b + 1) * P], keys[s][:, hh, o:e],
                                     start=True, stop=True)
                last.then_inc(s_done, 1)

            def long_before(i, n):
                return 2 * (QB - 4) * i + sum(n_blocks(x) > 4 for x in range(n))

            def turn(N, i, n):
                s, o = n % 2, turn_at(n)
                pe.wait_ge(normed, N + 1)
                apart = n and n_blocks(n) <= 4 and n_blocks(n - 1) <= 4
                wait(pe, turned_a, N - 1 if apart else N)
                wait(pe, turned_d, long_before(i, n))
                for b in range(n_blocks(n)):
                    last = pe.transpose(turn_bank[:, o + b * P:o + (b + 1) * P], prob[s][:, b * P:(b + 1) * P],
                                        k.ident[:])
                last.then_inc(turned, 1)

            def values(N, i, n, s):
                hh, b = divmod(n, QB)
                r = slice(64 * hh, 64 * hh + 64)
                pe.wait_ge(turned_a, N + 1)
                if n_blocks(n) > 4:
                    pe.wait_ge(turned_d, long_before(i, n) + 1)
                if n % 4 == 0:
                    wait(pe, o_out, 4 * i + n // 4)
                for kb in range(n_blocks(n)):
                    last = pe.matmul(o_bank[r, b % 4 * P:(b % 4 + 1) * P], vals[s][:, kb, r],
                                     prob_t[n % 2][:, kb * P:(kb + 1) * P], start=kb == 0, stop=kb == n_blocks(n) - 1)
                last.then_inc(o_done, 1)

            def pair(i, s, first=False, last=False):
                for n in range(STEPS):
                    if not (last and n + 2 >= STEPS):
                        score(*at(i, n, 2), s if n + 2 < STEPS else 1 - s)
                    if n in SLOT_OF_JOB and not last:
                        job(i + 1, SLOT_OF_JOB[n], 1 - s)
                    turn(*at(i, n, 0))
                    if not (first and n == 0):
                        values(*at(i, n, -1), s if n else 1 - s)

            pe.wait_ge(keys_init, 1)
            for j in range(len(JOBS)):
                job(0, j, 0)
            for n in range(2):
                score(n, 0, n, 0)
            pair(0, 0, first=True)
            with pe.Fori(0, HP // 2 - 1) as j:
                pair(2 * j + 1, 1)
                pair(2 * j + 2, 0)
            pair(HP - 1, 1, last=True)
            values(STEPS * HP - 1, HP - 1, STEPS - 1, 1)


def mla_sample_stage(k, m):
    nc, io = k.nc, k.io
    KEYS = PAST + NS
    SLOTS = 4
    with ExitStack() as own:
        wuk = k.sbuf(own, "wuk", [P, HP, KV_LORA])
        wuv = k.sbuf(own, "wuv", [P, LT, HEADS * V_DIM])
        smask = k.sbuf(own, "smask", [P, DEC_B, NS])
        table = k.sbuf(own, "page_table", [1, DEC_B * PAGES], I32)
        q_lat = k.sbuf(own, "q_lat", [P, LT, DEC_B, P])
        q_rot = k.sbuf(own, "q_rot", [P, DEC_B, P])
        cache = [k.sbuf(own, f"cache{s}", [P, PAGES, CACHE_W]) for s in range(SLOTS)]
        new_rows = k.sbuf(own, "new_rows", [NS, KV_LORA])
        prob = [k.sbuf(own, f"sprob{s}", [P, KEYS]) for s in range(2)]
        prob_t = [k.sbuf(own, f"sprob_t{s}", [P, (PAGES + 1) * P]) for s in range(2)]
        stats = k.sbuf(own, "sstats", [P, 2, 3])
        o_lat = k.sbuf(own, "o_lat", [P, KV_LORA])
        o_lat_t = k.sbuf(own, "o_lat_t", [P, LT, HEADS, NS])
        flat = lambda a, b: k.psum[:, a:b, :].rearrange("p b n -> p (b n)")
        scores, turn_bank, o_bank, ot_bank = flat(0, 3), flat(3, 6), k.banks[6], k.banks[7]
        table_in, wuk_in, smask_in, wuv_in = (k.sem(n + "_in") for n in ("table", "wuk", "smask", "wuv"))
        cache_in = [k.sem(f"cache_in{s}") for s in range(SLOTS)]
        ql_done, ql_out = k.sem("ql_done"), k.sem("ql_out")
        zeroed, rot_set = k.sem("q_rot_zeroed"), k.sem("q_rot_set")
        new_done, new_out = k.sem("new_done"), k.sem("new_out")
        s_done, masked, max_done = k.sem("ss_done"), k.sem("smasked"), k.sem("smax_done")
        exp_done, sum_inv, normed = k.sem("sexp_done"), k.sem("ssum_inv"), k.sem("snormed")
        turned, turned_a, turned_d = k.sem("sturned"), k.sem("sturned_a"), k.sem("sturned_d")
        o_done, o_out, ot_done, ot_out = k.sem("so_done"), k.sem("so_out"), k.sem("ot_done"), k.sem("ot_out")
        final, final_out = k.sem("s_final"), k.sem("s_final_out")
        block = own.enter_context(nc.Block())

        @block.sync
        def _(sp):
            sp.dma_start(table[:], io["page_table"]).then_inc(table_in, 16)
            sp.dma_start(wuk[:], io["wuk"]).then_inc(wuk_in, 16)
            sp.wait_ge(table_in, 16)

            pool_rows = io["cache"].rearrange("g p n -> (g p n)")
            size = P * CACHE_W

            def load(b, s, wait):
                at = [sp.snap(sp.value_load(table[0:1, bass.ds(b * PAGES + j, 1)], min_val=0, max_val=N_POOL - 1)
                              * size) for j in range(PAGES)]
                if wait:
                    sp.wait_ge(o_done, b - SLOTS + 1)
                for j in range(PAGES):
                    sp.dma_start(cache[s][:, j, :], pool_rows[bass.ds(at[j], size)].rearrange("(p n) -> p n", p=P))\
                      .then_inc(cache_in[s], 16)
            load(0, 0, False)
            sp.dma_start(smask[:], io["smask"]).then_inc(smask_in, 16)
            sp.wait_ge(cache_in[0], 16 * PAGES)
            for s in range(1, SLOTS):
                load(s, s, False)
            sp.dma_start(wuv[:], io["wuv"]).then_inc(wuv_in, 16)
            with sp.Fori(1, DEC_B // SLOTS) as i:
                for s in range(SLOTS):
                    load(SLOTS * i + s, s, True)

        def wait(eng, sem, value):
            if value > 0:
                eng.wait_ge(sem, value)

        @block.scalar
        def _(act):
            act.wait_ge(ql_done, 1)
            for hh in range(2):
                for t in range(LT):
                    dst = q_lat[:, t].rearrange("p s (a h t) -> p s a h t", h=2, t=DEC_S)[:, :, :, hh, :]
                    src = k.banks[2 * hh + t].rearrange("p (a s t) -> p s a t", s=DEC_B, t=DEC_S)
                    act.activation(dst, src, ACT.Copy).then_inc(ql_out, 1)
            act.wait_ge(new_done, 1)
            act.activation(new_rows[:], ot_bank[0:NS, 0:KV_LORA], ACT.Copy).then_inc(new_out, 1)

            def exps(b):
                act.wait_ge(max_done, b + 1)
                wait(act, turned, b - 1)
                wait(act, sum_inv, b - 1)
                act.activation(prob[b % 2][:], scores[:, 0:KEYS], ACT.Exp, bias=stats[:, b % 2, 0:1],
                               accum_out=stats[:, b % 2, 1:2]).then_inc(exp_done, 1)

            exps(0)
            for b in range(DEC_B):
                if b + 1 < DEC_B:
                    exps(b + 1)
                act.wait_ge(turned, b + 1)
                wait(act, o_done, b - 1)
                act.activation(prob_t[b % 2][:, 0:512], turn_bank[:, 0:512], ACT.Copy)
                act.activation(prob_t[b % 2][0:NS, PAST:PAST + P], turn_bank[0:NS, PAST:PAST + P], ACT.Copy)\
                   .then_inc(turned_a, 1)
                act.wait_ge(o_done, b + 1)
                wait(act, ot_done, b)
                act.activation(o_lat[:], o_bank[:, 0:KV_LORA], ACT.Copy).then_inc(o_out, 1)

        @block.vector
        def _(dve):
            dve.memset(q_rot[:], 0.0).then_inc(zeroed, 1)
            dve.wait_ge(zeroed, 1)
            for hh, r in ((0, slice(64, P)), (1, slice(0, 64))):
                src = m.qs[r].rearrange("p (a h) (s t) -> p s a h t", h=2, t=DEC_S)[:, :, :, hh, :]
                dst = q_rot[r].rearrange("p s (a h t) -> p s a h t", h=2, t=DEC_S)[:, :, :, hh, :]
                last = dve.tensor_copy(dst, src)
            last.then_inc(rot_set, 1)
            dve.wait_ge(rot_set, 1)
            dve.wait_ge(ql_out, 4)

            def maxes(b):
                new = scores[:, PAST:KEYS]
                dve.wait_ge(s_done, b + 1)
                dve.tensor_tensor(new, new, smask[:, b, :], ALU.add).then_inc(masked, 1)
                dve.wait_ge(masked, b + 1)
                wait(dve, exp_done, b - 1)
                dve.tensor_reduce(stats[:, b % 2, 0:1], scores[:, 0:KEYS], AX.X, ALU.max, negate=True)\
                   .then_inc(max_done, 1)

            def normalise(b):
                wait(dve, normed, b - 1)
                dve.wait_ge(exp_done, b + 1)
                dve.reciprocal(stats[:, b % 2, 2:3], stats[:, b % 2, 1:2]).then_inc(sum_inv, 1)
                dve.wait_ge(sum_inv, b + 1)
                dve.tensor_scalar(prob[b % 2][:], prob[b % 2][:], stats[:, b % 2, 2:3], None, ALU.mult)\
                   .then_inc(normed, 1)

            def take_output(b):
                dve.wait_ge(ot_done, b + 1)
                for t in range(LT):
                    last = dve.tensor_copy(o_lat_t[:, t, :, b * DEC_S:(b + 1) * DEC_S],
                                           ot_bank[:, t * P:(t + 1) * P].rearrange("p (h t) -> p h t", t=DEC_S))
                last.then_inc(ot_out, 1)

            dve.wait_ge(smask_in, 16)
            maxes(0)
            normalise(0)
            for b in range(DEC_B):
                if b + 1 < DEC_B:
                    maxes(b + 1)
                if b:
                    take_output(b - 1)
                dve.wait_ge(turned, b + 1)
                wait(dve, o_done, b - 1)
                dve.tensor_copy(prob_t[b % 2][:, 512:PAST], turn_bank[:, 512:PAST]).then_inc(turned_d, 1)
                if b + 1 < DEC_B:
                    normalise(b + 1)
            take_output(DEC_B - 1)
            dve.wait_ge(final, 1)
            dve.tensor_copy(m.o[:, :, SEQ:NT], o_bank.rearrange("p (a n) -> p a n", n=NS)).then_inc(final_out, 1)

        @block.tensor
        def _(pe):
            pe.wait_ge(wuk_in, 16)
            for hh in range(2):
                r = slice(64 * hh, 64 * hh + 64)
                for t in range(LT):
                    for a in range(HP):
                        last = pe.matmul(k.banks[2 * hh + t][:, a * NS:(a + 1) * NS], wuk[r, a, t * P:(t + 1) * P],
                                         m.qs[r, 2 * a + hh, :], start=True, stop=True)
            last.then_inc(ql_done, 1)
            for t in range(LT):
                last = pe.transpose(ot_bank[0:NS, t * P:(t + 1) * P], m.ckv[:, t, SEQ:NT], k.ident[:])
            last.then_inc(new_done, 1)
            pe.wait_ge(ql_out, 4)
            pe.wait_ge(new_out, 1)

            def score(b):
                s = b % SLOTS
                pe.wait_ge(cache_in[s], 16 * PAGES * (b // SLOTS + 1))
                wait(pe, exp_done, b)
                q = [q_lat[:, t, b, :] for t in range(LT)] + [q_rot[:, b, :]]
                for half in range(2):
                    pages = slice(half * 4, half * 4 + 4)
                    for t in range(LT + 1):
                        o = KV_LORA + t * PAGE
                        pe.matmul(scores[:, half * 512:(half + 1) * 512], q[t], cache[s][:, pages, o:o + PAGE],
                                  start=t == 0, stop=t == LT)
                new = scores[:, PAST:KEYS]
                for t in range(LT):
                    pe.matmul(new, q[t], m.ckv[:, t, SEQ:NT], start=t == 0, stop=False)
                pe.matmul(new, q[LT], m.kr[:, SEQ:NT], start=False, stop=True).then_inc(s_done, 1)

            def turn_output(b):
                pe.wait_ge(o_out, b + 1)
                wait(pe, ot_out, b)
                for t in range(LT):
                    last = pe.transpose(ot_bank[:, t * P:(t + 1) * P], o_lat[:, t * P:(t + 1) * P], k.ident[:])
                last.then_inc(ot_done, 1)

            pe.wait_ge(rot_set, 1)
            score(0)
            for b in range(DEC_B):
                if b + 1 < DEC_B:
                    score(b + 1)
                if b:
                    turn_output(b - 1)
                pe.wait_ge(normed, b + 1)
                wait(pe, turned_a, b)
                wait(pe, turned_d, b)
                for j in range(PAGES):
                    pe.transpose(turn_bank[:, j * P:(j + 1) * P], prob[b % 2][:, j * P:(j + 1) * P], k.ident[:])
                pe.transpose(turn_bank[0:NS, PAST:PAST + P], prob[b % 2][:, PAST:KEYS], k.ident[:]).then_inc(turned, 1)
                pe.wait_ge(turned_a, b + 1)
                pe.wait_ge(turned_d, b + 1)
                wait(pe, o_out, b)
                out = o_bank[:, 0:KV_LORA]
                for j in range(PAGES):
                    pe.matmul(out, prob_t[b % 2][:, j * P:(j + 1) * P], cache[b % SLOTS][:, j, 0:KV_LORA],
                              start=j == 0, stop=False)
                pe.matmul(out, prob_t[b % 2][0:NS, PAST:PAST + P], new_rows[:], start=False, stop=True)\
                  .then_inc(o_done, 1)
            turn_output(DEC_B - 1)
            pe.wait_ge(wuv_in, 16)
            pe.wait_ge(ot_out, DEC_B)
            for h in range(HEADS):
                a, hh = divmod(h, 2)
                for t in range(LT):
                    last = pe.matmul(o_bank[64 * hh:64 * hh + 64, a * NS:(a + 1) * NS],
                                     wuv[:, t, h * V_DIM:(h + 1) * V_DIM], o_lat_t[:, t, h, :],
                                     start=t == 0, stop=t == LT - 1)
            last.then_inc(final, 1)


def mla_out_stage(k, m):
    nc, io = k.nc, k.io
    with ExitStack() as own:
        o_hi = k.sbuf(own, "o_hi", [P, KT, NT], F32R)
        o_lo = k.sbuf(own, "o_lo", [P, KT, NT], F32R)
        y = k.sbuf(own, "mla_y", [P, KT, NT])
        raw = [k.sbuf(own, f"wo_raw{s}", [P, D_MODEL]) for s in range(2)]
        w_hi = [k.sbuf(own, f"wo_hi{s}", [P, D_MODEL], F32R) for s in range(2)]
        w_lo = [k.sbuf(own, f"wo_lo{s}", [P, D_MODEL], F32R) for s in range(2)]
        work = k.sbuf(own, "wo_work", [P, 2304])
        k.norm_work(work)
        exit_ = Exit(k, "mla_out", 0, GATE_MIX, y)
        raw_in = [k.sem(f"wo_raw_in{s}") for s in range(2)]
        hi_ready, lo_ready = k.sem("wo_hi_ready"), k.sem("wo_lo_ready")
        o_hi_ready, o_lo_ready = k.sem("o_hi_ready"), k.sem("o_lo_ready")
        x_in, done, evac = k.sem("x_back"), k.sem("wo_done"), k.sem("wo_evac")
        banks = [k.banks[0:3], k.banks[3:6]]
        block = own.enter_context(nc.Block())

        @block.sync
        def _(sp):
            for j in range(KT):
                if j >= 2:
                    sp.wait_ge(lo_ready, j - 1)
                sp.dma_start(raw[j % 2][:], io["wo"][j]).then_inc(raw_in[j % 2], 16)
                if j == 1:
                    sp.wait_ge(o_lo_ready, KT)
                    sp.dma_start(k.x[:], io["x"]).then_inc(x_in, 16)
            sp.wait_ge(x_in, 16)

        @block.scalar
        def _(act):
            def split(j):
                act.wait_ge(raw_in[j % 2], 16 * (j // 2 + 1))
                if j >= 2:
                    act.wait_ge(done, NC * (j - 1))
                act.activation(w_hi[j % 2][:], raw[j % 2][:], ACT.Copy).then_inc(hi_ready, 1)
            for t in range(KT):
                act.activation(o_hi[:, t], m.o[:, t], ACT.Copy).then_inc(o_hi_ready, 1)
                if t == 0:
                    split(0)
            for j in range(KT):
                if j + 1 < KT:
                    split(j + 1)
                for c, (t0, w) in enumerate(CHUNKS):
                    act.wait_ge(done, NC * j + c + 1)
                    act.activation(y[:, j, t0:t0 + w], banks[j % 2][c][:, 0:w], ACT.Copy).then_inc(evac, 1)
                    if j == KT - 1:
                        act.wait_ge(evac, NC * j + c + 1)
                        exit_.norm.act(k, act, c)
            exit_.act_x(k, act)

        @block.vector
        def _(dve):
            def split(j):
                dve.wait_ge(hi_ready, j + 1)
                dve.tensor_tensor(w_lo[j % 2][:], raw[j % 2][:], w_hi[j % 2][:], ALU.subtract).then_inc(lo_ready, 1)
            for t in range(KT):
                dve.wait_ge(o_hi_ready, t + 1)
                dve.tensor_tensor(o_lo[:, t], m.o[:, t], o_hi[:, t], ALU.subtract).then_inc(o_lo_ready, 1)
                if t == 0:
                    split(0)
            for j in range(1, KT):
                split(j)
            dve.wait_ge(x_in, 16)
            exit_.dve(k, dve, banks[0])

        @block.gpsimd
        def _(pool):
            pool.wait_ge(x_in, 16)
            exit_.pool(k, pool)

        @block.tensor
        def _(pe):
            for j in range(KT):
                pe.wait_ge(lo_ready, j + 1)
                for c, (t0, w) in enumerate(CHUNKS):
                    if j >= 2:
                        pe.wait_ge(evac, NC * (j - 2) + c + 1)
                    bank = banks[j % 2][c][:, 0:w]
                    for t in range(KT):
                        if j == 0 and c == 0:
                            pe.wait_ge(o_lo_ready, t + 1)
                        o = slice(t * P, t * P + P)
                        oh, ol = o_hi[:, t, t0:t0 + w], o_lo[:, t, t0:t0 + w]
                        pe.matmul(bank, w_hi[j % 2][:, o], oh, start=t == 0, stop=False)
                        pe.matmul(bank, w_hi[j % 2][:, o], ol, start=False, stop=False)
                        last = pe.matmul(bank, w_lo[j % 2][:, o], oh, start=False, stop=t == KT - 1)
                    last.then_inc(done, 1)
            exit_.pe(k, pe, banks[0])


class Latents:

    def __init__(self, k, ctx):
        self.o = k.x
        self.ckv = k.sbuf(ctx, "ckv", [P, LT, NT])
        self.kr = k.sbuf(ctx, "kr", [P, NT])
        self.qs = k.sbuf(ctx, "qs", [P, HEADS, NS])


def mla(k):
    with ExitStack() as own:
        m = Latents(k, own)
        with ExitStack() as latent:
            m.cq_hi = k.sbuf(latent, "cq_hi", [P, QT, NT], F32R)
            m.cq_lo = k.sbuf(latent, "cq_lo", [P, QT, NT], F32R)
            mla_project_stage(k, m)
            k.stage_done()
            mla_prompt_stage(k, m)
            k.stage_done()
        mla_sample_stage(k, m)
        k.stage_done()
        mla_out_stage(k, m)
        k.stage_done()


WINDOWS = (2, 4, 8, 16)
BUF = max(WINDOWS) - 1
GT = KT // len(WINDOWS)
SW = BUF + DEC_S


def pool_stage(k):
    nc, io = k.nc, k.io
    BY_POOL, BY_DVE = (0, 1), (2, 3)
    ORDER = (0, 2, 1, 3)
    W = BUF + SEQ
    with ExitStack() as own:
        h = k.sbuf(own, "pool_h", [P, KT, NT])
        hs = k.sbuf(own, "pool_hs", [P, KT, DEC_B, SW])
        sums = [[k.sbuf(own, f"pool_sum_{e}{s}", [P, GT, W]) for s in range(2)] for e in ("d", "p")]
        sums_s = [k.sbuf(own, f"pool_sum_s{s}", [P, KT, DEC_B, SW]) for s in range(2)]
        pooled = k.sbuf(own, "pooled", [P, KT, NT])
        w = k.sbuf(own, "pool_w", [P, KT, GT * P])
        ls = k.sbuf(own, "pool_scale", [P, KT])
        head = k.sbuf(own, "pool_head", [P, len(WINDOWS), BUF])
        last_rows = k.sbuf(own, "pool_last", [P, KT, N_SEQ, BUF])
        k.norm_work(k.sbuf(own, "pool_work", [P, 2304]))
        y = h
        scaled = [sums[0][0][:, s, 0:SEQ] for s in range(2)]
        scaled_s = pooled[:, :, SEQ:NT]
        a = k.ada[:, 1, SCALE_MIX:SCALE_MIX + KT, :]
        b = k.ada[:, 1, SHIFT_MIX:SHIFT_MIX + KT, :]
        k.stat_bank, k.col_bank = k.banks[6:8]
        late = last_x_norm(k, "pool_in")
        exit_ = Exit(k, "pool_out", 1, GATE_MIX, y)
        w_in, const_in, zeroed = k.sem("pool_w_in"), k.sem("pool_const_in"), k.sem("pool_zeroed")
        rms = k.sem("pool_rms")
        tile_scaled, tile_h = k.sem("pool_scaled"), k.sem("pool_h_tile")
        s_scaled, s_h = k.sem("pool_scaled_s"), k.sem("pool_h_s")
        step, step_p = k.sem("pool_step"), k.sem("pool_step_p")
        group_d, group_p = k.sem("pooled_d"), k.sem("pooled_p")
        kept, out = k.sem("pool_kept"), k.sem("pool_state_out")
        done, evac = k.sem("pool_done"), k.sem("pool_evac")
        rms_bank = k.psum[:, 3:6, :].rearrange("p b n -> p (b n)")
        block = own.enter_context(nc.Block())

        def pool_group(eng, g, sums, do):
            tiles, window = slice(g * GT, (g + 1) * GT), WINDOWS[g]
            src, lo, span = h[:, tiles], 0, 1
            while span < window:
                dst = sums[(span.bit_length() - 1) % 2]
                do(eng.tensor_tensor(dst[:, :, lo + span:W], src[:, :, lo + span:W], src[:, :, lo:W - span], ALU.add))
                src, lo, span = dst, lo + span, 2 * span
            do(eng.tensor_tensor(pooled[:, tiles, 0:BUF], src[:, :, BUF:2 * BUF],
                                 head[:, g].unsqueeze(1).to_broadcast([P, GT, BUF]), ALU.mult))
            do(eng.tensor_tensor(pooled[:, tiles, 0:BUF], pooled[:, tiles, 0:BUF], h[:, tiles, BUF:2 * BUF],
                                 ALU.subtract))
            return src, tiles, window

        def counted(eng, sem):
            n = [0]

            def do(instruction):
                n[0] += 1
                instruction.then_inc(sem, 1)
                eng.wait_ge(sem, n[0])
            return do

        @block.sync
        def _(sp):
            sp.dma_start(last_rows[:, :, 1:, :], io["pool_state"]).then_inc(const_in, 16)
            sp.dma_start(head[:], io["pool_head"]).then_inc(const_in, 16)
            sp.dma_start(ls[:], io["pool_scale"]).then_inc(w_in, 16)
            sp.dma_start(w[:], io["pool_w"]).then_inc(w_in, 16)
            sp.wait_ge(kept, 2)
            sp.dma_start(io["pool_out"], last_rows[:]).then_inc(out, 16)
            sp.wait_ge(out, 16)

        @block.gpsimd
        def _(pool):
            pool.memset(h[:, :, 0:BUF], 0.0).then_inc(zeroed, 1)
            pool.wait_ge(const_in, 32)
            pool.tensor_copy(hs[:, :, :, 0:BUF], last_rows[:, :, 1:, :]).then_inc(zeroed, 1)
            pool.wait_ge(zeroed, 2)
            do = counted(pool, step_p)
            for g in BY_POOL:
                pool.wait_ge(tile_h, (g + 1) * GT)
                src, tiles, window = pool_group(pool, g, sums[1], do)
                do(pool.tensor_scalar(src[:, :, 2 * BUF:W], src[:, :, 2 * BUF:W], 1.0 / window, None, ALU.mult))
                pool.tensor_tensor(pooled[:, tiles, BUF:SEQ], src[:, :, 2 * BUF:W], h[:, tiles, 2 * BUF:W],
                                   ALU.subtract).then_inc(group_p, 1)
                pool.wait_ge(group_p, g + 1)
            exit_.pool(k, pool)

        @block.scalar
        def _(act):
            late.act(k, act, 0)
            act.wait_ge(s_scaled, 3)
            act.activation(hs[:, :, :, BUF:], scaled_s.rearrange("p k (s t) -> p k s t", t=DEC_S), ACT.Copy)\
               .then_inc(s_h, 1)
            for kt in range(KT):
                act.wait_ge(tile_scaled, kt + 1)
                act.activation(h[:, kt, BUF:W], scaled[kt % 2], ACT.Identity, bias=b[:, kt, 0:1]).then_inc(tile_h, 1)
            act.wait_ge(zeroed, 2)
            act.wait_ge(s_h, 1)
            act.wait_ge(tile_h, KT)
            act.activation(last_rows[:, :, 0, :], h[:, :, SEQ:W], ACT.Copy).then_inc(kept, 1)
            act.activation(last_rows[:, :, 1:, :], hs[:, :, :, DEC_S:SW], ACT.Copy).then_inc(kept, 1)
            act.wait_ge(kept, 1)
            act.wait_ge(w_in, 32)
            for i, g in enumerate(ORDER):
                for mo in range(GT):
                    for c, (t0, n) in enumerate(CHUNKS):
                        j = (i * GT + mo) * NC + c
                        act.wait_ge(done, j + 1)
                        act.activation(y[:, g * GT + mo, t0:t0 + n], k.banks[j % 6][:, 0:n], ACT.Copy,
                                       scale=ls[:, g * GT + mo:g * GT + mo + 1]).then_inc(evac, 1)
            act.wait_ge(evac, NC * KT)
            for c in range(NC):
                exit_.norm.act(k, act, c)
            exit_.act_x(k, act)

        @block.vector
        def _(dve):
            seqs = lambda ap: ap.rearrange("p k (s t) -> p k s t", t=DEC_S)
            by_seq = lambda ap: ap[:, :, 1:].unsqueeze(3).to_broadcast([P, KT, DEC_B, DEC_S])
            late.dve(k, dve, 0)
            dve.wait_ge(rms, 1)
            dve.tensor_tensor(scaled_s, k.x[:, :, SEQ:NT], rms_bank[:, SEQ:NT].unsqueeze(1).to_broadcast([P, KT, NS]),
                              ALU.mult).then_inc(s_scaled, 1)
            for i, (vectors, op) in enumerate(((a, ALU.mult), (b, ALU.add))):
                dve.wait_ge(s_scaled, i + 1)
                dve.tensor_tensor(seqs(scaled_s), seqs(scaled_s), by_seq(vectors), op).then_inc(s_scaled, 1)
            for kt in range(KT):
                if kt >= 2:
                    dve.wait_ge(tile_h, kt - 1)
                dve.scalar_tensor_tensor(scaled[kt % 2], k.x[:, kt, 0:SEQ], a[:, kt, 0:1], rms_bank[:, 0:SEQ],
                                         ALU.mult, ALU.mult).then_inc(tile_scaled, 1)
            do = counted(dve, step)
            dve.wait_ge(const_in, 32)
            dve.wait_ge(zeroed, 2)
            dve.wait_ge(s_h, 1)
            src, span = hs, 1
            for g, window in enumerate(WINDOWS):
                rest = slice(g * GT, KT)
                while span < window:
                    dst = sums_s[(span.bit_length() - 1) % 2]
                    do(dve.tensor_tensor(dst[:, rest, :, 2 * span - 1:], src[:, rest, :, 2 * span - 1:],
                                         src[:, rest, :, span - 1:SW - span], ALU.add))
                    src, span = dst, 2 * span
                tiles = slice(g * GT, (g + 1) * GT)
                do(dve.scalar_tensor_tensor(seqs(pooled[:, tiles, SEQ:NT]), src[:, tiles, :, BUF:], 1.0 / window,
                                            hs[:, tiles, :, BUF:], ALU.mult, ALU.subtract))
            dve.wait_ge(tile_h, KT)
            for g in BY_DVE:
                src, tiles, window = pool_group(dve, g, sums[0], do)
                dve.scalar_tensor_tensor(pooled[:, tiles, BUF:SEQ], src[:, :, 2 * BUF:W], 1.0 / window,
                                         h[:, tiles, 2 * BUF:W], ALU.mult, ALU.subtract).then_inc(group_d, 1)
                dve.wait_ge(group_d, g - BY_DVE[0] + 1)
            exit_.dve(k, dve, k.banks[0:3])

        @block.tensor
        def _(pe):
            late.pe(k, pe, 0)
            pe.wait_ge(late.rstd, 1)
            for c in range(NC):
                last = spread(k, pe, c, k.rstd[:, 0, c, :], rms_bank[:, CHUNKS[c][0]:])
            last.then_inc(rms, 1)
            pe.wait_ge(w_in, 32)
            pe.wait_ge(tile_scaled, KT)
            pe.wait_ge(s_scaled, 1)
            for i, g in enumerate(ORDER):
                if g in BY_POOL:
                    pe.wait_ge(group_p, g + 1)
                else:
                    pe.wait_ge(group_d, g - BY_DVE[0] + 1)
                for mo in range(GT):
                    for c, (t0, n) in enumerate(CHUNKS):
                        j = (i * GT + mo) * NC + c
                        if j >= 6:
                            pe.wait_ge(evac, j - 5)
                        if c == NC - 1 and g in BY_POOL:
                            pe.wait_ge(step, 2 * len(WINDOWS))
                        for t in range(GT):
                            last = pe.matmul(k.banks[j % 6][:, 0:n], w[:, g * GT + t, mo * P:(mo + 1) * P],
                                             pooled[:, g * GT + t, t0:t0 + n], start=t == 0, stop=t == GT - 1)
                        last.then_inc(done, 1)
            pe.wait_ge(evac, NC * KT)
            exit_.pe(k, pe, k.banks[0:3])


G, U, D = range(3)


def ffn_stage(k, layer):
    nc, io = k.nc, k.io
    n = f"ffn{layer}_"
    with ExitStack() as own:
        h_hi = k.sbuf(own, n + "h_hi", [P, KT, NT], F32R)
        h_lo = k.sbuf(own, n + "h_lo", [P, KT, NT], F32R)
        y = k.sbuf(own, n + "y", [P, KT, NT])
        raw = [k.sbuf(own, f"{n}raw{s}", [P, D_MODEL]) for s in range(3)]
        w_hi = [k.sbuf(own, f"{n}w_hi{s}", [P, D_MODEL], F32R) for s in range(3)]
        w_lo = [k.sbuf(own, f"{n}w_lo{s}", [P, D_MODEL], F32R) for s in range(3)]
        PROMPT_W = SEQ + CONV_W - 1
        SAMPLE_W = DEC_S + CONV_W - 1
        u = [k.sbuf(own, f"{n}u{s}", [P, PROMPT_W + DEC_B * SAMPLE_W]) for s in range(2)]
        work = k.sbuf(own, n + "work", [P, 2304])
        conv = [work[:, 0:NT], work[:, NT:2 * NT]]
        g_hi = k.sbuf(own, n + "g_hi", [P, NT], F32R)
        g_lo = k.sbuf(own, n + "g_lo", [P, NT], F32R)
        taps = k.sbuf(own, n + "taps", [P, 2 * PAIRS, 4])
        state = k.sbuf(own, n + "state", [P, 2 * PAIRS, 18])
        k.norm_work(work)
        entry = Entry(k, n + "in", layer, SCALE_FFN, SHIFT_FFN,
                      u[0][:, 0:2 * MAXC].rearrange("p (b t) -> p b t", b=2),
                      u[1][:, 0:KT * NS].rearrange("p (k t) -> p k t", k=KT))
        exit_ = Exit(k, n + "out", layer, GATE_FFN, y, stats=layer == 0)
        x_out = k.sem(n + "x_out")
        per_half = lambda what: [k.sem(f"{n}{what}_{s}") for s in ("g", "u")]
        per_unit = lambda what: [k.sem(f"{n}{what}_{s}") for s in ("g", "u", "d")]
        raw_in = per_unit("raw_in")
        hi_ready = per_unit("hi_ready")
        lo_ready = per_unit("lo_ready")
        const_in = k.sem(n + "const_in")
        up_done = per_half("up_done")
        evac = per_half("evac")
        prev_in = per_half("prev_in")
        saved = per_half("saved")
        conv_step = per_half("conv_step")
        silu_done = k.sem(n + "silu_done")
        product = k.sem(n + "product")
        g_hi_ready, g_lo_ready = k.sem(n + "g_hi_ready"), k.sem(n + "g_lo_ready")
        down_done = k.sem(n + "down_done")
        acc_done = k.sem(n + "acc_done")
        cleared = k.sem(n + "cleared")
        state_out = k.sem(n + "state_out")
        half_bank = [k.banks[0:3], k.banks[3:6]]
        down_bank = k.banks[6:8]
        k.stat_bank, k.col_bank = half_bank[G][0:2]
        block = own.enter_context(nc.Block())

        @block.sync
        def _(sp):
            def load(p, wait):
                for s in (G, U, D):
                    if wait:
                        sp.wait_ge(lo_ready[s], p)
                    sp.dma_start(raw[s][:], io["ffn_w"][layer, bass.ds(p, 1), s].rearrange("a p n -> p (a n)"))\
                      .then_inc(raw_in[s], 16)

            load(0, False)
            sp.dma_start(taps[:], io["taps"][:, layer]).then_inc(const_in, 16)
            sp.dma_start(state[:], io["conv_state"][:, layer]).then_inc(const_in, 16)
            with sp.Fori(1, PAIRS) as p:
                load(p, True)
            for s in (G, U):
                sp.wait_ge(saved[s], PAIRS)
            sp.dma_start(io["conv_out"][:, layer], state[:]).then_inc(state_out, 16)
            if layer == 1:
                for c, (t0, n_) in enumerate(CHUNKS):
                    exit_.added(sp, c, KT)
                    sp.dma_start(io["x_out"][:, :, t0:t0 + n_], k.x[:, :, t0:t0 + n_]).then_inc(x_out, 16)
                sp.wait_ge(x_out, 16 * NC)
            sp.wait_ge(state_out, 16)

        @block.gpsimd
        def _(pool):
            pool.memset(y[:], 0.0).then_inc(cleared, 1)
            entry.ready(pool, NC - 1)
            for s in (G, U):
                pool.memset(u[s][:, 0:CONV_W - 1], 0.0).then_inc(cleared, 1)
            exit_.pool(k, pool)

        def split_hi(act, s, p):
            act.wait_ge(raw_in[s], 16 * p + 16)
            if s == D:
                act.wait_ge(down_done, 24 * p)
            else:
                act.wait_ge(up_done[s], 3 * p)
            act.activation(w_hi[s][:], raw[s][:], ACT.Copy).then_inc(hi_ready[s], 1)

        def evacuate(act, s, p):
            m = 2 * p + s
            rows = u[s][:, PROMPT_W:].rearrange("p (s t) -> p s t", t=SAMPLE_W)
            tap2, bias = taps[:, bass.ds(m, 1), 2], taps[:, bass.ds(m, 1), 3]
            act.wait_ge(conv_step[s], 4 * p)
            act.wait_ge(product, p)
            if s == G:
                act.wait_ge(g_lo_ready, p)
            for c, (t0, n_) in enumerate(CHUNKS):
                w = prompt_cols(c)[1]
                bank = half_bank[s][c]
                act.wait_ge(up_done[s], 3 * p + c + 1)
                act.activation(u[s][:, 2 + t0:2 + t0 + w], bank[:, 0:w], ACT.Copy)
                if w < n_:
                    act.activation(rows[:, :, 2:], bank[:, w:n_].rearrange("p (s t) -> p s t", t=DEC_S), ACT.Copy)
                act.activation(conv[s][:, t0:t0 + n_], bank[:, 0:n_], ACT.Identity, bias=bias, scale=tap2)\
                   .then_inc(evac[s], 1)

        @block.scalar
        def _(act):
            for c in range(NC):
                entry.act(k, act, c, *put_in(h_hi))
                if c == 0:
                    split_hi(act, G, 0)
            act.wait_ge(const_in, 32)
            entry.ready(act, NC - 1)
            act.wait_ge(cleared, 3)

            def pair(p, first=False, last=False):
                split_hi(act, U, p)
                if not first:
                    split_hi(act, D, p - 1)
                    act.wait_ge(product, p)
                    act.wait_ge(down_done, 24 * (p - 1))
                    act.activation(g_hi[:], conv[G], ACT.Copy).then_inc(g_hi_ready, 1)
                evacuate(act, G, p)
                if not last:
                    split_hi(act, G, p + 1)
                act.wait_ge(conv_step[G], 4 * p + 4)
                act.activation(conv[G], conv[G], ACT.Silu).then_inc(silu_done, 1)
                evacuate(act, U, p)

            pair(0, first=True)
            pair(1)
            with act.Fori(2, PAIRS - 1) as p:
                pair(p)
            pair(PAIRS - 1, last=True)
            split_hi(act, D, PAIRS - 1)
            act.wait_ge(product, PAIRS)
            act.wait_ge(down_done, 24 * (PAIRS - 1))
            act.activation(g_hi[:], conv[G], ACT.Copy).then_inc(g_hi_ready, 1)
            act.wait_ge(g_lo_ready, PAIRS)
            for c in range(NC):
                act.wait_ge(acc_done, 24 * (PAIRS - 1) + KT * (c + 1))
                exit_.norm.act(k, act, c)
            exit_.act_x(k, act)

        def split_lo(dve, s, p):
            dve.wait_ge(hi_ready[s], p + 1)
            dve.tensor_tensor(w_lo[s][:], raw[s][:], w_hi[s][:], ALU.subtract).then_inc(lo_ready[s], 1)

        def conv_steps(dve, s, p):
            m = 2 * p + s
            rows = u[s][:, PROMPT_W:].rearrange("p (s t) -> p s t", t=SAMPLE_W)
            cp, cs = conv[s][:, 0:SEQ], conv[s][:, SEQ:NT].rearrange("p (s t) -> p s t", t=DEC_S)

            mine = state[:, bass.ds(m, 1), :]
            mine_s = mine[:, :, 0:16].rearrange("p a (s t) -> p (a s) t", t=2)

            def prompt(tap):
                dve.scalar_tensor_tensor(cp, u[s][:, tap:tap + SEQ], taps[:, bass.ds(m, 1), tap], cp,
                                         ALU.mult, ALU.add).then_inc(conv_step[s], 1)

            def samples(tap):
                dve.scalar_tensor_tensor(cs, rows[:, :, tap:tap + DEC_S], taps[:, bass.ds(m, 1), tap], cs,
                                         ALU.mult, ALU.add).then_inc(conv_step[s], 1)

            def tap_1():
                dve.tensor_copy(rows[:, :, 0:2], mine_s).then_inc(prev_in[s], 1)
                dve.wait_ge(evac[s], 3 * p + 3)
                prompt(1)
                dve.wait_ge(prev_in[s], p + 1)
                samples(1)
                dve.tensor_copy(mine_s, rows[:, :, DEC_S:SAMPLE_W])
                dve.tensor_copy(mine[:, :, 16:18], u[s][:, SEQ:SEQ + 2].unsqueeze(1)).then_inc(saved[s], 1)

            def tap_0():
                dve.wait_ge(conv_step[s], 4 * p + 2)
                prompt(0)
                samples(0)
            return [tap_1, tap_0]

        def product_of(i, last):
            return divmod(i, KT)[::-1] if last else divmod(i, NC)

        def accumulate(dve, p, i, last=False):
            kt, c = product_of(i, last)
            t0, n_ = CHUNKS[c]
            dve.wait_ge(down_done, 24 * p + i + 1)
            dst = y[:, kt, t0:t0 + n_]
            dve.tensor_tensor(dst, down_bank[i % 2][:, 0:n_], dst, ALU.add).then_inc(acc_done, 1)

        @block.vector
        def _(dve):
            for c in range(NC):
                entry.dve(k, dve, c, half_bank[U][c], h_hi, h_lo)
                if c == 0:
                    split_lo(dve, G, 0)
            dve.wait_ge(const_in, 32)
            dve.wait_ge(cleared, 3)

            def finish_g(p):
                for f in conv_steps(dve, U, p):
                    f()
                dve.wait_ge(conv_step[U], 4 * p + 4)
                dve.wait_ge(silu_done, p + 1)
                dve.tensor_tensor(conv[G], conv[G], conv[U], ALU.mult).then_inc(product, 1)

            def split_g(p):
                dve.wait_ge(g_hi_ready, p + 1)
                dve.tensor_tensor(g_lo[:], conv[G], g_hi[:], ALU.subtract).then_inc(g_lo_ready, 1)

            def pair(p, first=False, last=False):
                if not first:
                    finish_g(p - 1)
                split_lo(dve, U, p)
                if not first:
                    split_lo(dve, D, p - 1)
                    split_g(p - 1)
                side = conv_steps(dve, G, p)
                if not last:
                    side = [lambda: split_lo(dve, G, p + 1)] + side
                for i in range(24):
                    if not first:
                        accumulate(dve, p - 1, i)
                    if i % 3 == 2 and side:
                        side.pop(0)()

            pair(0, first=True)
            pair(1)
            with dve.Fori(2, PAIRS - 1) as p:
                pair(p)
            pair(PAIRS - 1, last=True)
            finish_g(PAIRS - 1)
            split_lo(dve, D, PAIRS - 1)
            split_g(PAIRS - 1)
            for i in range(24):
                accumulate(dve, PAIRS - 1, i, last=True)
            exit_.dve(k, dve, half_bank[U])

        @block.tensor
        def _(pe):
            entry.pe(k, pe, half_bank[U])

            def products(bank, s, kt, c, act_hi, act_lo, first, last):
                w = slice(kt * P, kt * P + P)
                a = slice(0, CHUNKS[c][1])
                pe.matmul(bank[:, a], w_hi[s][:, w], act_hi, start=first, stop=False)
                pe.matmul(bank[:, a], w_hi[s][:, w], act_lo, start=False, stop=False)
                return pe.matmul(bank[:, a], w_lo[s][:, w], act_hi, start=False, stop=last)

            def down(p, i, last_pair=False):
                kt, c = product_of(i, last_pair)
                t0, n_ = CHUNKS[c]
                if i == 0:
                    pe.wait_ge(lo_ready[D], p + 1)
                    pe.wait_ge(g_lo_ready, p + 1)
                pe.wait_ge(acc_done, 24 * p + max(i - 1, 0))
                last = products(down_bank[i % 2], D, kt, c, g_hi[:, t0:t0 + n_], g_lo[:, t0:t0 + n_], True, True)
                last.then_inc(down_done, 1)
                return last

            def up(s, p, first, with_down):
                pe.wait_ge(lo_ready[s], p + 1)
                for c, (t0, n_) in enumerate(CHUNKS):
                    if s == U and first and c == 0:
                        entry.ready(pe, NC - 1)
                    if not first:
                        pe.wait_ge(evac[s], 3 * (p - 1) + c + 1)
                    for kt in range(KT):
                        if s == G and first:
                            entry.tile_ready(pe, c, kt)
                        last = products(half_bank[s][c], s, kt, c, h_hi[:, kt, t0:t0 + n_],
                                        h_lo[:, kt, t0:t0 + n_], kt == 0, kt == KT - 1)
                        if kt == KT - 1:
                            last.then_inc(up_done[s], 1)
                        if with_down:
                            down(p - 1, c * KT + kt)

            def pair(p, first=False):
                up(G, p, first, False)
                up(U, p, first, not first)

            pair(0, first=True)
            pair(1)
            with pe.Fori(2, PAIRS) as p:
                pair(p)
            for i in range(24):
                if i == 2 * KT:
                    exit_.norm.pe_sum(k, pe, 0)
                down(PAIRS - 1, i, last_pair=True)
            exit_.pe(k, pe, half_bank[U], summed=True)


def program(nc, io):
    with ExitStack() as ctx:
        k = Kernel(nc, ctx, io)
        adaln_stage(k)
        k.stage_done()
        mla(k)
        ffn_stage(k, 0)
        k.stage_done()
        pool_stage(k)
        k.stage_done()
        ffn_stage(k, 1)
        k.stage_done()


def columns(prompt, sample):
    rows = np.concatenate([prompt, sample.reshape(NS, -1)], axis=0)
    return np.ascontiguousarray(rows.T.reshape(-1, P, NT).transpose(1, 0, 2))


def units(w):
    kt = w.shape[0] // P
    return w.reshape(kt, P, w.shape[1] // P, P).transpose(2, 1, 0, 3).reshape(-1, P, kt * P)


def rotation():
    half = ROPE // 2
    inv = np.float32(10000.0) ** (-np.arange(half, dtype=np.float32) / half)
    pos = np.concatenate([np.arange(SEQ), PAST + np.tile(np.arange(DEC_S), DEC_B)]).astype(np.float32)
    ang = inv[:, None] * pos[None, :]
    cos, sin = np.cos(ang), np.sin(ang)
    return np.concatenate([cos, cos]), np.concatenate([-sin, sin])


def swapped(w):
    return np.concatenate([w[..., ROPE // 2:], w[..., :ROPE // 2]], axis=-1)


def attention_inputs(a):
    w_dkv, w_uq, w_uk, w_uv = (a[n][0] for n in ("mla_w_dkv", "mla_w_uq", "mla_w_uk", "mla_w_uv"))
    kr = w_dkv[:, KV_LORA:]
    proj = np.concatenate([units(w_dkv[:, :KV_LORA]), units(np.concatenate([swapped(kr)] * 2 + [kr] * 2, axis=1)),
                           units(a["mla_w_dq"][0])])
    uq = w_uq.reshape(Q_LORA, HEADS, NOPE + ROPE)
    nope, rope = uq[..., :NOPE], uq[..., NOPE:]
    rope = np.concatenate([rope, swapped(rope)], axis=-1)
    even = np.concatenate([nope, rope], axis=-1)[:, 0::2]
    odd = np.concatenate([rope, nope], axis=-1)[:, 1::2]
    heads = np.stack([even, odd], axis=2).reshape(QT, P, HP, 2, P).transpose(2, 1, 3, 0, 4).reshape(HP, P, -1)
    pairs = lambda w: w.reshape(LT, P, HP, P).transpose(2, 1, 0, 3).reshape(HP, P, -1)
    cos, sin = rotation()
    one = np.ones((NOPE, NT), np.float32)
    rot = np.stack([np.concatenate([one, cos, sin]), np.concatenate([cos, sin, one])], axis=1)
    lat, krope = a["cache_kv_latent"][0], a["cache_k_rope"][0]
    pages = lat.shape[0]
    lat_t = lat.reshape(pages, PAGE, LT, P).transpose(0, 3, 2, 1).reshape(pages, P, LT * PAGE)
    kr_t = np.tile(krope.transpose(0, 2, 1), (1, P // ROPE, 1))
    t = np.arange(DEC_S)
    own = np.eye(DEC_B, dtype=bool)[None, :, :, None] & (t[:, None, None, None] >= t)
    smask = np.where(own, 0.0, NEG).astype(np.float32).reshape(DEC_S, DEC_B, NS)
    tile = np.arange(P)
    return {
        "proj_w": proj,
        "ktab": np.concatenate([sin, sin, cos, cos]),
        "latent_gain": np.concatenate([a["mla_kv_norm"][0], a["mla_q_norm"][0]]).reshape(LT + QT, P).T,
        "pair_w": np.concatenate([heads, pairs(w_uk), pairs(w_uv)], axis=2),
        "rot": (rot * np.float32(SCALE)).astype(np.float32),
        "mask": np.where(tile[:, None] >= tile, 0.0, NEG).astype(np.float32),
        "cache": np.concatenate([lat, lat_t, kr_t], axis=2),
        "page_table": a["page_table"].astype(np.int32).reshape(1, -1),
        "wuk": w_uk.transpose(1, 2, 0).reshape(HP, P, KV_LORA).transpose(1, 0, 2),
        "wuv": w_uv.reshape(LT, P, HEADS * V_DIM).transpose(1, 0, 2),
        "smask": np.tile(smask, (HEADS, 1, 1)),
        "wo": units(a["mla_w_o"][0]),
    }


def pool_inputs(a):
    pos = np.arange(BUF)
    head = np.stack([1.0 / np.minimum(pos + 1, w) for w in WINDOWS]).astype(np.float32)
    return {
        "pool_w": a["pool_w"][0].reshape(KT, P, GT * P).transpose(1, 0, 2),
        "pool_scale": a["pool_scale"][0].reshape(KT, P).T,
        "pool_head": np.tile(head[None], (P, 1, 1)),
        "pool_state": a["state_pool"][0].reshape(DEC_B, BUF, KT, P).transpose(3, 2, 0, 1),
    }


def laid_out(a):
    pair_units = []
    for l in range(2):
        up = units(a["ffn_w_up"][l]).reshape(2, PAIRS, P, D_MODEL)
        down = a["ffn_w_down"][l].reshape(1, PAIRS, P, D_MODEL)
        pair_units.append(np.concatenate([up, down]).transpose(1, 0, 2, 3))
    by_pair = lambda v: v.reshape(2, PAIRS, P).transpose(2, 1, 0).reshape(P, 2 * PAIRS)
    taps = np.stack([np.stack([by_pair(a["ffn_conv_w"][l, t]) for t in range(CONV_W)]
                              + [by_pair(a["ffn_conv_b"][l])], axis=-1) for l in range(2)], axis=1)
    state = a["state_conv"].reshape(2, DEC_B, 2, 2, PAIRS, P).transpose(5, 0, 4, 3, 1, 2)
    state = state.reshape(P, 2, 2 * PAIRS, 16)
    state = np.concatenate([state, np.zeros((P, 2, 2 * PAIRS, 2), np.float32)], axis=-1)
    gains = np.stack([a["norm_mix_pre"], a["norm_mix_post"], a["norm_ffn_pre"], a["norm_ffn_post"]], axis=1)
    cond = np.concatenate([a["c_prompt"], a["c_sample"]])
    return {
        "x": columns(a["x_prompt"][0], a["x_sample"]),
        "cond": cond.T.reshape(KT, P, N_SEQ).transpose(1, 0, 2),
        "ada_w": a["ada_w"].reshape(2, KT, P, SIX // ADA_GROUP, ADA_GROUP * P).transpose(0, 3, 2, 1, 4)
        .reshape(2 * SIX // ADA_GROUP, P, ADA_GROUP * D_MODEL),
        "ada_b": a["ada_b"].reshape(2, SIX, P).transpose(2, 0, 1),
        "gains": gains.reshape(2, 4, KT, P).transpose(3, 0, 1, 2),
        "ident": np.eye(P, dtype=np.float32),
        "ffn_w": np.stack(pair_units),
        "taps": taps,
        "conv_state": state,
        **attention_inputs(a),
        **pool_inputs(a),
    }


OUTPUTS = {
    "x_out": [P, KT, NT],
    "conv_out": [P, 2, 2 * PAIRS, 18],
    "ckv_out": [P, LT, NT],
    "kr_out": [ROPE, NT],
    "pool_out": [P, KT, N_SEQ, BUF],
}


def kernel(**inputs):
    import concourse.bacc as bacc
    from concourse.bass_utils import run_bass_kernel_spmd

    a = {name: np.asarray(v) for name, v in inputs.items()}
    nc = bacc.Bacc("TRN2", target_bir_lowering=False, num_devices=1)
    arrays = {f"in_{n}": np.ascontiguousarray(v) for n, v in laid_out(a).items()}
    io = {n[3:]: nc.dram_tensor(n, list(v.shape), mybir.dt.from_np(v.dtype), kind="ExternalInput").ap()
          for n, v in arrays.items()}
    for n, shape in OUTPUTS.items():
        io[n] = nc.dram_tensor(f"out_{n}", shape, F32, kind="ExternalOutput").ap()
    program(nc, io)
    r = run_bass_kernel_spmd(nc, [arrays], core_ids=[0]).results[0]
    out = {n: np.asarray(r[f"out_{n}"]) for n in OUTPUTS}

    def rows(v, width):
        return v.transpose(1, 0, 2).reshape(width, -1).T

    x = rows(out["x_out"], D_MODEL)
    conv = out["conv_out"]
    conv_s = conv[..., 0:16].reshape(P, 2, PAIRS, 2, DEC_B, 2).transpose(1, 4, 5, 3, 2, 0)
    conv_p = conv[..., 16:18].reshape(P, 2, PAIRS, 2, 2).transpose(1, 4, 3, 2, 0)
    conv_s = conv_s.reshape(2, DEC_B, 2, 2 * D_FF)
    conv_p = conv_p.reshape(2, 1, 2, 2 * D_FF)
    ckv, kr = rows(out["ckv_out"], KV_LORA), out["kr_out"].T
    state = out["pool_out"].transpose(2, 3, 1, 0).reshape(N_SEQ, BUF, D_MODEL)
    sample = lambda v: v[SEQ:].reshape(DEC_B, DEC_S, -1)
    return (x[None, :SEQ], sample(x), ckv[None, None, :SEQ], kr[None, None, :SEQ], sample(ckv)[None],
            sample(kr)[None], state[None, :1], state[None, 1:], conv_p, conv_s)
```
